# Optimizing a Trainium2 kernel written in Bass

```python
import jax
import jax.numpy as jnp
from jax import lax
import numpy as np

D_MODEL = 2048
BATCH = 1
SEQ = 256
DEPTH = 2

HEAD_DIM = 128
DIL_CONFIGS = ((128, 1), (512, 4), (2048, 16))
N_GROUPS_A = len(DIL_CONFIGS)
HEADS_PER_GROUP_A = 8
WIDTH_A = HEADS_PER_GROUP_A * HEAD_DIM
N_HEADS_B = D_MODEL // HEAD_DIM
WIDTH_B = N_HEADS_B * HEAD_DIM
ROT_DIM = HEAD_DIM // 4
ROPE_THETA = 500000.0
D_FF = ((8 * D_MODEL + 3 * 256 - 1) // (3 * 256)) * 256
BLOCK = 128
N_A_LAYERS = DEPTH // 2
N_B_LAYERS = DEPTH - N_A_LAYERS
EPS = 1e-6
NEG_INF = -1e30

kernel_name = 'yoco_dilated_fox_hybrid'

def rmsnorm(x, g):
    xf = x.astype(jnp.float32)
    y = xf * lax.rsqrt(jnp.mean(xf * xf, axis=-1, keepdims=True) + EPS)
    return (y * g.astype(jnp.float32)).astype(x.dtype)

def modulate(h, shift, scale):
    return h * (1.0 + scale[:, None, :]) + shift[:, None, :]

def swiglu(h, w_in, w_out):
    g, u = jnp.split(h @ w_in, 2, axis=-1)
    return (jax.nn.silu(g) * u) @ w_out

def rope_tables(seq):
    inv = ROPE_THETA ** (-jnp.arange(0, ROT_DIM, 2, dtype=jnp.float32) / ROT_DIM)
    ang = jnp.arange(seq, dtype=jnp.float32)[:, None] * inv[None, :]
    return jnp.cos(ang), jnp.sin(ang)

def partial_rope(x, cos, sin):
    half = ROT_DIM // 2
    shape = (1, x.shape[1]) + (1,) * (x.ndim - 3) + (half,)
    cos = cos.reshape(shape).astype(x.dtype)
    sin = sin.reshape(shape).astype(x.dtype)
    x1 = x[..., :half]
    x2 = x[..., half:ROT_DIM]
    return jnp.concatenate([x1 * cos - x2 * sin, x2 * cos + x1 * sin, x[..., ROT_DIM:]], axis=-1)

def dilated_group_attention(q, k, v, window, dilation):
    b, s, h, dh = q.shape
    n_back = window // dilation
    sub_len = s // dilation
    nb = -(-sub_len // BLOCK)
    pad = nb * BLOCK - sub_len

    def to_blocks(t):
        t = t.reshape(b, sub_len, dilation, h, dh)
        t = jnp.pad(t, ((0, 0), (0, pad), (0, 0), (0, 0), (0, 0)))
        return t.reshape(b, nb, BLOCK, dilation, h, dh)

    def with_prev(t):
        prev = jnp.pad(t[:, :-1], ((0, 0), (1, 0), (0, 0), (0, 0), (0, 0), (0, 0)))
        return jnp.concatenate([prev, t], axis=2)

    qb = to_blocks(q)
    kb = with_prev(to_blocks(k))
    vb = with_prev(to_blocks(v))
    scores = jnp.einsum('bnqrhd,bnkrhd->bnrhqk', qb, kb,
                        preferred_element_type=jnp.float32) * (dh ** -0.5)
    qi = jnp.arange(BLOCK)[:, None]
    kj = jnp.arange(2 * BLOCK)[None, :]
    dist = qi + BLOCK - kj
    band = (dist >= 0) & (dist <= n_back)
    exists = (jnp.arange(nb)[:, None, None] > 0) | (kj >= BLOCK)[None]
    mask = band[None] & exists
    scores = jnp.where(mask[None, :, None, None], scores, NEG_INF)
    m = jnp.max(scores, axis=-1, keepdims=True)
    p = jnp.exp(scores - m)
    den = jnp.sum(p, axis=-1)
    o = jnp.einsum('bnrhqk,bnkrhd->bnqrhd', p.astype(v.dtype), vb,
                   preferred_element_type=jnp.float32)
    o = o / jnp.transpose(den, (0, 1, 4, 2, 3))[..., None]
    lse = jnp.transpose(m[..., 0] + jnp.log(den), (0, 1, 4, 2, 3))
    o = o.reshape(b, nb * BLOCK, dilation, h, dh)[:, :sub_len].reshape(b, s, h, dh)
    lse = lse.reshape(b, nb * BLOCK, dilation, h)[:, :sub_len].reshape(b, s, h)
    return o, lse

def dilated_mixture_attention(h, w_qkv, g_q, g_k, w_o, cos, sin):
    b, s, _ = h.shape
    qkv = (h @ w_qkv).reshape(b, s, 3, N_GROUPS_A, HEADS_PER_GROUP_A, HEAD_DIM)
    q = partial_rope(rmsnorm(qkv[:, :, 0], g_q[:, None, :]), cos, sin)
    k = partial_rope(rmsnorm(qkv[:, :, 1], g_k[:, None, :]), cos, sin)
    v = qkv[:, :, 2]
    outs, lses = [], []
    for gi, (window, dilation) in enumerate(DIL_CONFIGS):
        o, l = dilated_group_attention(q[:, :, gi], k[:, :, gi], v[:, :, gi], window, dilation)
        outs.append(o)
        lses.append(l)
    alpha = jax.nn.softmax(jnp.stack(lses), axis=0)
    o = jnp.sum(alpha[..., None] * jnp.stack(outs), axis=0)
    return o.astype(h.dtype).reshape(b, s, WIDTH_A) @ w_o

def shared_kv(x, mod_kv, g_norm_kv, w_kv, g_k, w_f, b_f):
    b, s, _ = x.shape
    shift, scale = jnp.split(mod_kv, 2, axis=-1)
    h = modulate(rmsnorm(x, g_norm_kv), shift, scale)
    kv = (h @ w_kv).reshape(b, s, 2, N_HEADS_B, HEAD_DIM)
    k = rmsnorm(kv[:, :, 0], g_k)
    v = kv[:, :, 1]
    log_f = jax.nn.log_sigmoid((h @ w_f + b_f).astype(jnp.float32))
    cum_log_f = jnp.cumsum(log_f, axis=1)
    return k, v, cum_log_f

def forgetting_attention(h, w_q, g_q, w_o, k, v, cum_log_f):
    b, s, _ = h.shape
    nb = s // BLOCK
    q = rmsnorm((h @ w_q).reshape(b, s, N_HEADS_B, HEAD_DIM), g_q)
    q_blocks = jnp.moveaxis(q.reshape(b, nb, BLOCK, N_HEADS_B, HEAD_DIM), 1, 0)
    fq_blocks = jnp.moveaxis(cum_log_f.reshape(b, nb, BLOCK, N_HEADS_B), 1, 0)
    fk = jnp.transpose(cum_log_f, (0, 2, 1))
    key_pos = jnp.arange(s)
    scale = HEAD_DIM ** -0.5

    def attend_block(args):
        q_blk, fq, blk = args
        logits = jnp.einsum('bqhd,bkhd->bhqk', q_blk, k,
                            preferred_element_type=jnp.float32) * scale
        logits = logits + jnp.transpose(fq, (0, 2, 1))[..., None] - fk[:, :, None, :]
        q_pos = blk * BLOCK + jnp.arange(BLOCK)
        logits = jnp.where(key_pos[None, :] <= q_pos[:, None], logits, NEG_INF)
        p = jax.nn.softmax(logits, axis=-1)
        return jnp.einsum('bhqk,bkhd->bqhd', p.astype(v.dtype), v)

    o = lax.map(attend_block, (q_blocks, fq_blocks, jnp.arange(nb)))
    o = jnp.moveaxis(o, 0, 1).reshape(b, s, WIDTH_B)
    return o @ w_o

def setup_inputs(seed: int = 0) -> dict:
    key = jax.random.key(seed)
    ks = jax.random.split(key, 24)

    def nrm(k, shape, scale):
        return jax.random.normal(k, shape, jnp.float32) * scale

    def gain(k, shape):
        return 1.0 + 0.02 * jax.random.normal(k, shape, jnp.float32)

    d = D_MODEL
    return {
        'x': nrm(ks[0], (BATCH, SEQ, d), 1.0),
        'c': nrm(ks[1], (BATCH, d), 1.0),
        'w_ada': nrm(ks[2], (DEPTH, d, 6 * d), 0.5 * d ** -0.5),
        'b_ada': nrm(ks[3], (DEPTH, 6 * d), 0.02),
        'g_norm_attn': gain(ks[4], (DEPTH, d)),
        'g_norm_ffn': gain(ks[5], (DEPTH, d)),
        'w_qkv_a': nrm(ks[6], (N_A_LAYERS, d, 3 * N_GROUPS_A * WIDTH_A), d ** -0.5),
        'g_qk_a': gain(ks[7], (N_A_LAYERS, 2, N_GROUPS_A, HEAD_DIM)),
        'w_o_a': nrm(ks[8], (N_A_LAYERS, WIDTH_A, d), WIDTH_A ** -0.5),
        'w_ada_kv': nrm(ks[9], (d, 2 * d), 0.5 * d ** -0.5),
        'b_ada_kv': nrm(ks[10], (2 * d,), 0.02),
        'g_norm_kv': gain(ks[11], (d,)),
        'w_kv': nrm(ks[12], (d, 2 * WIDTH_B), d ** -0.5),
        'g_k_b': gain(ks[13], (HEAD_DIM,)),
        'w_f': nrm(ks[14], (d, N_HEADS_B), 0.5 * d ** -0.5),
        'b_f': jax.random.uniform(ks[15], (N_HEADS_B,), jnp.float32, 1.0, 5.0),
        'w_q_b': nrm(ks[16], (N_B_LAYERS, d, WIDTH_B), d ** -0.5),
        'g_q_b': gain(ks[17], (N_B_LAYERS, HEAD_DIM)),
        'w_o_b': nrm(ks[18], (N_B_LAYERS, WIDTH_B, d), WIDTH_B ** -0.5),
        'w_ffn_in': nrm(ks[19], (DEPTH, d, 2 * D_FF), d ** -0.5),
        'w_ffn_out': nrm(ks[20], (DEPTH, D_FF, d), D_FF ** -0.5),
    }

def reference(x, c, w_ada, b_ada, g_norm_attn, g_norm_ffn, w_qkv_a, g_qk_a, w_o_a,
              w_ada_kv, b_ada_kv, g_norm_kv, w_kv, g_k_b, w_f, b_f, w_q_b, g_q_b, w_o_b,
              w_ffn_in, w_ffn_out):
    s = x.shape[1]
    cos, sin = rope_tables(s)
    c_act = jax.nn.silu(c)
    k_sh = None
    v_sh = None
    f_sh = None
    for layer in range(DEPTH):
        mods = c_act @ w_ada[layer] + b_ada[layer]
        sh_a, sc_a, gt_a, sh_f, sc_f, gt_f = jnp.split(mods, 6, axis=-1)
        h = modulate(rmsnorm(x, g_norm_attn[layer]), sh_a, sc_a)
        if layer < N_A_LAYERS:
            i = layer
            y = dilated_mixture_attention(h, w_qkv_a[i], g_qk_a[i, 0], g_qk_a[i, 1],
                                          w_o_a[i], cos, sin)
        else:
            i = layer - N_A_LAYERS
            y = forgetting_attention(h, w_q_b[i], g_q_b[i], w_o_b[i], k_sh, v_sh, f_sh)
        x = x + gt_a[:, None, :] * y
        h = modulate(rmsnorm(x, g_norm_ffn[layer]), sh_f, sc_f)
        x = x + gt_f[:, None, :] * swiglu(h, w_ffn_in[layer], w_ffn_out[layer])
        if layer == N_A_LAYERS - 1:
            mod_kv = c_act @ w_ada_kv + b_ada_kv
            k_sh, v_sh, f_sh = shared_kv(x, mod_kv, g_norm_kv, w_kv, g_k_b, w_f, b_f)
    return x


_drawn_inputs = setup_inputs


def setup_inputs(seed=0):
    import zlib

    import numpy as np

    out = dict(_drawn_inputs(seed))
    spreads = {}
    factors = {'g_norm_attn': 8.0,
     'g_norm_ffn': 6.483,
     'g_qk_a': 8.0,
     'b_ada_kv': 8.0,
     'g_norm_kv': 8.0,
     'g_k_b': 8.0,
     'w_f': 6.469,
     'g_q_b': 8.0}
    for name, (base, spread) in spreads.items():
        noise = np.random.default_rng([zlib.crc32(name.encode()), seed]).standard_normal(out[name].shape)
        drawn = base * np.exp(spread * noise) if base else spread * noise
        out[name] = jnp.asarray(drawn.astype(out[name].dtype))
    for name, factor in factors.items():
        out[name] = (out[name] * factor).astype(out[name].dtype)
    return out
```

```python
from contextlib import ExitStack, contextmanager

import concourse.bass as bass
from concourse import mybir

P = 128
SEQ, D = 256, 2048
RT = SEQ // P
KT = D // P
CW = 512
GK = 2
RAW = 8
SPLIT = 4
ADA = 4
ADA_W = 1024
GROUPS = 3
HEADS_A = 8
HEADS_B = 16
D_FF = 5632
FJ = D_FF // CW
FFN_OUT_KT = CW // P
NC = D // CW
CG = KT // GK
ADA_BLOCKS_LAYER = 6 * D // ADA_W
EPS = 1e-6
LOWEST = -3.0e38


class Tally:

    def __init__(self, n=0):
        self.n, self.i, self.per = n, None, 0

    def value(self, ahead=0):
        return self.n + ahead if self.i is None else self.i * self.per + (self.n + ahead)

    def step(self, k=1):
        self.n += k
        return self.value()


@contextmanager
def repeat(engine, times, *tallies):
    with engine.Fori(0, times) as i:
        start = [t.n for t, _ in tallies]
        for t, per in tallies:
            t.i, t.per = i, per
        yield i
        for (t, per), n in zip(tallies, start):
            assert t.n == n + per, (t.n, n, per)
            t.i, t.per = None, 0
            t.n = n + per * times


def build(nc, x, c, w_ada, b_ada, g_norm_attn, g_norm_ffn, w_qkv_a, g_qk_a, w_o_a, w_ada_kv, b_ada_kv, g_norm_kv,
          w_kv, g_k_b, w_f, b_f, w_q_b, g_q_b, w_o_b, w_ffn_in, w_ffn_out, rope, mask_a, causal, out):
    f32, f32r = mybir.dt.float32, mybir.dt.float32r
    ALU, ACT, AX = mybir.AluOpType, mybir.ActivationFunctionType, mybir.AxisListType
    ds = bass.ds
    x_spill = nc.dram_tensor("x_spill", (SEQ, D), f32, kind="Internal").ap()

    with ExitStack() as ctx:
        def sb(name, shape, dt=f32):
            return ctx.enter_context(nc.sbuf_tensor(name, shape, dt))

        def sem(name):
            return ctx.enter_context(nc.semaphore(name))

        raw = sb("raw", [P, RAW, GK, CW])
        w_hi = sb("w_hi", [P, SPLIT, GK, CW], f32r)
        w_lo = sb("w_lo", [P, SPLIT, GK, CW], f32r)
        h_hi = sb("h_hi", [P, KT, SEQ], f32r)
        h_lo = sb("h_lo", [P, KT, SEQ], f32r)
        m_hi = sb("m_hi", [P, FFN_OUT_KT, SEQ], f32r)
        m_lo = sb("m_lo", [P, FFN_OUT_KT, SEQ], f32r)
        ada = sb("ada", [P, ADA, ADA_W])
        acc = sb("acc", [P, ADA_W])
        arena = sb("arena", [P, 72 * 256])

        ident = sb("ident", [P, P])
        tri_ones = sb("tri_ones", [P, 2 * P])
        caus = sb("caus", [P, 2 * P])
        cols = sb("cols", [P, 322])
        mods = sb("mods", [P, 14 * KT])
        c_act = sb("c_act", [P, KT])
        gain = sb("gain", [P, KT])
        ss = sb("ss", [P, RT])
        ms = sb("ms", [P, RT])
        rms = sb("rms", [P, RT])
        rstd = sb("rstd", [P, RT])
        ss8 = sb("ss8", [P, 8])
        ms8 = sb("ms8", [P, 8])
        rms8 = sb("rms8", [P, 8])
        rstd8 = sb("rstd8", [P, 8])
        top = sb("top", [P, 2])
        neg_top = sb("neg_top", [P, 2])
        total = sb("total", [P, 2])
        inv_total = sb("inv_total", [P, 2])
        wf_raw = sb("wf_raw", [P, KT, HEADS_B])
        wf_hi = sb("wf_hi", [P, KT, HEADS_B], f32r)
        wf_lo = sb("wf_lo", [P, KT, HEADS_B], f32r)
        bf_rows = sb("bf_rows", [P, HEADS_B])
        gq_scaled = sb("gq_scaled", [P, 1])

        def area(kb, *shape):
            n = 1
            for s in shape:
                n *= s
            flat = arena[:, kb * 256:kb * 256 + n]
            if len(shape) == 1:
                return flat
            names = "abcd"[:len(shape)]
            return flat.rearrange(f"p ({' '.join(names)}) -> p {' '.join(names)}", **dict(zip(names, shape)))

        xs = area(0, RT, D)
        ys = area(16, RT, D)
        yacc = area(16, RT, D)
        vecs = area(52, 3, P)
        qT = area(0, GROUPS * 4, SEQ)
        kT = area(12, GROUPS * 4, SEQ)
        va = area(24, RT, GROUPS, CW)
        oa = area(36, RT, D // 2)
        tq = area(44, 8, P)
        sq = area(48, 8, P)
        s_a = area(52, 2, 3 * SEQ)
        pt_a = area(58, 2, 3 * SEQ)
        msk_a = area(64, RT * GROUPS * SEQ)
        ropes = area(70, 2, P)
        turn4 = area(52, 4, P)
        gate = area(48, D)
        silu = area(56, RT, CW)
        mid = area(60, RT, CW)
        diag = area(60, 2, CW)
        full = [area(64, 4, SEQ), area(68, 4, SEQ)]
        full0 = [area(36, 4, SEQ), area(40, 4, SEQ)]
        qo = area(0, HEADS_B, SEQ)
        fb = area(16, 4, 3, P)
        s_b = area(22, 2, SEQ)
        pt_b = area(24, 2, SEQ)
        bc = area(26, 4, 2, P)
        kTb = area(32, HEADS_B, SEQ)
        vb = area(48, RT, D)
        tqb = area(64, 8, P)
        sqb = area(68, 8, P)
        gqk = sb("gqk", [P, 2, GROUPS * P])
        n_f = RT * HEADS_B
        lf0, lf1, lf2, lf3, z_neg, neg_logf, fq = (
            gqk[:, 0, k * n_f:(k + 1) * n_f].rearrange("p (r h) -> p r h", r=RT) for k in range(7))
        lf = (lf0, lf1, lf2, lf3)

        A, B, C, E = [ctx.enter_context(nc.psum_tensor(f"pair{n}", [P, RT, CW], f32)) for n in "ABCE"]
        PAIR = (A, B, C, E)
        pA, pB, pC, pE = range(4)

        def wide(pair):
            return pair[:, :, :].rearrange("p a n -> p (a n)")

        raw_full = [sem(f"raw_full{k}") for k in range(RAW)]
        ada_full = [sem(f"ada_full{k}") for k in range(ADA)]
        vecs_in = sem("vecs_in")
        consts_in = sem("consts_in")
        x_in = sem("x_in")
        x_spilled = sem("x_spilled")
        stored = sem("stored")
        hi_done = sem("hi_done")
        split_done = sem("split_done")
        mm_done = sem("mm_done")
        ada_done = sem("ada_done")
        col_done = sem("col_done")
        emptied = [sem(f"emptied{n}") for n in "ABCE"]
        turned = sem("turned")
        lhs_hi = sem("lhs_hi")
        lhs_lo = sem("lhs_lo")
        c_done = sem("c_done")
        sumsq = sem("sumsq")
        rms_inv = sem("rms_inv")
        root = sem("root")
        y_done = sem("y_done")
        gain_done = sem("gain_done")
        squared = sem("squared")
        inv8 = sem("inv8")
        root8 = sem("root8")
        roped = sem("roped")
        pool_own = sem("pool_own")
        zeroed = sem("zeroed")
        own = sem("own")
        x_done = sem("x_done")
        diag_done = sem("diag_done")
        ones_done = sem("ones_done")
        gate_done = sem("gate_done")
        qk_done = sem("qk_done")
        top_done = sem("top_done")
        exp_done = sem("exp_done")
        p_turned = sem("p_turned")
        pv_done = sem("pv_done")
        wf_hi_done = sem("wf_hi_done")
        wf_done = sem("wf_done")
        z_done = sem("z_done")
        lf_act = sem("lf_act")
        lf_dve = sem("lf_dve")
        bc_done = sem("bc_done")
        fk_done = sem("fk_done")

        block = ctx.enter_context(nc.Block())


        plan = {}
        OFF_MODS = 0
        OFF_C, OFF_KV, OFF_ATTN, OFF_FFN, OFF_GK, OFF_GQ = 224, 240, 256, 288, 320, 321
        NORMS = [(0, 1, OFF_ATTN), (3, 4, OFF_FFN), (6, 7, OFF_KV), (8, 9, OFF_ATTN + KT), (11, 12, OFF_FFN + KT)]
        GATES = [2, 5, 10, 13]
        MOD_BLOCKS = 14 * D // ADA_W

        def vector(v):
            return mods[:, v * KT:(v + 1) * KT]

        def landed(t, ring):
            v = 16 * (t.n // ring + 1)
            return v if t.i is None else t.i * (t.per // ring * 16) + v

        def keys(qt):
            return (qt + 1) * P

        @block.tensor
        def _(pe):
            pe.sem_inc(mm_done, SPLIT)
            pe.sem_inc(col_done, 1)
            uses = [Tally() for _ in PAIR]
            split_t = Tally(RAW)
            ada_t = Tally(ADA)
            exp_t, y_t, roped_t, diag_t, bc_t = (Tally() for _ in range(5))

            def use(p):
                if uses[p].n:
                    pe.wait_ge(emptied[p], uses[p].value())
                uses[p].step()

            def granule(n, left_hi, left_lo, kt0, pair, first, last):
                pe.wait_ge(split_done, split_t.step())
                for t in range(GK):
                    for r in range(RT):
                        hi = left_hi[:, kt0 + t, r * P:(r + 1) * P]
                        lo = left_lo[:, kt0 + t, r * P:(r + 1) * P]
                        a, z = first and t == 0, last and t == GK - 1
                        nc.tensor.matmul(pair[:, r, :], hi, w_hi[:, n % SPLIT, t, :], start=a, stop=False)
                        nc.tensor.matmul(pair[:, r, :], hi, w_lo[:, n % SPLIT, t, :], start=False, stop=False)
                        mm = nc.tensor.matmul(pair[:, r, :], lo, w_hi[:, n % SPLIT, t, :], start=False, stop=z)
                mm.then_inc(mm_done, 1)

            def chunk(p, n0, norm=None, granules=CG):
                use(p)
                for k in range(granules):
                    if norm is not None and k % 2 == 0:
                        pe.wait_ge(lhs_lo, norm + k // 2 + 1)
                    granule(n0 + k, h_hi, h_lo, k * GK, PAIR[p], k == 0, k == granules - 1)

            def mod_block(p):
                pe.wait_ge(ada_done, ada_t.step(KT))
                use(p)
                for q in range(ADA_W // P):
                    mm = nc.tensor.matmul(PAIR[p][:, 0, q:q + 1], acc[:, q * P:(q + 1) * P], tri_ones[:, P:P + 1],
                                          start=True, stop=True)
                mm.then_inc(col_done, 1)

            def turn(p, tiles):
                use(p)
                for k, tile in enumerate(tiles):
                    mm = nc.tensor.matmul(wide(PAIR[p])[:, k * P:(k + 1) * P], tile, ident[:, :], start=True, stop=True,
                                          is_transpose=True)
                mm.then_inc(turned, 1)

            def turn_norm(e):
                if e != 3:
                    y_t.step(RT)
                pe.wait_ge(y_done, y_t.value())
                plan["norm", e] = [u.n for u in uses]
                for p in range(4):
                    turn(p, [ys[:, r, kt * P:(kt + 1) * P] for kt in range(4 * p, 4 * p + 4) for r in range(RT)])

            def gate_rows(pairs):
                plan["gate", diag_t.n // 4] = pairs, [u.n for u in uses]
                for p in pairs:
                    use(p)
                    for k in range(2):
                        pe.wait_ge(diag_done, diag_t.step())
                        nc.tensor.matmul(PAIR[p][:, k, :], tri_ones[:, P:2 * P], diag[:, k, :], start=True,
                                         stop=True).then_inc(ones_done, 1)

            def attention(steps, scores, probs, outs):
                for n in range(len(steps) + 1):
                    if n < len(steps):
                        use(n % 2)
                        scores(n, *steps[n]).then_inc(qk_done, 1)
                    if n:
                        pe.wait_ge(exp_done, exp_t.step())
                        use(pC)
                        probs(n - 1, *steps[n - 1]).then_inc(p_turned, 1)
                        pe.wait_ge(emptied[pC], uses[pC].value())
                        use(pE)
                        outs(n - 1, *steps[n - 1]).then_inc(pv_done, 1)

            pe.wait_ge(vecs_in, 16 * 10)
            use(pC)
            for k, n in enumerate((P, P, 66)):
                mm = nc.tensor.matmul(C[:, 0, k * P:k * P + n], vecs[0:n, k, :], ident[0:n, 0:n], start=True, stop=True,
                                      is_transpose=True)
            mm.then_inc(turned, 1)
            pe.wait_ge(consts_in, 16 * 7)
            for _ in range(4):
                mod_block(pB)
            turn_norm(0)

            for half in range(2):
                plan["qkv", half] = [u.n for u in uses]
                with repeat(pe, GROUPS, (split_t, 3 * CG), (ada_t, KT), (roped_t, 2), (uses[pA], 1), (uses[pB], 2),
                            (uses[pC], 1), (uses[pE], 2)):
                    chunk(pA, 0, norm=0)
                    chunk(pB, CG)
                    pe.wait_ge(roped, roped_t.step())
                    turn(pE, [tq[:, r * 4 + h, :] for h in range(4) for r in range(RT)])
                    chunk(pC, 2 * CG)
                    pe.wait_ge(roped, roped_t.step())
                    turn(pE, [tq[:, r * 4 + h, :] for h in range(4) for r in range(RT)])
                    mod_block(pB)

                def scores(n, h, qt):
                    for g in range(GROUPS):
                        mm = nc.tensor.matmul(wide(PAIR[n % 2])[:, g * SEQ:g * SEQ + keys(qt)],
                                              qT[:, g * 4 + h, qt * P:(qt + 1) * P], kT[:, g * 4 + h, 0:keys(qt)],
                                              start=True, stop=True)
                    return mm

                def probs(n, h, qt):
                    for g in range(GROUPS):
                        for kt in range(qt + 1):
                            at = g * SEQ + kt * P
                            mm = nc.tensor.matmul(wide(C)[:, at:at + P], s_a[:, n % 2, at:at + P], ident[:, :],
                                                  start=True, stop=True, is_transpose=True)
                    return mm

                def outs(n, h, qt):
                    for g in range(GROUPS):
                        for kt in range(qt + 1):
                            at = g * SEQ + kt * P
                            mm = nc.tensor.matmul(E[:, 0, 0:P], pt_a[:, n % 2, at:at + P],
                                                  va[:, kt, g, h * P:(h + 1) * P], start=g == 0 and kt == 0,
                                                  stop=g == GROUPS - 1 and kt == qt)
                    return mm

                plan["attn", half] = [u.n for u in uses]
                pe.wait_ge(emptied[pC], uses[pC].value())
                pe.wait_ge(emptied[pE], uses[pE].value())
                attention([(h, qt) for h in range(4) for qt in range(RT)], scores, probs, outs)

            pe.wait_ge(emptied[pE], uses[pE].value())
            for p in range(2):
                turn(p, [oa[:, r, kt * P:(kt + 1) * P] for kt in range(4 * p, 4 * p + 4) for r in range(RT)])
            gate_rows((pC, pE))
            for p in range(2):
                pe.wait_ge(emptied[p], uses[p].value())
            with repeat(pe, NC // 2, (split_t, CG), (uses[pA], 1), (uses[pB], 1)):
                chunk(pA, 0, granules=CG // 2)
                chunk(pB, CG // 2, granules=CG // 2)

            def out_chunk(p, n0):
                use(p)
                for k in range(2):
                    granule(n0 + k, m_hi, m_lo, k * GK, PAIR[p], k == 0, k == 1)

            def ffn(e, mod_loop):
                def hidden():
                    pe.wait_ge(emptied[pB], uses[pB].value())
                    turn(pE, [mid[:, r, k * P:(k + 1) * P] for k in range(4) for r in range(RT)])

                chunk(pA, 0, norm=4 * e)
                chunk(pB, CG)
                hidden()
                mod_block(pB)
                tallies = [(split_t, 3 * CG), (uses[pA], 2), (uses[pC], 2), (uses[pE], 2)]
                tallies += [(ada_t, KT), (uses[pB], 2)] if mod_loop else [(uses[pB], 1)]
                with repeat(pe, FJ - 1, *tallies):
                    chunk(pA, 0)
                    chunk(pB, CG)
                    pe.wait_ge(emptied[pE], uses[pE].value())
                    for k, p in enumerate((pC, pE, pA, pC)):
                        out_chunk(p, 2 * CG + 2 * k)
                    hidden()
                    if mod_loop:
                        mod_block(pB)
                gate_rows((pA, pB))
                pe.wait_ge(emptied[pE], uses[pE].value())
                for k, p in enumerate((pC, pE, pA, pC)):
                    out_chunk(p, 2 * k)

            turn_norm(1)
            ffn(1, True)

            turn_norm(2)
            with repeat(pe, 4, (split_t, 2 * CG), (ada_t, KT), (uses[pA], 1), (uses[pB], 1), (uses[pC], 1),
                        (uses[pE], 1)):
                chunk(pA, 0, norm=8)
                chunk(pB, CG)
                pe.wait_ge(emptied[pA], uses[pA].value())
                turn(pE, [tqb[:, r * 4 + h, :] for h in range(4) for r in range(RT)])
                mod_block(pC)
            pe.wait_ge(wf_done, 1)
            plan["z"] = [u.n for u in uses]
            use(pC)
            for r in range(RT):
                for kt in range(KT):
                    for k, (left, right) in enumerate(((h_hi, wf_hi), (h_hi, wf_lo), (h_lo, wf_hi))):
                        mm = nc.tensor.matmul(C[:, r, 0:HEADS_B], left[:, kt, r * P:(r + 1) * P], right[:, kt, :],
                                              start=kt == 0 and k == 0, stop=kt == KT - 1 and k == 2)
            mm.then_inc(z_done, 1)
            turn_norm(3)
            for q in range(4):
                chunk(q % 2, q * CG, norm=12)
                if q:
                    pe.wait_ge(emptied[1 - q % 2], uses[1 - q % 2].value())
                    turn(pE, [tqb[:, r * 4 + h, :] for h in range(4) for r in range(RT)])
                if q == 0:
                    pe.wait_ge(lf_dve, 2)
                    use(pC)
                    nc.tensor.matmul(C[:, 0, 0:HEADS_B], tri_ones[:, 0:P], neg_logf[:, 0, :], start=True, stop=True)
                    nc.tensor.matmul(C[:, 1, 0:HEADS_B], tri_ones[:, P:2 * P], neg_logf[:, 0, :], start=True, stop=False)
                    nc.tensor.matmul(C[:, 1, 0:HEADS_B], tri_ones[:, 0:P], neg_logf[:, 1, :], start=False,
                                     stop=True).then_inc(z_done, 1)
            mod_block(pC)
            pe.wait_ge(emptied[pB], uses[pB].value())
            turn(pE, [tqb[:, r * 4 + h, :] for h in range(4) for r in range(RT)])

            for hg in range(4):
                pe.wait_ge(bc_done, bc_t.step())
                plan["fk", hg] = [u.n for u in uses]
                use(pC)
                for h in range(4):
                    at = wide(C)[:, h * SEQ:(h + 1) * SEQ]
                    nc.tensor.matmul(at[:, 0:P], bc[:, h, 0, :], tri_ones[:, 0:P], start=True, stop=True)
                    nc.tensor.matmul(at[:, P:2 * P], bc[:, h, 0, :], tri_ones[:, P:2 * P], start=True, stop=False)
                    mm = nc.tensor.matmul(at[:, P:2 * P], bc[:, h, 1, :], tri_ones[:, 0:P], start=False, stop=True)
                mm.then_inc(fk_done, 1)
                pe.wait_ge(emptied[pE], uses[pE].value())

                def scores(n, h, qt):
                    return nc.tensor.matmul(PAIR[n % 2][:, 0, 0:keys(qt)], qo[:, h, qt * P:(qt + 1) * P],
                                            kTb[:, h, 0:keys(qt)], start=True, stop=True)

                def probs(n, h, qt):
                    for kt in range(qt + 1):
                        mm = nc.tensor.matmul(C[:, 0, kt * P:(kt + 1) * P], s_b[:, n % 2, kt * P:(kt + 1) * P],
                                              ident[:, :], start=True, stop=True, is_transpose=True)
                    return mm

                def outs(n, h, qt):
                    for kt in range(qt + 1):
                        mm = nc.tensor.matmul(E[:, 0, 0:P], pt_b[:, n % 2, kt * P:(kt + 1) * P],
                                              vb[:, kt, h * P:(h + 1) * P], start=kt == 0, stop=kt == qt)
                    return mm

                plan["attn_b", hg] = [u.n for u in uses]
                attention([(4 * hg + h, qt) for h in range(4) for qt in range(RT)], scores, probs, outs)

            pe.wait_ge(emptied[pE], uses[pE].value())
            mod_block(pE)
            for p in range(4):
                turn(p, [qo[:, kt, r * P:(r + 1) * P] for kt in range(4 * p, 4 * p + 4) for r in range(RT)])
            gate_rows((pC, pE))
            for p in range(2):
                pe.wait_ge(emptied[p], uses[p].value())
            with repeat(pe, NC // 2, (split_t, 2 * CG), (uses[pA], 1), (uses[pB], 1)):
                chunk(pA, 0)
                chunk(pB, CG)
            turn_norm(4)
            ffn(4, False)

        @block.sync
        def _(sp):
            used = Tally()
            m = Tally()

            def load(n, src):
                if used.n >= RAW:
                    sp.wait_ge(split_done, used.value(1))
                sp.dma_start(raw[:, n % RAW], src).then_inc(raw_full[n % RAW], 16)
                used.step()

            def load_ada(src):
                if m.n >= ADA:
                    sp.wait_ge(ada_done, m.value(1))
                slot = m.n % ADA
                sp.dma_start(ada[:, slot], src).then_inc(ada_full[slot], 16)
                m.step()

            def rows(w, g):
                return w[g * GK * P:(g + 1) * GK * P, :].rearrange("(t p) n -> p t n", p=P)

            def ada_src(w, kt, block_at):
                return w[kt * P:(kt + 1) * P, ds(block_at * ADA_W, ADA_W)]

            w_mod = [w_ada[0], w_ada_kv, w_ada[1]]
            by_tile = lambda t: t.rearrange("(a p) n -> p a n", p=P)

            def vec(row, tile, src, n):
                sp.dma_start(vecs[row:row + n, tile, :], src.rearrange("(a b) -> a b", b=P)).then_inc(vecs_in, 16)

            vec(0, 0, b_ada[0], 96)
            vec(96, 0, b_ada_kv, 32)
            vec(0, 1, b_ada[1], 96)
            vec(96, 1, c[0], 16)
            vec(112, 1, g_norm_kv, 16)
            vec(0, 2, g_norm_attn.rearrange("a b -> (a b)"), 32)
            vec(32, 2, g_norm_ffn.rearrange("a b -> (a b)"), 32)
            vec(64, 2, g_k_b, 1)
            vec(65, 2, g_q_b[0], 1)
            sp.dma_start(ident[:, :], causal[:, 2 * P:3 * P]).then_inc(vecs_in, 16)
            for kt in range(ADA):
                load_ada(ada_src(w_mod[0], kt, 0))
            sp.dma_start(xs, by_tile(x[0])).then_inc(x_in, 16)
            sp.dma_start(tri_ones[:, :], causal[:, 3 * P:5 * P]).then_inc(consts_in, 16)
            sp.dma_start(caus[:, :], causal[:, 0:2 * P]).then_inc(consts_in, 16)
            sp.dma_start(msk_a, mask_a).then_inc(consts_in, 16)
            sp.dma_start(ropes.rearrange("p a b -> p (a b)"), rope).then_inc(consts_in, 16)
            sp.dma_start(gqk[:, :, :].rearrange("p a b -> p (a b)"),
                         g_qk_a.rearrange("l a b d -> (l a b d)").partition_broadcast(P)).then_inc(consts_in, 16)
            sp.dma_start(wf_raw[:, :, :], w_f.rearrange("(k p) n -> p k n", p=P)).then_inc(consts_in, 16)
            sp.dma_start(bf_rows[:, :], b_f.partition_broadcast(P)).then_inc(consts_in, 16)
            for k in range(ADA, 4 * KT):
                load_ada(ada_src(w_mod[0], k % KT, k // KT))

            for half in range(2):
                if half == 0:
                    for n in range(CG):
                        load(n, rows(w_qkv_a[0], n)[:, :, 0:CW])
                first = CG if half == 0 else 0
                for lo_g, hi_g in ((0, 1), (1, GROUPS)) if half == 0 else ((0, GROUPS),):
                    with repeat(sp, hi_g - lo_g, (used, 3 * CG - (first if lo_g == 0 else 0)), (m, KT)) as g:
                        for n in range(first if lo_g == 0 else 0, 3 * CG):
                            at = (g + lo_g) * (HEADS_A * P) + (n // CG * GROUPS * HEADS_A * P + half * CW)
                            load(n, rows(w_qkv_a[0], n % CG)[:, :, ds(at, CW)])
                            if n >= CG:
                                load_ada(ada_src(w_mod[0], n - CG, g + (lo_g + 4 + GROUPS * half)))
            for n in range(2 * CG):
                if n == CG:
                    sp.wait_ge(turned, 1 + 4 + 12 + 2)
                    sp.dma_start(xs, by_tile(x[0])).then_inc(x_in, 16)
                k = n % (CG // 2)
                load(n, rows(w_o_a[0], k)[:, :, n // (CG // 2) * CW:(n // (CG // 2) + 1) * CW])

            def ffn(layer, passes, first_block):
                wi, wo = w_ffn_in[layer], w_ffn_out[layer]
                for n in range(2 * CG):
                    load(n, rows(wi, n % CG)[:, :, n // CG * D_FF:n // CG * D_FF + CW])
                    if n >= CG:
                        for k in range(2):
                            load_ada(ada_src(w_mod[first_block[0]], 2 * (n - CG) + k, first_block[1]))
                done = 0
                for times, which, first in passes:
                    with repeat(sp, times, (used, 3 * CG), *([(m, KT)] if which is not None else [])) as i:
                        for n in range(3 * CG):
                            if n < 2 * CG:
                                at = i * CW + (n // CG * D_FF + (done + 1) * CW)
                                load(n, rows(wi, n % CG)[:, :, ds(at, CW)])
                            else:
                                q, k = (n - 2 * CG) // 2, n % 2
                                hidden = wo.rearrange("(j k t p) n -> k p t j n", p=P, t=GK, k=2)[k]
                                src = hidden[:, :, ds(i + done, 1), q * CW:(q + 1) * CW]
                                load(n, src.rearrange("p t j n -> p t (j n)"))
                            if which is not None and n >= CG:
                                load_ada(ada_src(w_mod[which], n - CG, i + first))
                    done += times
                for n in range(CG):
                    q, k = n // 2, n % 2
                    at = (FJ - 1) * CW + k * GK * P
                    load(n, wo[at:at + GK * P, q * CW:(q + 1) * CW].rearrange("(t p) n -> p t n", p=P))

            ffn(0, [(1, 0, 11), (4, 1, 0), (5, 2, 0)], (0, 10))
            with repeat(sp, 4, (used, 2 * CG), (m, KT)) as i:
                for n in range(2 * CG):
                    load(n, rows(w_kv, n % CG)[:, :, ds(i * CW + n // CG * D, CW)])
                    if n >= CG:
                        for k in range(2):
                            load_ada(ada_src(w_mod[2], 2 * (n - CG) + k, i + 5))
            sp.wait_ge(x_done, 8)
            sp.dma_start(by_tile(x_spill), xs).then_inc(x_spilled, 16)
            for n in range(4 * CG):
                load(n, rows(w_q_b[0], n % CG)[:, :, n // CG * CW:(n // CG + 1) * CW])
                if n % CG >= 4:
                    load_ada(ada_src(w_mod[2], n // CG * 4 + n % CG - 4, 9))
            for n in range(4 * CG):
                if n == CG:
                    for kt in range(KT):
                        load_ada(ada_src(w_mod[2], kt, 10))
                    sp.wait_ge(turned, 54)
                    sp.wait_ge(x_spilled, 16)
                    sp.dma_start(xs, by_tile(x_spill)).then_inc(x_in, 16)
                load(n, rows(w_o_b[0], n % CG)[:, :, n // CG * CW:(n // CG + 1) * CW])
            ffn(1, [(FJ - 1, None, 0)], (2, 11))
            for q in range(NC):
                sp.wait_ge(x_done, 12 + q + 1)
                sp.dma_start(by_tile(out[0])[:, :, q * CW:(q + 1) * CW], xs[:, :, q * CW:(q + 1) * CW]
                             ).then_inc(stored, 16)
            sp.wait_ge(stored, 16 * NC)

        @block.scalar
        def _(act):
            w_t = Tally()
            turned_t, p_t, top_t, lo_t, root_t, gain_t, inv8_t, ones_t = (Tally() for _ in range(8))

            def split(k):
                act.wait_ge(raw_full[k % RAW], landed(w_t, RAW))
                act.wait_ge(mm_done, w_t.value(1))
                nc.scalar.activation(w_hi[:, k % SPLIT], raw[:, k % RAW], ACT.Copy).then_inc(hi_done, 1)
                w_t.step()

            def round_lhs(p, into):
                act.wait_ge(turned, turned_t.step())
                nc.scalar.activation(into, wide(PAIR[p]), ACT.Copy).then_inc(lhs_hi, 1)

            def norm(e, full):
                shift, _, _ = NORMS[e]
                if e != 3:
                    if e == 0:
                        act.wait_ge(x_in, 16)
                    else:
                        act.wait_ge(x_done, {1: 4, 2: 8, 4: 12}[e])
                    for r in range(RT):
                        ins = nc.scalar.activation(ys[:, r, :], xs[:, r, :], ACT.Square, accum_out=ss[:, r:r + 1])
                    ins.then_inc(sumsq, 1)
                    act.wait_ge(rms_inv, root_t.step())
                    nc.scalar.activation(rstd[:, :], rms[:, :], ACT.Sqrt).then_inc(root, 1)
                act.wait_ge(gain_done, gain_t.step())
                for p in range(4):
                    act.wait_ge(turned, turned_t.step())
                    if p % 2 == 0:
                        if p:
                            act.wait_ge(lhs_lo, lo_t.value(1))
                        for k in range(4):
                            kt = 4 * p + k
                            ins = nc.scalar.activation(full[p % 2][:, k, :], wide(PAIR[p])[:, k * SEQ:(k + 1) * SEQ],
                                                       ACT.Identity, scale=gain[:, kt:kt + 1],
                                                       bias=vector(shift)[:, kt:kt + 1])
                        ins.then_inc(emptied[p], 1)
                        act.wait_ge(emptied[p], plan["norm", e][p] + 1)
                    else:
                        act.wait_ge(emptied[p], plan["norm", e][p] + 1)
                    nc.scalar.activation(h_hi[:, 4 * p:4 * p + 4, :], full[p % 2], ACT.Copy).then_inc(lhs_hi, 1)
                lo_t.step(4)

            def keep_gate():
                pairs = plan["gate", ones_t.n // 4][0]
                for k in range(4):
                    p = pairs[k // 2]
                    act.wait_ge(ones_done, ones_t.step())
                    ins = nc.scalar.activation(gate[:, k * CW:(k + 1) * CW], PAIR[p][:, k % 2, :], ACT.Copy)
                    ins.then_inc(gate_done if k % 2 == 0 else emptied[p], 1)

            def attention(n_steps, s_tile, pt_tile, n_groups):
                def view(t, qt):
                    return t.rearrange("p (g k) -> p g k", g=n_groups)[:, :, 0:keys(qt)]

                def turn_back(n):
                    act.wait_ge(p_turned, p_t.step())
                    nc.scalar.activation(view(pt_tile[:, n % 2], n % 2), view(wide(C)[:, 0:n_groups * SEQ], n % 2),
                                         ACT.Copy).then_inc(emptied[pC], 1)

                for n in range(n_steps + 1):
                    if n < n_steps:
                        act.wait_ge(top_done, top_t.step())
                        s = view(s_tile[:, n % 2], n % 2)
                        nc.scalar.activation(s, s, ACT.Exp, bias=neg_top[:, n % 2:n % 2 + 1],
                                             accum_out=total[:, n % 2:n % 2 + 1]).then_inc(exp_done, 1)
                    if n:
                        turn_back(n - 1)

            def square(p, into):
                act.wait_ge(mm_done, w_t.value())
                nc.scalar.activation(into, PAIR[p][:, :, :], ACT.Square).then_inc(squared, 1)

            def root_heads():
                act.wait_ge(inv8, inv8_t.step())
                nc.scalar.activation(rstd8[:, :], rms8[:, :], ACT.Sqrt).then_inc(root8, 1)

            act.wait_ge(emptied[pC], 1)
            nc.scalar.activation(c_act[:, :], cols[:, OFF_C:OFF_C + KT], ACT.Silu).then_inc(c_done, 1)
            act.wait_ge(consts_in, 16 * 7)
            nc.scalar.activation(wf_hi[:, :, :], wf_raw[:, :, :], ACT.Copy).then_inc(wf_hi_done, 1)
            turned_t.step()
            norm(0, full0)
            for k in range(SPLIT):
                split(k)

            for half in range(2):
                with repeat(act, GROUPS, (w_t, 3 * CG), (turned_t, 2), (inv8_t, 2)) as g:
                    for k in range(3 * CG):
                        split(SPLIT + k)
                        if k == 7:
                            square(pA, sq)
                        if k == 8:
                            root_heads()
                        if k == 15:
                            square(pB, sq)
                        if k == 16:
                            act.wait_ge(turned, turned_t.step())
                            act.wait_ge(turned, 1)
                            nc.scalar.activation(qT[:, ds(g * 4, 4), :].rearrange("p a b -> p (a b)"), wide(E), ACT.Copy,
                                                 scale=float(P) ** -0.5).then_inc(emptied[pE], 1)
                            root_heads()
                    act.wait_ge(turned, turned_t.step())
                    act.wait_ge(turned, 1)
                    nc.scalar.activation(va[:, :, ds(g, 1), :].rearrange("p r g n -> p r (g n)"), C[:, :, :], ACT.Copy
                                         ).then_inc(emptied[pC], 1)
                    nc.scalar.activation(kT[:, ds(g * 4, 4), :].rearrange("p a b -> p (a b)"), wide(E), ACT.Copy
                                         ).then_inc(emptied[pE], 1)
                attention(8, s_a, pt_a, GROUPS)
            for p in range(2):
                round_lhs(p, h_hi[:, 4 * p:4 * p + 4, :])
            keep_gate()
            with repeat(act, 2, (w_t, CG)):
                for k in range(CG):
                    split(SPLIT + k)

            def ffn():
                def half_hidden(k0, n):
                    for k in range(n):
                        split(SPLIT + k0 + k)
                        if k0 + k == 8:
                            act.wait_ge(mm_done, w_t.value())
                            nc.scalar.activation(silu, A[:, :, :], ACT.Silu).then_inc(emptied[pA], 1)

                half_hidden(0, 2 * CG)
                round_lhs(pE, m_hi[:, :, :])
                with repeat(act, FJ - 1, (w_t, 3 * CG), (turned_t, 1)):
                    half_hidden(0, 3 * CG)
                    round_lhs(pE, m_hi[:, :, :])
                keep_gate()

            norm(1, full)
            ffn()
            for k in range(CG):
                split(SPLIT + k)
            norm(2, full)
            with repeat(act, 4, (w_t, 2 * CG), (turned_t, 1), (inv8_t, 1)) as i:
                for k in range(2 * CG):
                    split(SPLIT + k)
                    if k == 7:
                        square(pA, sqb)
                    if k == 8:
                        root_heads()
                act.wait_ge(turned, turned_t.step())
                act.wait_ge(turned, 1)
                nc.scalar.activation(vb[:, :, ds(i * CW, CW)], B[:, :, :], ACT.Copy).then_inc(emptied[pB], 1)
                nc.scalar.activation(kTb[:, ds(i * 4, 4), :].rearrange("p a b -> p (a b)"), wide(E), ACT.Copy,
                                     scale=cols[:, OFF_GK:OFF_GK + 1]).then_inc(emptied[pE], 1)
            act.wait_ge(lf_dve, 1)
            nc.scalar.activation(lf[1][:, :, :], lf[0][:, :, :], ACT.Abs).then_inc(lf_act, 1)
            act.wait_ge(lf_act, 1)
            nc.scalar.activation(lf[2][:, :, :], lf[1][:, :, :], ACT.Exp, scale=-1.0).then_inc(lf_act, 1)
            act.wait_ge(lf_act, 2)
            nc.scalar.activation(lf[3][:, :, :], lf[2][:, :, :], ACT.Ln, bias=1.0).then_inc(lf_act, 1)
            norm(3, full)

            def keep_q(q):
                act.wait_ge(turned, turned_t.step())
                if q == 0:
                    act.wait_ge(x_spilled, 16)
                nc.scalar.activation(qo[:, 4 * q:4 * q + 4, :].rearrange("p a b -> p (a b)"), wide(E), ACT.Copy,
                                     scale=gq_scaled[:, 0:1]).then_inc(emptied[pE], 1)

            for q in range(4):
                for k in range(CG):
                    split(SPLIT + k)
                square(q % 2, sqb)
                root_heads()
                if q:
                    keep_q(q - 1)
            keep_q(3)
            for hg in range(4):
                if hg == 0:
                    act.wait_ge(lf_dve, 2)
                for h in range(4):
                    for j in range(RT):
                        ins = nc.scalar.activation(bc[:, h, j, :], tri_ones[:, P:2 * P], ACT.Copy,
                                                   scale=neg_logf[:, j, 4 * hg + h:4 * hg + h + 1])
                ins.then_inc(bc_done, 1)
                attention(8, s_b, pt_b, 1)
            for p in range(4):
                round_lhs(p, h_hi[:, 4 * p:4 * p + 4, :])
            keep_gate()
            with repeat(act, 2, (w_t, 2 * CG)):
                for k in range(2 * CG):
                    split(SPLIT + k)
            norm(4, full)
            ffn()
            for k in range(CG - SPLIT):
                split(SPLIT + k)

        @block.vector
        def _(dve):
            dve.sem_inc(split_done, RAW)
            dve.sem_inc(ada_done, ADA)
            lo_t = Tally()
            m_t = Tally()
            blk_t = Tally()
            own_t, turned_t, lhs_hi_t, lhs_lo_t, sq_t, root8_t, root_t = (Tally() for _ in range(7))
            qk_t, exp_t, pv_t, ones_t, silu_t = (Tally() for _ in range(5))

            def chained(ins):
                ins.then_inc(own, 1)
                dve.wait_ge(own, own_t.step())

            def split(k):
                dve.wait_ge(hi_done, lo_t.value(1))
                nc.vector.tensor_tensor(w_lo[:, k % SPLIT], raw[:, k % RAW], w_hi[:, k % SPLIT].bitcast(f32),
                                        ALU.subtract).then_inc(split_done, 1)
                lo_t.step()

            def modulate():
                slot, kt = m_t.n % ADA, m_t.n % KT
                dve.wait_ge(ada_full[slot], landed(m_t, ADA))
                if kt == 0:
                    done = m_t.n // KT + 1
                    dve.wait_ge(col_done, done if m_t.i is None else m_t.i * (m_t.per // KT) + done)
                    ins = nc.vector.tensor_scalar(acc[:, :], ada[:, slot], c_act[:, 0:1], None, ALU.mult)
                else:
                    dve.wait_ge(ada_done, m_t.value(ADA))
                    ins = nc.vector.scalar_tensor_tensor(out=acc[:, :], in0=ada[:, slot], scalar=c_act[:, kt:kt + 1],
                                                         in1=acc[:, :], op0=ALU.mult, op1=ALU.add)
                ins.then_inc(ada_done, 1)
                m_t.step()

            def keep_block(p):
                n = ADA_W // P
                at = blk_t.value() * n
                dve.wait_ge(col_done, blk_t.value(2))
                nc.vector.tensor_tensor(mods[:, ds(at, n)], PAIR[p][:, 0, 0:n], cols[:, ds(at, n)], ALU.add
                                        ).then_inc(emptied[p], 1)
                blk_t.step()

            def norm_stats():
                dve.wait_ge(sumsq, root_t.value(1))
                chained(nc.vector.tensor_scalar(ms[:, :], ss[:, :], 1.0 / D, EPS, ALU.mult, ALU.add))
                nc.vector.reciprocal(rms[:, :], ms[:, :]).then_inc(rms_inv, 1)
                dve.wait_ge(root, root_t.step())
                for r in range(RT):
                    nc.vector.tensor_scalar(ys[:, r, :], xs[:, r, :], rstd[:, r:r + 1], None, ALU.mult
                                            ).then_inc(y_done, 1)

            def norm_gain(e):
                _, scale, g = NORMS[e]
                nc.vector.scalar_tensor_tensor(out=gain[:, :], in0=vector(scale), scalar=1.0, in1=cols[:, g:g + KT],
                                               op0=ALU.add, op1=ALU.mult).then_inc(gain_done, 1)

            def norm_split(e, full):
                shift, _, _ = NORMS[e]

                def modulated(p):
                    dve.wait_ge(turned, turned_t.value(p + 1))
                    for k in range(4):
                        kt = 4 * p + k
                        ins = nc.vector.tensor_scalar(full[1][:, k, :], wide(PAIR[p])[:, k * SEQ:(k + 1) * SEQ],
                                                      gain[:, kt:kt + 1], vector(shift)[:, kt:kt + 1], ALU.mult,
                                                      ALU.add)
                    ins.then_inc(emptied[p], 1)

                def lo(p):
                    dve.wait_ge(lhs_hi, lhs_hi_t.step())
                    nc.vector.tensor_tensor(h_lo[:, 4 * p:4 * p + 4, :], full[p % 2],
                                            h_hi[:, 4 * p:4 * p + 4, :].bitcast(f32), ALU.subtract
                                            ).then_inc(lhs_lo, 1)
                    lhs_lo_t.step()

                dve.wait_ge(gain_done, e + 1)
                modulated(1)
                lo(0)
                lo(1)
                dve.wait_ge(lhs_lo, lhs_lo_t.value())
                modulated(3)
                lo(2)
                lo(3)
                turned_t.step(4)

            def lo_of(p, hi, lo):
                dve.wait_ge(lhs_hi, lhs_hi_t.step())
                nc.vector.tensor_tensor(lo, wide(PAIR[p]), hi.bitcast(f32), ALU.subtract).then_inc(emptied[p], 1)

            def head_stats(squares):
                dve.wait_ge(squared, sq_t.step())
                chained(nc.vector.reduce_sum(ss8[:, :], squares, AX.X))
                chained(nc.vector.tensor_scalar(ms8[:, :], ss8[:, :], 1.0 / P, EPS, ALU.mult, ALU.add))
                nc.vector.reciprocal(rms8[:, :], ms8[:, :]).then_inc(inv8, 1)

            def head_scale(p, into):
                dve.wait_ge(root8, root8_t.step())
                dve.wait_ge(turned, turned_t.value())
                nc.vector.tensor_tensor(into, wide(PAIR[p]).rearrange("p (h d) -> p h d", d=P),
                                        rstd8[:, :].unsqueeze(2).to_broadcast([P, 8, P]), ALU.mult
                                        ).then_inc(emptied[p], 1)

            def diagonal(v, k):
                if k >= 2:
                    dve.wait_ge(ones_done, ones_t.value(k - 1))
                nc.vector.tensor_tensor(diag[:, k % 2].rearrange("p (a b) -> p a b", b=P),
                                        ident[:, :].unsqueeze(1).to_broadcast([P, 4, P]),
                                        vector(v)[:, 4 * k:4 * k + 4].unsqueeze(2).to_broadcast([P, 4, P]), ALU.mult
                                        ).then_inc(diag_done, 1)

            def gate_ready(n):
                pairs, before = plan["gate", n]
                dve.wait_ge(emptied[pairs[1]], before[pairs[1]] + 1)

            def add_gated(p, at):
                dve.wait_ge(mm_done, mm_at.value())
                dve.wait_ge(split_done, lo_t.value(RAW))
                for r in range(RT):
                    ins = nc.vector.tensor_tensor(silu[:, r, :], PAIR[p][:, r, :], gate[:, ds(at, CW)], ALU.mult)
                chained(ins)
                for r in range(RT):
                    nc.vector.tensor_tensor(xs[:, r, ds(at, CW)], xs[:, r, ds(at, CW)], silu[:, r, :], ALU.add
                                            ).then_inc(x_done if r else emptied[p], 1)

            def attention(heads, s_tile, bias, n_groups, key, o_rows, with_ada):
                before = plan[key]

                def view(t, qt):
                    return t.rearrange("p (g k) -> p g k", g=n_groups)[:, :, 0:keys(qt)]

                steps = [(h, qt) for h in heads for qt in range(RT)]
                for n in range(len(steps) + 1):
                    if n < len(steps):
                        h, qt = steps[n]
                        dve.wait_ge(qk_done, qk_t.step())
                        nc.vector.tensor_tensor_reduce(
                            out=view(s_tile[:, n % 2], qt), in0=view(wide(PAIR[n % 2])[:, 0:n_groups * SEQ], qt),
                            in1=bias(h, qt), scale=1.0, scalar=LOWEST, op0=ALU.add, op1=ALU.max,
                            accum_out=top[:, n % 2:n % 2 + 1]).then_inc(emptied[n % 2], 1)
                        dve.wait_ge(emptied[n % 2], before[n % 2] + n // 2 + 1)
                        nc.vector.tensor_scalar(neg_top[:, n % 2:n % 2 + 1], top[:, n % 2:n % 2 + 1], -1.0, None,
                                                ALU.mult).then_inc(top_done, 1)
                        if with_ada and n % 2:
                            modulate()
                    if n:
                        h, qt = steps[n - 1]
                        o = (n - 1) % 2
                        dve.wait_ge(exp_done, exp_t.step())
                        chained(nc.vector.reciprocal(inv_total[:, o:o + 1], total[:, o:o + 1]))
                        dve.wait_ge(pv_done, pv_t.step())
                        nc.vector.tensor_scalar(o_rows(h, qt), E[:, 0, 0:P], inv_total[:, o:o + 1], None, ALU.mult
                                                ).then_inc(emptied[pE], 1)

            dve.wait_ge(turned, turned_t.step())
            nc.vector.tensor_copy(cols[:, :], C[:, 0, 0:322]).then_inc(emptied[pC], 1)
            dve.wait_ge(emptied[pC], 1)
            chained(nc.vector.tensor_scalar(gq_scaled[:, :], cols[:, OFF_GQ:OFF_GQ + 1], float(P) ** -0.5, None,
                                            ALU.mult))
            dve.wait_ge(c_done, 1)
            for b in range(4):
                for _ in range(KT):
                    modulate()
                keep_block(pB)
                if b == 0:
                    norm_stats()
                    dve.wait_ge(wf_hi_done, 1)
                    nc.vector.tensor_tensor(wf_lo[:, :, :], wf_raw[:, :, :], wf_hi[:, :, :].bitcast(f32), ALU.subtract
                                            ).then_inc(wf_done, 1)
            dve.wait_ge(emptied[pB], 4)
            norm_gain(0)
            norm_split(0, full0)
            for k in range(SPLIT):
                split(k)

            for half in range(2):
                with repeat(dve, GROUPS, (lo_t, 3 * CG), (m_t, KT), (blk_t, 1), (own_t, 4), (turned_t, 2), (sq_t, 2),
                            (root8_t, 2)):
                    for k in range(3 * CG):
                        split(SPLIT + k)
                        if k < KT:
                            modulate()
                        if k in (7, 16):
                            head_stats(sq)
                        if k == 9:
                            head_scale(pA, tq)
                            turned_t.step()
                        if k == 18:
                            head_scale(pB, tq)
                            turned_t.step()
                    keep_block(pB)
                masks = msk_a.rearrange("p (r g k) -> p r g k", r=RT, g=GROUPS)
                attention(range(4), s_a, lambda h, qt: masks[:, qt, :, 0:keys(qt)], GROUPS, ("attn", half),
                          lambda h, qt, half=half: oa[:, qt, (4 * half + h) * P:(4 * half + h + 1) * P], False)
            diagonal(GATES[0], 0)
            diagonal(GATES[0], 1)
            for p in range(2):
                lo_of(p, h_hi[:, 4 * p:4 * p + 4, :].rearrange("p a b -> p (a b)"),
                      h_lo[:, 4 * p:4 * p + 4, :].rearrange("p a b -> p (a b)"))
            turned_t.step(2)
            diagonal(GATES[0], 2)
            diagonal(GATES[0], 3)
            ones_t.step(4)
            gate_ready(0)
            dve.wait_ge(x_in, 32)
            mm_at = Tally(SPLIT + lo_t.n - SPLIT)
            with repeat(dve, 2, (lo_t, CG), (own_t, 2), (mm_at, CG)) as i:
                for k in range(CG):
                    split(SPLIT + k)
                    mm_at.step()
                    if k % 4 == 3:
                        add_gated(k // 4, i * (2 * CW) + k // 4 * CW)

            def ffn(e, layer, mod_loop):
                def upper(k0, n, out_k, ada_at):
                    for k in range(n):
                        split(SPLIT + k0 + k)
                        for _ in range(ada_at(k)):
                            modulate()
                        if k0 + k == 2 * CG - 1 and out_k is None or k0 + k == 2 * CG and out_k is not None:
                            dve.wait_ge(emptied[pA], a_t.value(1))
                            chained(nc.vector.tensor_tensor(mid[:, 0, :], silu[:, 0, :], B[:, 0, :], ALU.mult))
                            nc.vector.tensor_tensor(mid[:, 1, :], silu[:, 1, :], B[:, 1, :], ALU.mult
                                                    ).then_inc(emptied[pB], 1)
                        if out_k is not None and k >= 2 * CG and k % 2:
                            q = (k - 2 * CG) // 2
                            p = (pC, pE, pA, pC)[q]
                            at = yacc[:, :, q * CW:(q + 1) * CW]
                            nc.vector.tensor_tensor(at, PAIR[p][:, :, :], at, ALU.add).then_inc(emptied[p], 1)
                    a_t.step(1 if out_k is None else 2)

                a_t = Tally(plan["norm", e][pA] + 1)
                upper(0, 2 * CG, None, lambda k: 2 if k < CG else 0)
                lo_of(pE, m_hi[:, :, :].rearrange("p a b -> p (a b)"), m_lo[:, :, :].rearrange("p a b -> p (a b)"))
                keep_block(pB)
                turned_t.step()
                dve.wait_ge(zeroed, layer + 1)
                tallies = [(lo_t, 3 * CG), (own_t, 1), (lhs_hi_t, 1), (turned_t, 1), (a_t, 2)]
                tallies += [(m_t, KT), (blk_t, 1)] if mod_loop else []
                with repeat(dve, FJ - 1, *tallies):
                    upper(0, 3 * CG, True, lambda k: 1 if mod_loop and k < KT else 0)
                    lo_of(pE, m_hi[:, :, :].rearrange("p a b -> p (a b)"),
                          m_lo[:, :, :].rearrange("p a b -> p (a b)"))
                    if mod_loop:
                        keep_block(pB)
                    turned_t.step()
                if not mod_loop:
                    pass
                for k in range(4):
                    diagonal(GATES[2 * layer + 1], k)
                ones_t.step(4)
                last = layer == 1
                n0 = lo_t.n - SPLIT
                for k in range(CG):
                    if k < SPLIT or not last:
                        split(SPLIT + k)
                    if k % 2:
                        q = k // 2
                        p = (pC, pE, pA, pC)[q]
                        if q == 0:
                            gate_ready(2 * layer + 1)
                        dve.wait_ge(mm_done, SPLIT + n0 + k + 1)
                        at = slice(q * CW, (q + 1) * CW)
                        if q:
                            dve.wait_ge(x_done, 8 * layer + 4 + q)
                        chained(nc.vector.tensor_tensor(yacc[:, :, at], PAIR[p][:, :, :], yacc[:, :, at], ALU.add))
                        for r in range(RT):
                            ins = nc.vector.tensor_tensor(silu[:, r, :], yacc[:, r, at], gate[:, at], ALU.mult)
                        chained(ins)
                        for r in range(RT):
                            nc.vector.tensor_tensor(xs[:, r, at], xs[:, r, at], silu[:, r, :], ALU.add
                                                    ).then_inc(x_done if r else emptied[p], 1)

            norm_stats()
            norm_gain(1)
            norm_split(1, full)
            ffn(1, 0, True)

            norm_stats()
            norm_gain(2)
            norm_split(2, full)
            with repeat(dve, 4, (lo_t, 2 * CG), (m_t, KT), (blk_t, 1), (own_t, 2), (turned_t, 1), (sq_t, 1),
                        (root8_t, 1)):
                for k in range(2 * CG):
                    split(SPLIT + k)
                    if k < CG:
                        modulate()
                        modulate()
                    if k == 7:
                        head_stats(sqb)
                    if k == 9:
                        head_scale(pA, tqb)
                        turned_t.step()
                keep_block(pC)
            dve.wait_ge(z_done, 1)
            for r in range(RT):
                ins = nc.vector.tensor_tensor(lf[0][:, r, :], C[:, r, 0:HEADS_B], bf_rows[:, :], ALU.add)
            ins.then_inc(emptied[pC], 1)
            dve.wait_ge(emptied[pC], plan["z"][pC] + 1)
            chained(nc.vector.tensor_scalar(z_neg[:, :, :], lf[0][:, :, :], 0.0, None, ALU.min))
            nc.vector.tensor_scalar(z_neg[:, :, :], z_neg[:, :, :], -1.0, None, ALU.mult).then_inc(lf_dve, 1)
            norm_gain(3)
            norm_split(3, full)
            dve.wait_ge(lf_act, 3)
            nc.vector.tensor_tensor(neg_logf[:, :, :], lf[3][:, :, :], z_neg[:, :, :], ALU.add).then_inc(lf_dve, 1)
            for q in range(4):
                for k in range(CG):
                    split(SPLIT + k)
                    if k < 4:
                        modulate()
                head_stats(sqb)
                head_scale(q % 2, tqb)
                turned_t.step()
                if q == 0:
                    dve.wait_ge(z_done, 2)
                    nc.vector.tensor_scalar(fq[:, :, :], C[:, :, 0:HEADS_B], -1.0, None, ALU.mult
                                            ).then_inc(emptied[pC], 1)
            keep_block(pC)

            def forget(h, qt):
                if qt == 0:
                    return fb[:, h % 4, 0:1, :]
                return fb[:, h % 4, 1:3, :].rearrange("p a b -> p (a b)").unsqueeze(1)

            for hg in range(4):
                dve.wait_ge(fk_done, hg + 1)
                for h in range(4):
                    head = 4 * hg + h
                    fk = wide(C)[:, h * SEQ:(h + 1) * SEQ]
                    nc.vector.scalar_tensor_tensor(out=fb[:, h, 0, :], in0=fk[:, 0:P], scalar=fq[:, 0, head:head + 1],
                                                   in1=caus[:, P:2 * P], op0=ALU.add, op1=ALU.add)
                    ins = nc.vector.scalar_tensor_tensor(out=fb[:, h, 1:3, :].rearrange("p a b -> p (a b)"), in0=fk,
                                                         scalar=fq[:, 1, head:head + 1], in1=caus[:, :], op0=ALU.add,
                                                         op1=ALU.add)
                ins.then_inc(emptied[pC], 1)
                dve.wait_ge(emptied[pC], plan["fk", hg][pC] + 1)
                attention(range(4 * hg, 4 * hg + 4), s_b, forget, 1, ("attn_b", hg),
                          lambda h, qt: qo[:, h, qt * P:(qt + 1) * P], True)
            keep_block(pE)
            diagonal(GATES[2], 0)
            diagonal(GATES[2], 1)
            for p in range(4):
                lo_of(p, h_hi[:, 4 * p:4 * p + 4, :].rearrange("p a b -> p (a b)"),
                      h_lo[:, 4 * p:4 * p + 4, :].rearrange("p a b -> p (a b)"))
            turned_t.step(4)
            diagonal(GATES[2], 2)
            diagonal(GATES[2], 3)
            ones_t.step(4)
            gate_ready(2)
            dve.wait_ge(x_in, 48)
            mm_at = Tally(lo_t.n)
            with repeat(dve, 2, (lo_t, 2 * CG), (own_t, 2), (mm_at, 2 * CG)) as i:
                for k in range(2 * CG):
                    split(SPLIT + k)
                    mm_at.step()
                    if k % CG == CG - 1:
                        add_gated(k // CG, i * (2 * CW) + k // CG * CW)
            norm_stats()
            norm_gain(4)
            norm_split(4, full)
            ffn(4, 1, False)

        @block.gpsimd
        def _(pool):
            own_p = Tally()

            def gain_and_rotate(pair, uses_t, which, g):
                def chained(*ins):
                    for one in ins:
                        one.then_inc(pool_own, 1)
                    pool.wait_ge(pool_own, own_p.step(len(ins)))

                def half(k):
                    return tq[:, :, 16 * k:16 * k + 16]

                def part(k):
                    return turn4[:, k, :].rearrange("p (h d) -> p h d", d=16)

                cos, sin = (ropes[:, k, :].rearrange("p (h d) -> p h d", d=16) for k in range(2))
                pool.wait_ge(emptied[pair], uses_t)
                pool.wait_ge(consts_in, 16 * 7)
                chained(nc.gpsimd.tensor_tensor(tq, tq, gqk[:, which, ds(g * P, P)].unsqueeze(1).to_broadcast([P, 8, P]),
                                                ALU.mult))
                chained(nc.gpsimd.tensor_tensor(part(0), half(0), cos, ALU.mult),
                        nc.gpsimd.tensor_tensor(part(1), half(1), sin, ALU.mult),
                        nc.gpsimd.tensor_tensor(part(2), half(1), cos, ALU.mult),
                        nc.gpsimd.tensor_tensor(part(3), half(0), sin, ALU.mult))
                chained(nc.gpsimd.tensor_tensor(half(0), part(0), part(1), ALU.subtract))
                nc.gpsimd.tensor_tensor(half(1), part(2), part(3), ALU.add).then_inc(roped, 1)

            for half_n in range(2):
                before = plan["qkv", half_n]
                with repeat(pool, GROUPS, (own_p, 12)) as g:
                    gain_and_rotate(pA, g + (before[pA] + 1), 0, g)
                    gain_and_rotate(pB, g * 2 + (before[pB] + 1), 1, g)
            for layer, at in ((0, 1 + 4 + 12 + 2 + 4), (1, 54 + 4)):
                pool.wait_ge(turned, at)
                nc.gpsimd.memset(yacc, 0.0).then_inc(zeroed, 1)


_INS = ["x", "c", "w_ada", "b_ada", "g_norm_attn", "g_norm_ffn", "w_qkv_a", "g_qk_a", "w_o_a", "w_ada_kv", "b_ada_kv",
        "g_norm_kv", "w_kv", "g_k_b", "w_f", "b_f", "w_q_b", "g_q_b", "w_o_b", "w_ffn_in", "w_ffn_out"]


def _tables():
    import numpy as np

    rot = P // 4
    inv = np.float32(500000.0) ** (-np.arange(0, rot, 2, dtype=np.float32) / np.float32(rot))
    ang = np.arange(SEQ, dtype=np.float32)[:, None] * inv[None, :].astype(np.float32)
    rope = np.empty((P, 2, RT, 4, rot // 2), np.float32)
    for k, t in enumerate((np.cos(ang), np.sin(ang))):
        rope[:, k] = t.reshape(RT, P, 1, rot // 2).transpose(1, 0, 2, 3)
    q, k = np.arange(SEQ)[:, None], np.arange(SEQ)[None, :]
    masks = np.empty((SEQ, GROUPS, SEQ), np.float32)
    for g, (window, dilation) in enumerate(((128, 1), (512, 4), (2048, 16))):
        seen = (k <= q) & ((q - k) % dilation == 0) & ((q - k) // dilation <= window // dilation)
        masks[:, g] = np.where(seen, 0.0, -1e30)
    masks = masks.reshape(RT, P, GROUPS * SEQ).transpose(1, 0, 2).reshape(P, -1)
    a, b = np.arange(P)[:, None], np.arange(P)[None, :]
    causal = np.zeros((P, 5 * P), np.float32)
    causal[:, P:2 * P] = np.where(b <= a, 0.0, -1e30)
    causal[:, 2 * P:3 * P] = a == b
    causal[:, 3 * P:4 * P] = a <= b
    causal[:, 4 * P:] = 1.0
    return np.ascontiguousarray(rope.reshape(P, -1)), np.ascontiguousarray(masks), causal


def kernel(**inputs):
    import numpy as np
    import concourse.bacc as bacc
    from concourse.bass_utils import run_bass_kernel_spmd

    nc = bacc.Bacc("TRN2", target_bir_lowering=False, num_devices=1)
    arrays = {f"in_{n}": np.ascontiguousarray(inputs[n]) for n in _INS}
    arrays.update(zip(("rope", "mask_a", "causal"), _tables()))
    aps = [nc.dram_tensor(n, a.shape, mybir.dt.from_np(a.dtype), kind="ExternalInput").ap() for n, a in arrays.items()]
    out = nc.dram_tensor("out", (1, SEQ, D), mybir.dt.float32, kind="ExternalOutput").ap()
    build(nc, *aps, out)
    return run_bass_kernel_spmd(nc, [arrays], core_ids=[0]).results[0]["out"]
```

```python
from contextlib import ExitStack, contextmanager

import concourse.bass as bass
from concourse import mybir

P = 128
SEQ, D = 256, 2048
RT = SEQ // P
KT = D // P
CW = 512
GK = 2
RAW = 8
SPLIT = 4
ADA = 4
ADA_W = 1024
GROUPS = 3
HEADS_A = 8
HEADS_B = 16
HEAD_BATCH = 4
S_RING = 3
D_FF = 5632
FJ = D_FF // CW
FFN_OUT_KT = CW // P
NC = D // CW
CG = KT // GK
ADA_BLOCKS_LAYER = 6 * D // ADA_W
EPS = 1e-6
LOWEST = -3.0e38


class Tally:

    def __init__(self, n=0):
        self.n, self.i, self.per = n, None, 0

    def value(self, ahead=0):
        return self.n + ahead if self.i is None else self.i * self.per + (self.n + ahead)

    def step(self, k=1):
        self.n += k
        return self.value()


@contextmanager
def repeat(engine, times, *tallies):
    with engine.Fori(0, times) as i:
        start = [t.n for t, _ in tallies]
        for t, per in tallies:
            t.i, t.per = i, per
        yield i
        for (t, per), n in zip(tallies, start):
            assert t.n == n + per, (t.n, n, per)
            t.i, t.per = None, 0
            t.n = n + per * times


def build(nc, x, c, w_ada, b_ada, g_norm_attn, g_norm_ffn, w_qkv_a, g_qk_a, w_o_a, w_ada_kv, b_ada_kv, g_norm_kv,
          w_kv, g_k_b, w_f, b_f, w_q_b, g_q_b, w_o_b, w_ffn_in, w_ffn_out, rope, mask_a, causal, out):
    f32, f32r = mybir.dt.float32, mybir.dt.float32r
    ALU, ACT, AX = mybir.AluOpType, mybir.ActivationFunctionType, mybir.AxisListType
    ds = bass.ds
    x_spill = nc.dram_tensor("x_spill", (SEQ, D), f32, kind="Internal").ap()

    with ExitStack() as ctx:
        def sb(name, shape, dt=f32):
            return ctx.enter_context(nc.sbuf_tensor(name, shape, dt))

        def sem(name):
            return ctx.enter_context(nc.semaphore(name))

        raw = sb("raw", [P, RAW, GK, CW])
        w_hi = sb("w_hi", [P, SPLIT, GK, CW], f32r)
        w_lo = sb("w_lo", [P, SPLIT, GK, CW], f32r)
        h_hi = sb("h_hi", [P, KT, SEQ], f32r)
        h_lo = sb("h_lo", [P, KT, SEQ], f32r)
        m_hi = sb("m_hi", [P, FFN_OUT_KT, SEQ], f32r)
        m_lo = sb("m_lo", [P, FFN_OUT_KT, SEQ], f32r)
        ada = sb("ada", [P, ADA, ADA_W])
        acc = sb("acc", [P, ADA_W])
        arena = sb("arena", [P, 72 * 256])

        ident = sb("ident", [P, P])
        tri_ones = sb("tri_ones", [P, 2 * P])
        caus = sb("caus", [P, 2 * P])
        cols = sb("cols", [P, 322])
        mods = sb("mods", [P, 14 * KT])
        c_act = sb("c_act", [P, KT])
        block_sum = sb("block_sum", [P, ADA_W // P])
        gain = sb("gain", [P, KT])
        ss_parts = sb("ss_parts", [P, RT, NC])
        ss = sb("ss", [P, RT])
        ms = sb("ms", [P, RT])
        rms = sb("rms", [P, RT])
        rstd = sb("rstd", [P, RT])
        ss8 = sb("ss8", [P, 8])
        ms8 = sb("ms8", [P, 8])
        rms8 = sb("rms8", [P, 8])
        rstd8 = sb("rstd8", [P, 8])
        top = sb("top", [P, S_RING, HEAD_BATCH])
        neg_top = sb("neg_top", [P, S_RING, HEAD_BATCH])
        total = sb("total", [P, S_RING, HEAD_BATCH])
        inv_total = sb("inv_total", [P, S_RING, HEAD_BATCH])
        wf_raw = sb("wf_raw", [P, KT, HEADS_B])
        wf_hi = sb("wf_hi", [P, KT, HEADS_B], f32r)
        wf_lo = sb("wf_lo", [P, KT, HEADS_B], f32r)
        bf_rows = sb("bf_rows", [P, HEADS_B])
        gq_scaled = sb("gq_scaled", [P, 1])

        def area(kb, *shape):
            n = 1
            for s in shape:
                n *= s
            flat = arena[:, kb * 256:kb * 256 + n]
            if len(shape) == 1:
                return flat
            names = "abcd"[:len(shape)]
            return flat.rearrange(f"p ({' '.join(names)}) -> p {' '.join(names)}", **dict(zip(names, shape)))

        xs = area(0, RT, D)
        ys = area(16, RT, D)
        yacc = area(16, RT, D)
        vecs = area(52, 3, P)
        qT = area(0, GROUPS * 4, SEQ)
        kT = area(12, GROUPS * 4, SEQ)
        va = area(24, RT, GROUPS, CW)
        oa = area(36, RT, D // 2)
        tq = area(44, 8, P)
        sq = area(48, 8, P)
        s_a = [area(52 + 3 * k, GROUPS, SEQ) for k in range(S_RING)]
        msk_a = area(64, RT * GROUPS * SEQ)
        ropes = area(70, 2, P)
        turn4 = area(52, 4, P)
        gate = area(48, D)
        silu = area(56, RT, CW)
        mid = area(60, RT, CW)
        diag = area(60, 2, CW)
        full = [area(64, 4, SEQ), area(68, 4, SEQ)]
        full0 = [area(36, 4, SEQ), area(40, 4, SEQ)]
        qo = area(0, HEADS_B, SEQ)
        fb = area(16, 2, HEAD_BATCH, 3, P)
        s_b = [area(at, HEAD_BATCH, SEQ) for at in (28, 64, 68)]
        bc = acc[:, :].rearrange("p (a h j n) -> p a h j n", a=2, h=2, j=2)
        kTb = area(32, HEADS_B, SEQ)
        vb = area(48, RT, D)
        tqb = area(64, 8, P)
        sqb = area(68, 8, P)
        gqk = sb("gqk", [P, 2, GROUPS * P])
        n_f = RT * HEADS_B
        lf0, lf1, lf2, lf3, z_neg, neg_logf, fq = (
            gqk[:, 0, k * n_f:(k + 1) * n_f].rearrange("p (r h) -> p r h", r=RT) for k in range(7))
        lf = (lf0, lf1, lf2, lf3)

        A, B, C, E = [ctx.enter_context(nc.psum_tensor(f"pair{n}", [P, RT, CW], f32)) for n in "ABCE"]
        PAIR = (A, B, C, E)
        pA, pB, pC, pE = range(4)

        def wide(pair):
            return pair[:, :, :].rearrange("p a n -> p (a n)")

        raw_full = [sem(f"raw_full{k}") for k in range(RAW)]
        ada_full = [sem(f"ada_full{k}") for k in range(ADA)]
        vecs_in = sem("vecs_in")
        consts_in = sem("consts_in")
        x_in = sem("x_in")
        x_spilled = sem("x_spilled")
        stored = sem("stored")
        hi_done = sem("hi_done")
        split_done = sem("split_done")
        mm_done = sem("mm_done")
        ada_done = sem("ada_done")
        col_done = sem("col_done")
        emptied = [sem(f"emptied{n}") for n in "ABCE"]
        turned = sem("turned")
        lhs_hi = sem("lhs_hi")
        lhs_lo = sem("lhs_lo")
        c_done = sem("c_done")
        sumsq = sem("sumsq")
        rms_inv = sem("rms_inv")
        root = sem("root")
        y_done = sem("y_done")
        y_act_done = sem("y_act_done")
        gain_done = sem("gain_done")
        squared = sem("squared")
        inv8 = sem("inv8")
        root8 = sem("root8")
        roped = sem("roped")
        pool_own = sem("pool_own")
        zeroed = sem("zeroed")
        own = sem("own")
        x_done = sem("x_done")
        diag_done = sem("diag_done")
        ones_done = sem("ones_done")
        gate_done = sem("gate_done")
        qk_done = sem("qk_done")
        top_done = sem("top_done")
        exp_done = sem("exp_done")
        p_turned = sem("p_turned")
        pv_done = sem("pv_done")
        wf_hi_done = sem("wf_hi_done")
        wf_done = sem("wf_done")
        z_done = sem("z_done")
        lf_act = sem("lf_act")
        lf_dve = sem("lf_dve")
        bc_done = sem("bc_done")
        fk_done = sem("fk_done")
        fk_read = sem("fk_read")

        block = ctx.enter_context(nc.Block())


        plan = {}
        OFF_MODS = 0
        OFF_C, OFF_KV, OFF_ATTN, OFF_FFN, OFF_GK, OFF_GQ = 224, 240, 256, 288, 320, 321
        NORMS = [(0, 1, OFF_ATTN), (3, 4, OFF_FFN), (6, 7, OFF_KV), (8, 9, OFF_ATTN + KT), (11, 12, OFF_FFN + KT)]
        GATES = [2, 5, 10, 13]
        MOD_BLOCKS = 14 * D // ADA_W

        def vector(v):
            return mods[:, v * KT:(v + 1) * KT]

        def landed(t, ring):
            v = 16 * (t.n // ring + 1)
            return v if t.i is None else t.i * (t.per // ring * 16) + v

        def keys(qt):
            return (qt + 1) * P

        @block.tensor
        def _(pe):
            pe.sem_inc(mm_done, SPLIT)
            pe.sem_inc(col_done, 1)
            uses = [Tally() for _ in PAIR]
            split_t = Tally(RAW)
            ada_t = Tally(ADA)
            exp_t, y_t, roped_t, diag_t, bc_t = (Tally() for _ in range(5))

            def use(p):
                if uses[p].n:
                    pe.wait_ge(emptied[p], uses[p].value())
                uses[p].step()

            def granule(n, left_hi, left_lo, kt0, pair, first, last):
                pe.wait_ge(split_done, split_t.step())
                for t in range(GK):
                    for r in range(RT):
                        hi = left_hi[:, kt0 + t, r * P:(r + 1) * P]
                        lo = left_lo[:, kt0 + t, r * P:(r + 1) * P]
                        a, z = first and t == 0, last and t == GK - 1
                        nc.tensor.matmul(pair[:, r, :], hi, w_hi[:, n % SPLIT, t, :], start=a, stop=False)
                        nc.tensor.matmul(pair[:, r, :], hi, w_lo[:, n % SPLIT, t, :], start=False, stop=False)
                        mm = nc.tensor.matmul(pair[:, r, :], lo, w_hi[:, n % SPLIT, t, :], start=False, stop=z)
                mm.then_inc(mm_done, 1)

            def chunk(p, n0, norm=None, granules=CG):
                use(p)
                for k in range(granules):
                    if norm is not None and k % 2 == 0:
                        pe.wait_ge(lhs_lo, norm + k // 2 + 1)
                    granule(n0 + k, h_hi, h_lo, k * GK, PAIR[p], k == 0, k == granules - 1)

            def mod_block(p):
                pe.wait_ge(ada_done, ada_t.step(KT))
                use(p)
                for q in range(ADA_W // P):
                    mm = nc.tensor.matmul(wide(PAIR[p])[:, q * P:(q + 1) * P], acc[:, q * P:(q + 1) * P], ident[:, :],
                                          start=True, stop=True, is_transpose=True)
                mm.then_inc(col_done, 1)

            def turn(p, tiles):
                use(p)
                for k, tile in enumerate(tiles):
                    mm = nc.tensor.matmul(wide(PAIR[p])[:, k * P:(k + 1) * P], tile, ident[:, :], start=True, stop=True,
                                          is_transpose=True)
                mm.then_inc(turned, 1)

            def turn_norm(e):
                plan["norm", e] = [u.n for u in uses]
                for p in range(4):
                    if e != 3:
                        pe.wait_ge(y_done, y_t.step())
                        pe.wait_ge(y_act_done, y_t.value())
                    turn(p, [ys[:, r, kt * P:(kt + 1) * P] for kt in range(4 * p, 4 * p + 4) for r in range(RT)])

            def gate_rows(pairs):
                plan["gate", diag_t.n // 4] = pairs, [u.n for u in uses]
                for p in pairs:
                    use(p)
                    for k in range(2):
                        pe.wait_ge(diag_done, diag_t.step())
                        nc.tensor.matmul(PAIR[p][:, k, :], tri_ones[:, P:2 * P], diag[:, k, :], start=True,
                                         stop=True).then_inc(ones_done, 1)

            def attention(steps, scores, probs, outs, between=None):
                last = len(steps) - 1
                for n in range(len(steps) + 2):
                    if n <= last:
                        use(n % 2)
                        scores(n, *steps[n]).then_inc(qk_done, 1)
                        if between is not None:
                            between(n)
                    if 1 <= n <= last + 1:
                        pe.wait_ge(exp_done, exp_t.step())
                        use(pC)
                        probs(n - 1, *steps[n - 1]).then_inc(p_turned, 1)
                    if n >= 2:
                        if n == last + 2:
                            pe.wait_ge(emptied[pC], uses[pC].value())
                        use(pE)
                        outs(n - 2, *steps[n - 2]).then_inc(pv_done, 1)

            pe.wait_ge(vecs_in, 16 * 10)
            use(pC)
            for k, n in enumerate((P, P, 66)):
                mm = nc.tensor.matmul(C[:, 0, k * P:k * P + n], vecs[0:n, k, :], ident[0:n, 0:n], start=True, stop=True,
                                      is_transpose=True)
            mm.then_inc(turned, 1)
            pe.wait_ge(consts_in, 16 * 7)
            for _ in range(4):
                mod_block(pB)
            turn_norm(0)

            for half in range(2):
                plan["qkv", half] = [u.n for u in uses]
                with repeat(pe, GROUPS, (split_t, 3 * CG), (ada_t, KT), (roped_t, 2), (uses[pA], 1), (uses[pB], 2),
                            (uses[pC], 1), (uses[pE], 2)):
                    chunk(pA, 0, norm=0)
                    chunk(pB, CG)
                    pe.wait_ge(roped, roped_t.step())
                    turn(pE, [tq[:, r * 4 + h, :] for h in range(4) for r in range(RT)])
                    chunk(pC, 2 * CG)
                    pe.wait_ge(roped, roped_t.step())
                    turn(pE, [tq[:, r * 4 + h, :] for h in range(4) for r in range(RT)])
                    mod_block(pB)

                def scores(n, h, qt):
                    for g in range(GROUPS):
                        mm = nc.tensor.matmul(wide(PAIR[n % 2])[:, g * SEQ:g * SEQ + keys(qt)],
                                              qT[:, g * 4 + h, qt * P:(qt + 1) * P], kT[:, g * 4 + h, 0:keys(qt)],
                                              start=True, stop=True)
                    return mm

                def probs(n, h, qt):
                    for g in range(GROUPS):
                        for kt in range(qt + 1):
                            at = g * SEQ + kt * P
                            mm = nc.tensor.matmul(wide(C)[:, at:at + P], s_a[n % S_RING][:, g, kt * P:(kt + 1) * P],
                                                  ident[:, :], start=True, stop=True, is_transpose=True)
                    return mm

                def outs(n, h, qt):
                    for g in range(GROUPS):
                        for kt in range(qt + 1):
                            mm = nc.tensor.matmul(E[:, 0, 0:P], s_a[n % S_RING][:, g, kt * P:(kt + 1) * P],
                                                  va[:, kt, g, h * P:(h + 1) * P], start=g == 0 and kt == 0,
                                                  stop=g == GROUPS - 1 and kt == qt)
                    return mm

                plan["attn", half] = [u.n for u in uses]
                pe.wait_ge(emptied[pC], uses[pC].value())
                pe.wait_ge(emptied[pE], uses[pE].value())
                attention([(h, qt) for h in range(4) for qt in range(RT)], scores, probs, outs)

            pe.wait_ge(emptied[pE], uses[pE].value())
            for p in range(2):
                turn(p, [oa[:, r, kt * P:(kt + 1) * P] for kt in range(4 * p, 4 * p + 4) for r in range(RT)])
            gate_rows((pC, pE))
            for p in range(2):
                pe.wait_ge(emptied[p], uses[p].value())
            for q in range(NC):
                chunk(q % 2, q * (CG // 2), granules=CG // 2)
            mod_block(pC)

            def out_chunk(p, n0):
                use(p)
                for k in range(2):
                    granule(n0 + k, m_hi, m_lo, k * GK, PAIR[p], k == 0, k == 1)

            def ffn(e, passes, mod_first):
                def hidden():
                    pe.wait_ge(emptied[pB], uses[pB].value())
                    turn(pE, [mid[:, r, k * P:(k + 1) * P] for k in range(4) for r in range(RT)])

                chunk(pA, 0, norm=4 * e)
                chunk(pB, CG)
                if mod_first:
                    mod_block(pC)
                for times, with_mod in passes:
                    tallies = [(split_t, 3 * CG), (uses[pA], 2), (uses[pB], 1), (uses[pC], 2)]
                    tallies += [(ada_t, KT), (uses[pE], 3)] if with_mod else [(uses[pE], 2)]
                    with repeat(pe, times, *tallies):
                        chunk(pA, 0)
                        hidden()
                        chunk(pB, CG)
                        pe.wait_ge(emptied[pE], uses[pE].value())
                        for k, p in enumerate((pC, pE, pA, pC)):
                            out_chunk(p, 2 * CG + 2 * k)
                        if with_mod:
                            mod_block(pE)
                hidden()
                gate_rows((pA, pB))
                pe.wait_ge(emptied[pE], uses[pE].value())
                for k, p in enumerate((pC, pE, pA, pC)):
                    out_chunk(p, 2 * k)

            turn_norm(1)
            ffn(1, [(FJ - 1, True)], True)

            turn_norm(2)
            with repeat(pe, 2, (split_t, 4 * CG), (ada_t, KT), (uses[pA], 2), (uses[pB], 2), (uses[pC], 1),
                        (uses[pE], 2)):
                for c2 in range(2):
                    chunk(pA, 2 * c2 * CG, norm=8)
                    chunk(pB, (2 * c2 + 1) * CG)
                    pe.wait_ge(emptied[pA], uses[pA].value())
                    turn(pE, [tqb[:, r * 4 + h, :] for h in range(4) for r in range(RT)])
                mod_block(pC)
            pe.wait_ge(wf_done, 1)
            plan["z"] = [u.n for u in uses]
            use(pC)
            for r in range(RT):
                for kt in range(KT):
                    for k, (left, right) in enumerate(((h_hi, wf_hi), (h_hi, wf_lo), (h_lo, wf_hi))):
                        mm = nc.tensor.matmul(C[:, r, 0:HEADS_B], left[:, kt, r * P:(r + 1) * P], right[:, kt, :],
                                              start=kt == 0 and k == 0, stop=kt == KT - 1 and k == 2)
            mm.then_inc(z_done, 1)
            turn_norm(3)
            for q in range(4):
                chunk(q % 2, q * CG, norm=12)
                if q:
                    pe.wait_ge(emptied[1 - q % 2], uses[1 - q % 2].value())
                    turn(pE, [tqb[:, r * 4 + h, :] for h in range(4) for r in range(RT)])
                if q == 0:
                    pe.wait_ge(lf_dve, 2)
                    use(pC)
                    nc.tensor.matmul(C[:, 0, 0:HEADS_B], tri_ones[:, 0:P], neg_logf[:, 0, :], start=True, stop=True)
                    nc.tensor.matmul(C[:, 1, 0:HEADS_B], tri_ones[:, P:2 * P], neg_logf[:, 0, :], start=True, stop=False)
                    nc.tensor.matmul(C[:, 1, 0:HEADS_B], tri_ones[:, 0:P], neg_logf[:, 1, :], start=False,
                                     stop=True).then_inc(z_done, 1)
                if q == 2:
                    mod_block(pC)

            def forget_keys(i, into):
                pe.wait_ge(bc_done, bc_t.step())
                if i > 2:
                    pe.wait_ge(fk_read, i - 1)
                for h in range(2):
                    at = into[:, h * SEQ:(h + 1) * SEQ]
                    nc.tensor.matmul(at[:, 0:P], bc[:, i % 2, h, 0, :], tri_ones[:, 0:P], start=True, stop=True)
                    nc.tensor.matmul(at[:, P:2 * P], bc[:, i % 2, h, 0, :], tri_ones[:, P:2 * P], start=True,
                                     stop=False)
                    mm = nc.tensor.matmul(at[:, P:2 * P], bc[:, i % 2, h, 1, :], tri_ones[:, 0:P], start=False,
                                          stop=True)
                mm.then_inc(fk_done, 1)

            plan["fk"] = uses[pC].n
            use(pC)
            for i in range(2):
                forget_keys(i, C[:, i, :])
            pe.wait_ge(emptied[pB], uses[pB].value())
            turn(pE, [tqb[:, r * 4 + h, :] for h in range(4) for r in range(RT)])
            pe.wait_ge(emptied[pE], uses[pE].value())

            def scores(n, hg, qt):
                for h in range(HEAD_BATCH):
                    head = hg * HEAD_BATCH + h
                    mm = nc.tensor.matmul(wide(PAIR[n % 2])[:, h * SEQ:h * SEQ + keys(qt)],
                                          qo[:, head, qt * P:(qt + 1) * P], kTb[:, head, 0:keys(qt)], start=True,
                                          stop=True)
                return mm

            def probs(n, hg, qt):
                for h in range(HEAD_BATCH):
                    for kt in range(qt + 1):
                        at = h * SEQ + kt * P
                        mm = nc.tensor.matmul(wide(C)[:, at:at + P], s_b[n % S_RING][:, h, kt * P:(kt + 1) * P],
                                              ident[:, :], start=True, stop=True, is_transpose=True)
                return mm

            def outs(n, hg, qt):
                for h in range(HEAD_BATCH):
                    head = hg * HEAD_BATCH + h
                    for kt in range(qt + 1):
                        mm = nc.tensor.matmul(E[:, 0, h * P:(h + 1) * P], s_b[n % S_RING][:, h, kt * P:(kt + 1) * P],
                                              vb[:, kt, head * P:(head + 1) * P], start=kt == 0, stop=kt == qt)
                return mm

            def between(n):
                if n < 6:
                    forget_keys(n + 2, E[:, 1, :])

            plan["attn_b"] = [u.n for u in uses]
            attention([(hg, qt) for hg in range(4) for qt in range(RT)], scores, probs, outs, between)

            pe.wait_ge(emptied[pE], uses[pE].value())
            for p in range(4):
                turn(p, [qo[:, kt, r * P:(r + 1) * P] for kt in range(4 * p, 4 * p + 4) for r in range(RT)])
            gate_rows((pC, pE))
            for p in range(2):
                pe.wait_ge(emptied[p], uses[p].value())
            for q in range(NC):
                chunk(q % 2, q * CG)
                if q == 2:
                    mod_block(pC)
            turn_norm(4)
            ffn(4, [(2, True), (FJ - 3, False)], False)

        @block.sync
        def _(sp):
            used = Tally()
            m = Tally()

            def load(n, src):
                if used.n >= RAW:
                    sp.wait_ge(split_done, used.value(1))
                sp.dma_start(raw[:, n % RAW], src).then_inc(raw_full[n % RAW], 16)
                used.step()

            def load_ada(src):
                if m.n >= ADA:
                    sp.wait_ge(ada_done, m.value(1))
                slot = m.n % ADA
                sp.dma_start(ada[:, slot], src).then_inc(ada_full[slot], 16)
                m.step()

            def rows(w, g):
                return w[g * GK * P:(g + 1) * GK * P, :].rearrange("(t p) n -> p t n", p=P)

            def ada_src(w, kt, block_at):
                return w[kt * P:(kt + 1) * P, ds(block_at * ADA_W, ADA_W)]

            w_mod = [w_ada[0], w_ada_kv, w_ada[1]]
            by_tile = lambda t: t.rearrange("(a p) n -> p a n", p=P)

            def vec(row, tile, src, n):
                sp.dma_start(vecs[row:row + n, tile, :], src.rearrange("(a b) -> a b", b=P)).then_inc(vecs_in, 16)

            vec(0, 0, b_ada[0], 96)
            vec(96, 0, b_ada_kv, 32)
            vec(0, 1, b_ada[1], 96)
            vec(96, 1, c[0], 16)
            vec(112, 1, g_norm_kv, 16)
            vec(0, 2, g_norm_attn.rearrange("a b -> (a b)"), 32)
            vec(32, 2, g_norm_ffn.rearrange("a b -> (a b)"), 32)
            vec(64, 2, g_k_b, 1)
            vec(65, 2, g_q_b[0], 1)
            sp.dma_start(ident[:, :], causal[:, 2 * P:3 * P]).then_inc(vecs_in, 16)
            for kt in range(ADA):
                load_ada(ada_src(w_mod[0], kt, 0))
            sp.dma_start(xs, by_tile(x[0])).then_inc(x_in, 16)
            sp.dma_start(tri_ones[:, :], causal[:, 3 * P:5 * P]).then_inc(consts_in, 16)
            sp.dma_start(caus[:, :], causal[:, 0:2 * P]).then_inc(consts_in, 16)
            sp.dma_start(msk_a, mask_a).then_inc(consts_in, 16)
            sp.dma_start(ropes.rearrange("p a b -> p (a b)"), rope).then_inc(consts_in, 16)
            sp.dma_start(gqk[:, :, :].rearrange("p a b -> p (a b)"),
                         g_qk_a.rearrange("l a b d -> (l a b d)").partition_broadcast(P)).then_inc(consts_in, 16)
            sp.dma_start(wf_raw[:, :, :], w_f.rearrange("(k p) n -> p k n", p=P)).then_inc(consts_in, 16)
            sp.dma_start(bf_rows[:, :], b_f.partition_broadcast(P)).then_inc(consts_in, 16)
            for k in range(ADA, 4 * KT):
                load_ada(ada_src(w_mod[0], k % KT, k // KT))

            for half in range(2):
                if half == 0:
                    for n in range(CG):
                        load(n, rows(w_qkv_a[0], n)[:, :, 0:CW])
                first = CG if half == 0 else 0
                for lo_g, hi_g in ((0, 1), (1, GROUPS)) if half == 0 else ((0, GROUPS),):
                    with repeat(sp, hi_g - lo_g, (used, 3 * CG - (first if lo_g == 0 else 0)), (m, KT)) as g:
                        for n in range(first if lo_g == 0 else 0, 3 * CG):
                            at = (g + lo_g) * (HEADS_A * P) + (n // CG * GROUPS * HEADS_A * P + half * CW)
                            load(n, rows(w_qkv_a[0], n % CG)[:, :, ds(at, CW)])
                            if n >= CG:
                                load_ada(ada_src(w_mod[0], n - CG, g + (lo_g + 4 + GROUPS * half)))
            for n in range(2 * CG):
                if n == CG:
                    sp.wait_ge(turned, 1 + 4 + 12 + 2)
                    sp.dma_start(xs, by_tile(x[0])).then_inc(x_in, 16)
                k = n % (CG // 2)
                load(n, rows(w_o_a[0], k)[:, :, n // (CG // 2) * CW:(n // (CG // 2) + 1) * CW])
                if n >= CG:
                    load_ada(ada_src(w_mod[0], n - CG, 10))

            def ffn(layer, passes, tiles, pass_tiles=()):
                wi, wo = w_ffn_in[layer], w_ffn_out[layer]
                for n in range(2 * CG):
                    load(n, rows(wi, n % CG)[:, :, n // CG * D_FF:n // CG * D_FF + CW])
                    if n < len(tiles):
                        load_ada(ada_src(w_mod[0], *tiles[n]))
                done = 0
                for times, which, first in passes:
                    with repeat(sp, times, (used, 3 * CG), *([(m, KT + (len(pass_tiles) if done == 0 else 0))] if which is not None else [])) as i:
                        for n in range(3 * CG):
                            if n < 2 * CG:
                                at = i * CW + (n // CG * D_FF + (done + 1) * CW)
                                load(n, rows(wi, n % CG)[:, :, ds(at, CW)])
                            else:
                                q, k = (n - 2 * CG) // 2, n % 2
                                hidden = wo.rearrange("(j k t p) n -> k p t j n", p=P, t=GK, k=2)[k]
                                src = hidden[:, :, ds(i + done, 1), q * CW:(q + 1) * CW]
                                load(n, src.rearrange("p t j n -> p t (j n)"))
                            if done == 0 and n < len(pass_tiles):
                                load_ada(ada_src(w_mod[0], *pass_tiles[n]))
                            if which is not None and n >= CG:
                                load_ada(ada_src(w_mod[which], n - CG, i + first))
                    done += times
                for n in range(CG):
                    q, k = n // 2, n % 2
                    at = (FJ - 1) * CW + k * GK * P
                    load(n, wo[at:at + GK * P, q * CW:(q + 1) * CW].rearrange("(t p) n -> p t n", p=P))

            ffn(0, [(1, 1, 0), (3, 1, 1), (6, 2, 0)],
                [(kt, 10) for kt in range(CG, KT)] + [(kt, 11) for kt in range(CG)], [(kt, 11) for kt in range(CG, KT)])
            with repeat(sp, 2, (used, 4 * CG), (m, KT)) as i:
                for n in range(4 * CG):
                    q = n // CG
                    load(n, rows(w_kv, n % CG)[:, :, ds(i * (2 * CW) + (q // 2 * CW + q % 2 * D), CW)])
                    if n % CG >= CG - 4:
                        load_ada(ada_src(w_mod[2], 4 * q + n % CG - (CG - 4), i + 6))
            sp.wait_ge(x_done, 8)
            sp.dma_start(by_tile(x_spill), xs).then_inc(x_spilled, 16)
            for n in range(4 * CG):
                load(n, rows(w_q_b[0], n % CG)[:, :, n // CG * CW:(n // CG + 1) * CW])
                if CG <= n < CG + KT:
                    load_ada(ada_src(w_mod[2], n - CG, 8))
            for n in range(4 * CG):
                if n == CG:
                    sp.wait_ge(turned, 54)
                    sp.wait_ge(x_spilled, 16)
                    sp.dma_start(xs, by_tile(x_spill)).then_inc(x_in, 16)
                load(n, rows(w_o_b[0], n % CG)[:, :, n // CG * CW:(n // CG + 1) * CW])
                if CG <= n < CG + KT:
                    load_ada(ada_src(w_mod[2], n - CG, 9))
            ffn(1, [(2, 2, 10), (FJ - 3, None, 0)], ())
            for q in range(NC):
                sp.wait_ge(x_done, 12 + q + 1)
                sp.dma_start(by_tile(out[0])[:, :, q * CW:(q + 1) * CW], xs[:, :, q * CW:(q + 1) * CW]
                             ).then_inc(stored, 16)
            sp.wait_ge(stored, 16 * NC)

        @block.scalar
        def _(act):
            w_t = Tally()
            turned_t, p_t, top_t, lo_t, root_t, gain_t, inv8_t, ones_t = (Tally() for _ in range(8))

            def split(k):
                act.wait_ge(raw_full[k % RAW], landed(w_t, RAW))
                act.wait_ge(mm_done, w_t.value(1))
                nc.scalar.activation(w_hi[:, k % SPLIT], raw[:, k % RAW], ACT.Copy).then_inc(hi_done, 1)
                w_t.step()

            def round_lhs(p, into):
                act.wait_ge(turned, turned_t.step())
                nc.scalar.activation(into, wide(PAIR[p]), ACT.Copy).then_inc(lhs_hi, 1)

            def square_sums(e, q):
                if e == 0:
                    act.wait_ge(x_in, 16)
                else:
                    act.wait_ge(x_done, {1: 0, 2: 4, 4: 8}[e] + q + 1)
                at = slice(q * CW, (q + 1) * CW)
                for r in range(RT):
                    ins = nc.scalar.activation(ys[:, r, at], xs[:, r, at], ACT.Square, accum_out=ss_parts[:, r, q:q + 1])
                if q == NC - 1:
                    ins.then_inc(sumsq, 1)

            def norm(e, full):
                shift, _, _ = NORMS[e]

                def normalize(q):
                    at = slice(q * CW, (q + 1) * CW)
                    nc.scalar.activation(ys[:, 1, at], xs[:, 1, at], ACT.Copy, scale=rstd[:, 1:2]).then_inc(y_act_done, 1)

                if e != 3:
                    square_sums(e, NC - 1)
                    act.wait_ge(rms_inv, root_t.step())
                    nc.scalar.activation(rstd[:, :], rms[:, :], ACT.Sqrt).then_inc(root, 1)
                    act.wait_ge(root, root_t.value())
                    for q in range(2):
                        normalize(q)
                act.wait_ge(gain_done, gain_t.step())
                for p in range(4):
                    act.wait_ge(turned, turned_t.step())
                    if p % 2 == 0:
                        if p:
                            act.wait_ge(lhs_lo, lo_t.value(1))
                        for k in range(4):
                            kt = 4 * p + k
                            ins = nc.scalar.activation(full[p % 2][:, k, :], wide(PAIR[p])[:, k * SEQ:(k + 1) * SEQ],
                                                       ACT.Identity, scale=gain[:, kt:kt + 1],
                                                       bias=vector(shift)[:, kt:kt + 1])
                        ins.then_inc(emptied[p], 1)
                        act.wait_ge(emptied[p], plan["norm", e][p] + 1)
                    else:
                        act.wait_ge(emptied[p], plan["norm", e][p] + 1)
                    nc.scalar.activation(h_hi[:, 4 * p:4 * p + 4, :], full[p % 2], ACT.Copy).then_inc(lhs_hi, 1)
                    if p == 0 and e != 3:
                        for q in range(2, NC):
                            normalize(q)
                lo_t.step(4)

            def keep_gate():
                pairs = plan["gate", ones_t.n // 4][0]
                for k in range(4):
                    p = pairs[k // 2]
                    act.wait_ge(ones_done, ones_t.step())
                    ins = nc.scalar.activation(gate[:, k * CW:(k + 1) * CW], PAIR[p][:, k % 2, :], ACT.Copy)
                    ins.then_inc(gate_done if k % 2 == 0 else emptied[p], 1)

            def attention(n_steps, s_tiles, n_parts, n_tops):
                def turn_back(n):
                    act.wait_ge(p_turned, p_t.step())
                    turned_p = wide(C)[:, 0:n_parts * SEQ].rearrange("p (g k) -> p g k", g=n_parts)
                    nc.scalar.activation(s_tiles[n % S_RING][:, :, 0:keys(n % 2)], turned_p[:, :, 0:keys(n % 2)],
                                         ACT.Copy).then_inc(emptied[pC], 1)

                for n in range(n_steps + 1):
                    if n < n_steps:
                        act.wait_ge(top_done, top_t.step())
                        o, per = n % S_RING, n_parts // n_tops
                        for j in range(n_tops):
                            s = s_tiles[o][:, j * per:(j + 1) * per, 0:keys(n % 2)]
                            ins = nc.scalar.activation(s, s, ACT.Exp, bias=neg_top[:, o, j:j + 1],
                                                       accum_out=total[:, o, j:j + 1])
                        ins.then_inc(exp_done, 1)
                    if n:
                        turn_back(n - 1)

            def square(p, into):
                act.wait_ge(mm_done, w_t.value())
                nc.scalar.activation(into, PAIR[p][:, :, :], ACT.Square).then_inc(squared, 1)

            def root_heads():
                act.wait_ge(inv8, inv8_t.step())
                nc.scalar.activation(rstd8[:, :], rms8[:, :], ACT.Sqrt).then_inc(root8, 1)

            act.wait_ge(emptied[pC], 1)
            nc.scalar.activation(c_act[:, :], cols[:, OFF_C:OFF_C + KT], ACT.Silu).then_inc(c_done, 1)
            act.wait_ge(consts_in, 16 * 7)
            nc.scalar.activation(wf_hi[:, :, :], wf_raw[:, :, :], ACT.Copy).then_inc(wf_hi_done, 1)
            turned_t.step()
            for q in range(NC - 1):
                square_sums(0, q)
            norm(0, full0)
            for k in range(SPLIT):
                split(k)

            for half in range(2):
                with repeat(act, GROUPS, (w_t, 3 * CG), (turned_t, 2), (inv8_t, 2)) as g:
                    for k in range(3 * CG):
                        split(SPLIT + k)
                        if k == 7:
                            square(pA, sq)
                        if k == 8:
                            root_heads()
                        if k == 15:
                            square(pB, sq)
                        if k == 16:
                            act.wait_ge(turned, turned_t.step())
                            act.wait_ge(turned, 1)
                            nc.scalar.activation(qT[:, ds(g * 4, 4), :].rearrange("p a b -> p (a b)"), wide(E), ACT.Copy,
                                                 scale=float(P) ** -0.5).then_inc(emptied[pE], 1)
                            root_heads()
                    act.wait_ge(turned, turned_t.step())
                    act.wait_ge(turned, 1)
                    nc.scalar.activation(va[:, :, ds(g, 1), :].rearrange("p r g n -> p r (g n)"), C[:, :, :], ACT.Copy
                                         ).then_inc(emptied[pC], 1)
                    nc.scalar.activation(kT[:, ds(g * 4, 4), :].rearrange("p a b -> p (a b)"), wide(E), ACT.Copy
                                         ).then_inc(emptied[pE], 1)
                attention(8, s_a, GROUPS, 1)
            for p in range(2):
                round_lhs(p, h_hi[:, 4 * p:4 * p + 4, :])
            keep_gate()
            for k in range(2 * CG):
                split(SPLIT + k)
                if k % 4 == 1 and k > 4:
                    square_sums(1, k // 4 - 1)

            def ffn():
                def part(n, turned_before):
                    for k in range(n):
                        split(SPLIT + k)
                        if k == CG - 1 and turned_before:
                            round_lhs(pE, m_hi[:, :, :])
                        if k == CG:
                            act.wait_ge(mm_done, w_t.value())
                            nc.scalar.activation(silu, A[:, :, :], ACT.Silu).then_inc(emptied[pA], 1)

                part(2 * CG, False)
                with repeat(act, FJ - 1, (w_t, 3 * CG), (turned_t, 1)):
                    part(3 * CG, True)
                round_lhs(pE, m_hi[:, :, :])
                keep_gate()

            norm(1, full)
            ffn()
            for k in range(CG):
                split(SPLIT + k)
                if k % 2 and k > 1:
                    square_sums(2, k // 2 - 1)
            norm(2, full)
            with repeat(act, 2, (w_t, 4 * CG), (turned_t, 2), (inv8_t, 2)) as i:
                for k in range(4 * CG):
                    split(SPLIT + k)
                    if k % (2 * CG) == 7:
                        square(pA, sqb)
                    if k % (2 * CG) == 8:
                        root_heads()
                    if k % (2 * CG) == 2 * CG - 1:
                        q = k // (2 * CG)
                        act.wait_ge(turned, turned_t.step())
                        act.wait_ge(turned, 1)
                        nc.scalar.activation(vb[:, :, ds(i * (2 * CW) + q * CW, CW)], B[:, :, :], ACT.Copy
                                             ).then_inc(emptied[pB], 1)
                        nc.scalar.activation(kTb[:, ds(i * 8 + q * 4, 4), :].rearrange("p a b -> p (a b)"), wide(E),
                                             ACT.Copy, scale=cols[:, OFF_GK:OFF_GK + 1]).then_inc(emptied[pE], 1)
            act.wait_ge(lf_dve, 1)
            nc.scalar.activation(lf[1][:, :, :], lf[0][:, :, :], ACT.Abs).then_inc(lf_act, 1)
            act.wait_ge(lf_act, 1)
            nc.scalar.activation(lf[2][:, :, :], lf[1][:, :, :], ACT.Exp, scale=-1.0).then_inc(lf_act, 1)
            act.wait_ge(lf_act, 2)
            nc.scalar.activation(lf[3][:, :, :], lf[2][:, :, :], ACT.Ln, bias=1.0).then_inc(lf_act, 1)
            norm(3, full)

            def keep_q(q):
                act.wait_ge(turned, turned_t.step())
                if q == 0:
                    act.wait_ge(x_spilled, 16)
                nc.scalar.activation(qo[:, 4 * q:4 * q + 4, :].rearrange("p a b -> p (a b)"), wide(E), ACT.Copy,
                                     scale=gq_scaled[:, 0:1]).then_inc(emptied[pE], 1)

            for q in range(4):
                for k in range(CG):
                    split(SPLIT + k)
                square(q % 2, sqb)
                root_heads()
                if q:
                    keep_q(q - 1)
            keep_q(3)
            attention(8, s_b, HEAD_BATCH, HEAD_BATCH)
            for p in range(4):
                round_lhs(p, h_hi[:, 4 * p:4 * p + 4, :])
            keep_gate()
            for k in range(4 * CG):
                split(SPLIT + k)
                if k % CG == 1 and k > CG:
                    square_sums(4, k // CG - 1)
            norm(4, full)
            ffn()
            for k in range(CG - SPLIT):
                split(SPLIT + k)

        @block.vector
        def _(dve):
            dve.sem_inc(split_done, RAW)
            dve.sem_inc(ada_done, ADA)
            lo_t = Tally()
            m_t = Tally()
            blk_t = Tally()
            own_t, turned_t, lhs_hi_t, lhs_lo_t, sq_t, root8_t, root_t = (Tally() for _ in range(7))
            qk_t, exp_t, pv_t, ones_t, silu_t = (Tally() for _ in range(5))

            def chained(ins):
                ins.then_inc(own, 1)
                dve.wait_ge(own, own_t.step())

            def split(k):
                dve.wait_ge(hi_done, lo_t.value(1))
                nc.vector.tensor_tensor(w_lo[:, k % SPLIT], raw[:, k % RAW], w_hi[:, k % SPLIT].bitcast(f32),
                                        ALU.subtract).then_inc(split_done, 1)
                lo_t.step()

            def modulate():
                slot, kt = m_t.n % ADA, m_t.n % KT
                dve.wait_ge(ada_full[slot], landed(m_t, ADA))
                if kt == 0:
                    done = m_t.n // KT + 1
                    dve.wait_ge(col_done, done if m_t.i is None else m_t.i * (m_t.per // KT) + done)
                    ins = nc.vector.tensor_scalar(acc[:, :], ada[:, slot], c_act[:, 0:1], None, ALU.mult)
                else:
                    dve.wait_ge(ada_done, m_t.value(ADA))
                    ins = nc.vector.scalar_tensor_tensor(out=acc[:, :], in0=ada[:, slot], scalar=c_act[:, kt:kt + 1],
                                                         in1=acc[:, :], op0=ALU.mult, op1=ALU.add)
                ins.then_inc(ada_done, 1)
                m_t.step()

            def keep_block(p):
                n = ADA_W // P
                at = blk_t.value() * n
                dve.wait_ge(col_done, blk_t.value(2))
                chained(nc.vector.reduce_sum(block_sum[:, :], wide(PAIR[p]).rearrange("p (a b) -> p a b", b=P), AX.X))
                nc.vector.tensor_tensor(mods[:, ds(at, n)], block_sum[:, :], cols[:, ds(at, n)], ALU.add
                                        ).then_inc(emptied[p], 1)
                blk_t.step()

            def norm_stats():
                dve.wait_ge(sumsq, root_t.value(1))
                chained(nc.vector.reduce_sum(ss[:, :], ss_parts[:, :, :], AX.X))
                chained(nc.vector.tensor_scalar(ms[:, :], ss[:, :], 1.0 / D, EPS, ALU.mult, ALU.add))
                nc.vector.reciprocal(rms[:, :], ms[:, :]).then_inc(rms_inv, 1)
                dve.wait_ge(root, root_t.step())
                for q in range(NC):
                    at = slice(q * CW, (q + 1) * CW)
                    nc.vector.tensor_scalar(ys[:, 0, at], xs[:, 0, at], rstd[:, 0:1], None, ALU.mult
                                            ).then_inc(y_done, 1)

            def norm_gain(e):
                _, scale, g = NORMS[e]
                nc.vector.scalar_tensor_tensor(out=gain[:, :], in0=vector(scale), scalar=1.0, in1=cols[:, g:g + KT],
                                               op0=ALU.add, op1=ALU.mult).then_inc(gain_done, 1)

            def norm_split(e, full):
                shift, _, _ = NORMS[e]

                def modulated(p):
                    dve.wait_ge(turned, turned_t.value(p + 1))
                    for k in range(4):
                        kt = 4 * p + k
                        ins = nc.vector.tensor_scalar(full[1][:, k, :], wide(PAIR[p])[:, k * SEQ:(k + 1) * SEQ],
                                                      gain[:, kt:kt + 1], vector(shift)[:, kt:kt + 1], ALU.mult,
                                                      ALU.add)
                    ins.then_inc(emptied[p], 1)

                def lo(p):
                    dve.wait_ge(lhs_hi, lhs_hi_t.step())
                    nc.vector.tensor_tensor(h_lo[:, 4 * p:4 * p + 4, :], full[p % 2],
                                            h_hi[:, 4 * p:4 * p + 4, :].bitcast(f32), ALU.subtract
                                            ).then_inc(lhs_lo, 1)
                    lhs_lo_t.step()

                dve.wait_ge(gain_done, e + 1)
                modulated(1)
                lo(0)
                lo(1)
                dve.wait_ge(lhs_lo, lhs_lo_t.value())
                modulated(3)
                lo(2)
                lo(3)
                turned_t.step(4)

            def lo_of(p, hi, lo):
                dve.wait_ge(lhs_hi, lhs_hi_t.step())
                nc.vector.tensor_tensor(lo, wide(PAIR[p]), hi.bitcast(f32), ALU.subtract).then_inc(emptied[p], 1)

            def head_stats(squares):
                dve.wait_ge(squared, sq_t.step())
                chained(nc.vector.reduce_sum(ss8[:, :], squares, AX.X))
                chained(nc.vector.tensor_scalar(ms8[:, :], ss8[:, :], 1.0 / P, EPS, ALU.mult, ALU.add))
                nc.vector.reciprocal(rms8[:, :], ms8[:, :]).then_inc(inv8, 1)

            def head_scale(p, into):
                dve.wait_ge(root8, root8_t.step())
                dve.wait_ge(turned, turned_t.value())
                nc.vector.tensor_tensor(into, wide(PAIR[p]).rearrange("p (h d) -> p h d", d=P),
                                        rstd8[:, :].unsqueeze(2).to_broadcast([P, 8, P]), ALU.mult
                                        ).then_inc(emptied[p], 1)

            def diagonal(v, k):
                if k >= 2:
                    dve.wait_ge(ones_done, ones_t.value(k - 1))
                nc.vector.tensor_tensor(diag[:, k % 2].rearrange("p (a b) -> p a b", b=P),
                                        ident[:, :].unsqueeze(1).to_broadcast([P, 4, P]),
                                        vector(v)[:, 4 * k:4 * k + 4].unsqueeze(2).to_broadcast([P, 4, P]), ALU.mult
                                        ).then_inc(diag_done, 1)

            def gate_ready(n):
                pairs, before = plan["gate", n]
                dve.wait_ge(emptied[pairs[1]], before[pairs[1]] + 1)

            def add_gated(p, at, ahead):
                dve.wait_ge(mm_done, lo_t.value(ahead))
                dve.wait_ge(split_done, lo_t.value(RAW))
                for r in range(RT):
                    ins = nc.vector.tensor_tensor(silu[:, r, :], PAIR[p][:, r, :], gate[:, ds(at, CW)], ALU.mult)
                chained(ins)
                for r in range(RT):
                    nc.vector.tensor_tensor(xs[:, r, ds(at, CW)], xs[:, r, ds(at, CW)], silu[:, r, :], ALU.add
                                            ).then_inc(x_done if r else emptied[p], 1)

            def attention(steps, s_tiles, bias, n_parts, n_tops, key, o_rows, between=None):
                before, per = plan[key], n_parts // n_tops
                for n in range(len(steps) + 2):
                    if n < len(steps):
                        o, seen = n % S_RING, keys(steps[n][1])
                        dve.wait_ge(qk_done, qk_t.step())
                        for j in range(n_tops):
                            scores = wide(PAIR[n % 2])[:, j * per * SEQ:(j + 1) * per * SEQ]
                            ins = nc.vector.tensor_tensor_reduce(
                                out=s_tiles[o][:, j * per:(j + 1) * per, 0:seen],
                                in0=scores.rearrange("p (g k) -> p g k", g=per)[:, :, 0:seen],
                                in1=bias(j, *steps[n]), scale=1.0, scalar=LOWEST, op0=ALU.add, op1=ALU.max,
                                accum_out=top[:, o, j:j + 1])
                        ins.then_inc(emptied[n % 2], 1)
                        dve.wait_ge(emptied[n % 2], before[n % 2] + n // 2 + 1)
                        nc.vector.tensor_scalar(neg_top[:, o, 0:n_tops], top[:, o, 0:n_tops], -1.0, None, ALU.mult
                                                ).then_inc(top_done, 1)
                        if between is not None:
                            between(n)
                    if n >= 2:
                        o = (n - 2) % S_RING
                        dve.wait_ge(exp_done, exp_t.step())
                        chained(nc.vector.reciprocal(inv_total[:, o, 0:n_tops], total[:, o, 0:n_tops]))
                        dve.wait_ge(pv_done, pv_t.step())
                        nc.vector.tensor_tensor(
                            o_rows(*steps[n - 2]), E[:, 0, 0:n_tops * P].rearrange("p (h d) -> p h d", d=P),
                            inv_total[:, o, 0:n_tops].unsqueeze(2).to_broadcast([P, n_tops, P]), ALU.mult
                        ).then_inc(emptied[pE], 1)

            dve.wait_ge(turned, turned_t.step())
            nc.vector.tensor_copy(cols[:, :], C[:, 0, 0:322]).then_inc(emptied[pC], 1)
            dve.wait_ge(emptied[pC], 1)
            chained(nc.vector.tensor_scalar(gq_scaled[:, :], cols[:, OFF_GQ:OFF_GQ + 1], float(P) ** -0.5, None,
                                            ALU.mult))
            dve.wait_ge(c_done, 1)
            for b in range(4):
                for _ in range(KT):
                    modulate()
                keep_block(pB)
                if b == 0:
                    norm_stats()
                    dve.wait_ge(wf_hi_done, 1)
                    nc.vector.tensor_tensor(wf_lo[:, :, :], wf_raw[:, :, :], wf_hi[:, :, :].bitcast(f32), ALU.subtract
                                            ).then_inc(wf_done, 1)
            dve.wait_ge(emptied[pB], 4)
            norm_gain(0)
            norm_split(0, full0)
            for k in range(SPLIT):
                split(k)

            for half in range(2):
                with repeat(dve, GROUPS, (lo_t, 3 * CG), (m_t, KT), (blk_t, 1), (own_t, 5), (turned_t, 2), (sq_t, 2),
                            (root8_t, 2)):
                    for k in range(3 * CG):
                        split(SPLIT + k)
                        if k < KT:
                            modulate()
                        if k in (7, 16):
                            head_stats(sq)
                        if k == 9:
                            head_scale(pA, tq)
                            turned_t.step()
                        if k == 18:
                            head_scale(pB, tq)
                            turned_t.step()
                    keep_block(pB)
                masks = msk_a.rearrange("p (r g k) -> p r g k", r=RT, g=GROUPS)
                attention([(h, qt) for h in range(4) for qt in range(RT)], s_a,
                          lambda _, h, qt: masks[:, qt, :, 0:keys(qt)], GROUPS, 1, ("attn", half),
                          lambda h, qt, half=half: oa[:, qt, (4 * half + h) * P:(4 * half + h + 1) * P].unsqueeze(1))
            diagonal(GATES[0], 0)
            diagonal(GATES[0], 1)
            for p in range(2):
                lo_of(p, h_hi[:, 4 * p:4 * p + 4, :].rearrange("p a b -> p (a b)"),
                      h_lo[:, 4 * p:4 * p + 4, :].rearrange("p a b -> p (a b)"))
            turned_t.step(2)
            diagonal(GATES[0], 2)
            diagonal(GATES[0], 3)
            ones_t.step(4)
            gate_ready(0)
            dve.wait_ge(x_in, 32)
            for k in range(2 * CG):
                last = k == 2 * CG - 1
                if last:
                    modulate()
                    add_gated(k // 4 % 2, k // 4 * CW, 1)
                split(SPLIT + k)
                if not last:
                    modulate()
                    if k % 4 == 3:
                        add_gated(k // 4 % 2, k // 4 * CW, 0)

            def ffn(e, layer, passes, mod_first):
                def turned_lo():
                    lo_of(pE, m_hi[:, :, :].rearrange("p a b -> p (a b)"), m_lo[:, :, :].rearrange("p a b -> p (a b)"))
                    turned_t.step()

                def part(n, with_mod, outputs):
                    for k in range(n):
                        split(SPLIT + k)
                        if with_mod and k < KT:
                            modulate()
                        if k == CG and outputs:
                            turned_lo()
                        if k == 2 * CG - 1:
                            dve.wait_ge(emptied[pA], a_t.value(1))
                            chained(nc.vector.tensor_tensor(mid[:, 0, :], silu[:, 0, :], B[:, 0, :], ALU.mult))
                            nc.vector.tensor_tensor(mid[:, 1, :], silu[:, 1, :], B[:, 1, :], ALU.mult
                                                    ).then_inc(emptied[pB], 1)
                        if k >= 2 * CG and k % 2:
                            q = (k - 2 * CG) // 2
                            p = (pC, pE, pA, pC)[q]
                            at = yacc[:, :, q * CW:(q + 1) * CW]
                            nc.vector.tensor_tensor(at, PAIR[p][:, :, :], at, ALU.add).then_inc(emptied[p], 1)
                    a_t.step(2 if outputs else 1)

                a_t = Tally(plan["norm", e][pA] + 1)
                part(2 * CG, mod_first, False)
                if mod_first:
                    keep_block(pC)
                dve.wait_ge(zeroed, layer + 1)
                for times, with_mod in passes:
                    tallies = [(lo_t, 3 * CG), (own_t, 2 if with_mod else 1), (lhs_hi_t, 1), (turned_t, 1), (a_t, 2)]
                    tallies += [(m_t, KT), (blk_t, 1)] if with_mod else []
                    with repeat(dve, times, *tallies):
                        part(3 * CG, with_mod, True)
                        if with_mod:
                            keep_block(pE)
                turned_lo()
                for k in range(4):
                    diagonal(GATES[2 * layer + 1], k)
                ones_t.step(4)
                last = layer == 1
                n0 = lo_t.n - SPLIT
                for k in range(CG):
                    if k < SPLIT or not last and k < CG - 1:
                        split(SPLIT + k)
                    if k % 2:
                        q = k // 2
                        p = (pC, pE, pA, pC)[q]
                        if q == 0:
                            gate_ready(2 * layer + 1)
                        dve.wait_ge(mm_done, SPLIT + n0 + k + 1)
                        at = slice(q * CW, (q + 1) * CW)
                        if q:
                            dve.wait_ge(x_done, 8 * layer + 4 + q)
                        chained(nc.vector.tensor_tensor(yacc[:, :, at], PAIR[p][:, :, :], yacc[:, :, at], ALU.add))
                        for r in range(RT):
                            ins = nc.vector.tensor_tensor(silu[:, r, :], yacc[:, r, at], gate[:, at], ALU.mult)
                        chained(ins)
                        for r in range(RT):
                            nc.vector.tensor_tensor(xs[:, r, at], xs[:, r, at], silu[:, r, :], ALU.add
                                                    ).then_inc(x_done if r else emptied[p], 1)
                if not last:
                    split(SPLIT + CG - 1)

            norm_gain(1)
            norm_stats()
            keep_block(pC)
            norm_split(1, full)
            ffn(1, 0, [(FJ - 1, True)], True)

            norm_gain(2)
            norm_stats()
            norm_split(2, full)
            with repeat(dve, 2, (lo_t, 4 * CG), (m_t, KT), (blk_t, 1), (own_t, 5), (turned_t, 2), (sq_t, 2),
                        (root8_t, 2)):
                for k in range(4 * CG):
                    split(SPLIT + k)
                    if k % CG < 4:
                        modulate()
                    if k % (2 * CG) == 7:
                        head_stats(sqb)
                    if k % (2 * CG) == 9:
                        head_scale(pA, tqb)
                        turned_t.step()
                keep_block(pC)
            dve.wait_ge(z_done, 1)
            for r in range(RT):
                ins = nc.vector.tensor_tensor(lf[0][:, r, :], C[:, r, 0:HEADS_B], bf_rows[:, :], ALU.add)
            ins.then_inc(emptied[pC], 1)
            dve.wait_ge(emptied[pC], plan["z"][pC] + 1)
            chained(nc.vector.tensor_scalar(z_neg[:, :, :], lf[0][:, :, :], 0.0, None, ALU.min))
            nc.vector.tensor_scalar(z_neg[:, :, :], z_neg[:, :, :], -1.0, None, ALU.mult).then_inc(lf_dve, 1)
            norm_gain(3)
            norm_split(3, full)
            dve.wait_ge(lf_act, 3)
            nc.vector.tensor_tensor(neg_logf[:, :, :], lf[3][:, :, :], z_neg[:, :, :], ALU.add).then_inc(lf_dve, 1)
            for q in range(4):
                for k in range(CG):
                    split(SPLIT + k)
                    if q * CG + k < KT:
                        modulate()
                head_stats(sqb)
                head_scale(q % 2, tqb)
                turned_t.step()
                if q == 0:
                    dve.wait_ge(z_done, 2)
                    nc.vector.tensor_scalar(fq[:, :, :], C[:, :, 0:HEADS_B], -1.0, None, ALU.mult
                                            ).then_inc(emptied[pC], 1)
                if q == 2:
                    keep_block(pC)

            def forget_bias(i, keys_at):
                dve.wait_ge(fk_done, i + 1)
                for h in range(2):
                    head = 2 * i + h
                    into = fb[:, head // HEAD_BATCH % 2, head % HEAD_BATCH]
                    fk = keys_at[:, h * SEQ:(h + 1) * SEQ]
                    nc.vector.scalar_tensor_tensor(out=into[:, 0, :], in0=fk[:, 0:P], scalar=fq[:, 0, head:head + 1],
                                                   in1=caus[:, P:2 * P], op0=ALU.add, op1=ALU.add)
                    ins = nc.vector.scalar_tensor_tensor(out=into[:, 1:3, :].rearrange("p a b -> p (a b)"), in0=fk,
                                                         scalar=fq[:, 1, head:head + 1], in1=caus[:, :], op0=ALU.add,
                                                         op1=ALU.add)
                ins.then_inc(emptied[pC] if i == 1 else fk_read, 1)
                if i == 1:
                    dve.wait_ge(emptied[pC], plan["fk"] + 1)
                elif i % 2:
                    dve.wait_ge(fk_read, i)

            def forget(h, hg, qt):
                if qt == 0:
                    return fb[:, hg % 2, h, 0:1, :]
                return fb[:, hg % 2, h, 1:3, :].rearrange("p a b -> p (a b)").unsqueeze(1)

            def between(n):
                if n < 6:
                    forget_bias(n + 2, E[:, 1, :])

            for i in range(2):
                forget_bias(i, C[:, i, :])
            attention([(hg, qt) for hg in range(4) for qt in range(RT)], s_b, forget, HEAD_BATCH, HEAD_BATCH, "attn_b",
                      lambda hg, qt: qo[:, hg * HEAD_BATCH:(hg + 1) * HEAD_BATCH, qt * P:(qt + 1) * P], between)
            diagonal(GATES[2], 0)
            diagonal(GATES[2], 1)
            for p in range(4):
                lo_of(p, h_hi[:, 4 * p:4 * p + 4, :].rearrange("p a b -> p (a b)"),
                      h_lo[:, 4 * p:4 * p + 4, :].rearrange("p a b -> p (a b)"))
            turned_t.step(4)
            diagonal(GATES[2], 2)
            diagonal(GATES[2], 3)
            ones_t.step(4)
            gate_ready(2)
            dve.wait_ge(x_in, 48)
            for k in range(4 * CG):
                last = k == 4 * CG - 1
                if last:
                    add_gated(k // CG % 2, k // CG * CW, 1)
                split(SPLIT + k)
                if k < KT:
                    modulate()
                if k % CG == CG - 1 and not last:
                    add_gated(k // CG % 2, k // CG * CW, 0)
                if k == 3 * CG:
                    keep_block(pC)
            norm_gain(4)
            norm_stats()
            norm_split(4, full)
            ffn(4, 1, [(2, True), (FJ - 3, False)], False)

        @block.gpsimd
        def _(pool):
            own_p = Tally()

            def gain_and_rotate(pair, uses_t, which, g):
                def chained(*ins):
                    for one in ins:
                        one.then_inc(pool_own, 1)
                    pool.wait_ge(pool_own, own_p.step(len(ins)))

                def half(k):
                    return tq[:, :, 16 * k:16 * k + 16]

                def part(k):
                    return turn4[:, k, :].rearrange("p (h d) -> p h d", d=16)

                cos, sin = (ropes[:, k, :].rearrange("p (h d) -> p h d", d=16) for k in range(2))
                pool.wait_ge(emptied[pair], uses_t)
                pool.wait_ge(consts_in, 16 * 7)
                chained(nc.gpsimd.tensor_tensor(tq, tq, gqk[:, which, ds(g * P, P)].unsqueeze(1).to_broadcast([P, 8, P]),
                                                ALU.mult))
                chained(nc.gpsimd.tensor_tensor(part(0), half(0), cos, ALU.mult),
                        nc.gpsimd.tensor_tensor(part(1), half(1), sin, ALU.mult),
                        nc.gpsimd.tensor_tensor(part(2), half(1), cos, ALU.mult),
                        nc.gpsimd.tensor_tensor(part(3), half(0), sin, ALU.mult))
                chained(nc.gpsimd.tensor_tensor(half(0), part(0), part(1), ALU.subtract))
                nc.gpsimd.tensor_tensor(half(1), part(2), part(3), ALU.add).then_inc(roped, 1)

            for half_n in range(2):
                before = plan["qkv", half_n]
                with repeat(pool, GROUPS, (own_p, 12)) as g:
                    gain_and_rotate(pA, g + (before[pA] + 1), 0, g)
                    gain_and_rotate(pB, g * 2 + (before[pB] + 1), 1, g)
            pool.wait_ge(turned, 1 + 4 + 12 + 2 + 4)
            nc.gpsimd.memset(yacc, 0.0).then_inc(zeroed, 1)
            pool.wait_ge(col_done, 25 + 1)
            pool.wait_ge(lf_dve, 2)
            for i in range(HEADS_B // 2):
                if i >= 2:
                    pool.wait_ge(fk_done, i - 1)
                for h in range(2):
                    for j in range(RT):
                        ins = nc.gpsimd.tensor_scalar(bc[:, i % 2, h, j, :], tri_ones[:, P:2 * P],
                                                      neg_logf[:, j, 2 * i + h:2 * i + h + 1], None, ALU.mult)
                ins.then_inc(bc_done, 1)
            pool.wait_ge(turned, 54 + 4)
            nc.gpsimd.memset(yacc, 0.0).then_inc(zeroed, 1)


_INS = ["x", "c", "w_ada", "b_ada", "g_norm_attn", "g_norm_ffn", "w_qkv_a", "g_qk_a", "w_o_a", "w_ada_kv", "b_ada_kv",
        "g_norm_kv", "w_kv", "g_k_b", "w_f", "b_f", "w_q_b", "g_q_b", "w_o_b", "w_ffn_in", "w_ffn_out"]


def _tables():
    import numpy as np

    rot = P // 4
    inv = np.float32(500000.0) ** (-np.arange(0, rot, 2, dtype=np.float32) / np.float32(rot))
    ang = np.arange(SEQ, dtype=np.float32)[:, None] * inv[None, :].astype(np.float32)
    rope = np.empty((P, 2, RT, 4, rot // 2), np.float32)
    for k, t in enumerate((np.cos(ang), np.sin(ang))):
        rope[:, k] = t.reshape(RT, P, 1, rot // 2).transpose(1, 0, 2, 3)
    q, k = np.arange(SEQ)[:, None], np.arange(SEQ)[None, :]
    masks = np.empty((SEQ, GROUPS, SEQ), np.float32)
    for g, (window, dilation) in enumerate(((128, 1), (512, 4), (2048, 16))):
        seen = (k <= q) & ((q - k) % dilation == 0) & ((q - k) // dilation <= window // dilation)
        masks[:, g] = np.where(seen, 0.0, -1e30)
    masks = masks.reshape(RT, P, GROUPS * SEQ).transpose(1, 0, 2).reshape(P, -1)
    a, b = np.arange(P)[:, None], np.arange(P)[None, :]
    causal = np.zeros((P, 5 * P), np.float32)
    causal[:, P:2 * P] = np.where(b <= a, 0.0, -1e30)
    causal[:, 2 * P:3 * P] = a == b
    causal[:, 3 * P:4 * P] = a <= b
    causal[:, 4 * P:] = 1.0
    return np.ascontiguousarray(rope.reshape(P, -1)), np.ascontiguousarray(masks), causal


def kernel(**inputs):
    import numpy as np
    import concourse.bacc as bacc
    from concourse.bass_utils import run_bass_kernel_spmd

    nc = bacc.Bacc("TRN2", target_bir_lowering=False, num_devices=1)
    arrays = {f"in_{n}": np.ascontiguousarray(inputs[n]) for n in _INS}
    arrays.update(zip(("rope", "mask_a", "causal"), _tables()))
    aps = [nc.dram_tensor(n, a.shape, mybir.dt.from_np(a.dtype), kind="ExternalInput").ap() for n, a in arrays.items()]
    out = nc.dram_tensor("out", (1, SEQ, D), mybir.dt.float32, kind="ExternalOutput").ap()
    build(nc, *aps, out)
    return run_bass_kernel_spmd(nc, [arrays], core_ids=[0]).results[0]["out"]
```

```python
from contextlib import ExitStack, contextmanager

import concourse.bass as bass
from concourse import mybir

P = 128
SEQ, D = 256, 2048
RT = SEQ // P
KT = D // P
CW = 512
GK = 2
RAW = 8
SPLIT = 4
ADA = 4
PE_TILE = 4
ADA_W = 1024
GROUPS = 3
HEADS_A = 8
HEADS_B = 16
HEAD_BATCH = 4
S_RING = 3
D_FF = 5632
FJ = D_FF // CW
FFN_OUT_KT = CW // P
NC = D // CW
CG = KT // GK
HALF = CG // 2
TILES_FIRST = (3, 3, 2) * 4
TILES_SECOND = (2,) * 8 + (0,) * 4
EPS = 1e-6
LOWEST = -3.0e38


class Tally:

    def __init__(self, n=0):
        self.n, self.i, self.per = n, None, 0

    def value(self, ahead=0):
        return self.n + ahead if self.i is None else self.i * self.per + (self.n + ahead)

    def step(self, k=1):
        self.n += k
        return self.value()


@contextmanager
def repeat(engine, times, *tallies):
    with engine.Fori(0, times) as i:
        start = [t.n for t, _ in tallies]
        for t, per in tallies:
            t.i, t.per = i, per
        yield i
        for (t, per), n in zip(tallies, start):
            assert t.n == n + per, (t.n, n, per)
            t.i, t.per = None, 0
            t.n = n + per * times


def build(nc, x, c, w_ada, b_ada, g_norm_attn, g_norm_ffn, w_qkv_a, g_qk_a, w_o_a, w_ada_kv, b_ada_kv, g_norm_kv,
          w_kv, g_k_b, w_f, b_f, w_q_b, g_q_b, w_o_b, w_ffn_in, w_ffn_out, rope, mask_a, causal, out):
    f32, f32r = mybir.dt.float32, mybir.dt.float32r
    ALU, ACT, AX = mybir.AluOpType, mybir.ActivationFunctionType, mybir.AxisListType
    ds = bass.ds
    x_spill = nc.dram_tensor("x_spill", (SEQ, D), f32, kind="Internal").ap()

    with ExitStack() as ctx:
        def sb(name, shape, dt=f32):
            return ctx.enter_context(nc.sbuf_tensor(name, shape, dt))

        def sem(name):
            return ctx.enter_context(nc.semaphore(name))

        raw = sb("raw", [P, RAW, GK, CW])
        w_hi = sb("w_hi", [P, SPLIT, GK, CW], f32r)
        w_lo = sb("w_lo", [P, SPLIT, GK, CW], f32r)
        h_hi = sb("h_hi", [P, KT, SEQ], f32r)
        h_lo = sb("h_lo", [P, KT, SEQ], f32r)
        m_hi = sb("m_hi", [P, FFN_OUT_KT, SEQ], f32r)
        m_lo = sb("m_lo", [P, FFN_OUT_KT, SEQ], f32r)
        ada = sb("ada", [P, ADA, ADA_W])
        acc = sb("acc", [P, ADA_W])
        arena = sb("arena", [P, 72 * 256])

        ident = sb("ident", [P, P])
        tri_ones = sb("tri_ones", [P, 2 * P])
        caus = sb("caus", [P, 2 * P])
        cols = sb("cols", [P, 322])
        mods = sb("mods", [P, 14 * KT])
        c_act = sb("c_act", [P, KT])
        block_sum = sb("block_sum", [P, ADA_W // P])
        gain = sb("gain", [P, KT])
        ss_parts = sb("ss_parts", [P, RT, NC])
        ss = sb("ss", [P, RT])
        warm = sb("warm", [P, 1])
        ms = sb("ms", [P, RT])
        rms = sb("rms", [P, RT])
        rstd = sb("rstd", [P, RT])
        ss8 = sb("ss8", [P, 8])
        ms8 = sb("ms8", [P, 8])
        rms8 = sb("rms8", [P, 8])
        rstd8 = sb("rstd8", [P, 8])
        top = sb("top", [P, S_RING, HEAD_BATCH])
        neg_top = sb("neg_top", [P, S_RING, HEAD_BATCH])
        total = sb("total", [P, S_RING, HEAD_BATCH])
        inv_total = sb("inv_total", [P, S_RING, HEAD_BATCH])
        wf_raw = sb("wf_raw", [P, KT, HEADS_B])
        wf_hi = sb("wf_hi", [P, KT, HEADS_B], f32r)
        wf_lo = sb("wf_lo", [P, KT, HEADS_B], f32r)
        bf_rows = sb("bf_rows", [P, HEADS_B])
        gq_scaled = sb("gq_scaled", [P, 1])

        def area(kb, *shape):
            n = 1
            for s in shape:
                n *= s
            flat = arena[:, kb * 256:kb * 256 + n]
            if len(shape) == 1:
                return flat
            names = "abcd"[:len(shape)]
            return flat.rearrange(f"p ({' '.join(names)}) -> p {' '.join(names)}", **dict(zip(names, shape)))

        xs = area(0, RT, D)
        ys = area(16, RT, D)
        yacc = area(16, RT, D)
        vecs = area(52, 3, P)
        qT = area(0, GROUPS * 4, SEQ)
        kT = area(12, GROUPS * 4, SEQ)
        va = area(24, RT, GROUPS, CW)
        oa = area(36, RT, D // 2)
        tq = area(44, 8, P)
        sq = area(48, 8, P)
        s_a = [area(52 + 3 * k, GROUPS, SEQ) for k in range(S_RING)]
        msk_a = area(64, RT * GROUPS * SEQ)
        tq_first = area(56, 8, P)
        pe_tiles = area(64, 2, ADA_W)
        ropes = area(70, 2, P)
        turn4 = area(52, 4, P)
        gate = area(48, D)
        silu = area(56, RT, CW)
        mid = area(60, RT, CW)
        diag = area(64, 2, CW)
        full = [area(64, 4, SEQ), area(68, 4, SEQ)]
        full0 = [area(36, 4, SEQ), area(40, 4, SEQ)]
        qo = area(0, HEADS_B, SEQ)
        fb = area(16, 2, HEAD_BATCH, 3, P)
        s_b = [area(at, HEAD_BATCH, SEQ) for at in (28, 64, 68)]
        bc = acc[:, :].rearrange("p (a h j n) -> p a h j n", a=2, h=2, j=2)
        kTb = area(32, HEADS_B, SEQ)
        vb = area(48, RT, D)
        tqb = area(64, 8, P)
        sqb = area(68, 8, P)
        gqk = sb("gqk", [P, 2, GROUPS * P])
        n_f = RT * HEADS_B
        lf0, lf1, lf2, lf3, z_neg, neg_logf, fq = (
            gqk[:, 0, k * n_f:(k + 1) * n_f].rearrange("p (r h) -> p r h", r=RT) for k in range(7))
        lf = (lf0, lf1, lf2, lf3)

        A, B, C, E = [ctx.enter_context(nc.psum_tensor(f"pair{n}", [P, RT, CW], f32)) for n in "ABCE"]
        PAIR = (A, B, C, E)
        pA, pB, pC, pE = range(4)

        def wide(pair):
            return pair[:, :, :].rearrange("p a n -> p (a n)")

        raw_full = [sem(f"raw_full{k}") for k in range(RAW)]
        ada_full = [sem(f"ada_full{k}") for k in range(ADA)]
        vecs_in = sem("vecs_in")
        rope_in = sem("rope_in")
        consts_in = sem("consts_in")
        x_in = sem("x_in")
        x_spilled = sem("x_spilled")
        stored = sem("stored")
        hi_done = sem("hi_done")
        split_done = sem("split_done")
        mm_done = sem("mm_done")
        ada_done = sem("ada_done")
        ada_pe_full = [sem(f"ada_pe_full{k}") for k in range(2)]
        ada_pe_done = sem("ada_pe_done")
        col_done = sem("col_done")
        emptied = [sem(f"emptied{n}") for n in "ABCE"]
        turned = sem("turned")
        lhs_hi = sem("lhs_hi")
        lhs_lo = sem("lhs_lo")
        c_done = sem("c_done")
        warmed = sem("warmed")
        sumsq = sem("sumsq")
        rms_inv = sem("rms_inv")
        root = sem("root")
        y_done = sem("y_done")
        y_act_done = sem("y_act_done")
        part_act = sem("part_act")
        part_dve = sem("part_dve")
        gain_done = sem("gain_done")
        squared = sem("squared")
        inv8 = sem("inv8")
        root8 = sem("root8")
        roped = sem("roped")
        pool_own = sem("pool_own")
        zeroed = sem("zeroed")
        own = sem("own")
        x_done = sem("x_done")
        diag_done = sem("diag_done")
        ones_done = sem("ones_done")
        gate_done = sem("gate_done")
        qk_done = sem("qk_done")
        top_done = sem("top_done")
        exp_done = sem("exp_done")
        p_turned = sem("p_turned")
        pv_done = sem("pv_done")
        wf_hi_done = sem("wf_hi_done")
        wf_done = sem("wf_done")
        z_done = sem("z_done")
        lf_act = sem("lf_act")
        lf_dve = sem("lf_dve")
        bc_done = sem("bc_done")
        fk_done = sem("fk_done")
        fk_read = sem("fk_read")

        block = ctx.enter_context(nc.Block())


        plan = {}
        OFF_C, OFF_KV, OFF_ATTN, OFF_FFN, OFF_GK, OFF_GQ = 224, 240, 256, 288, 320, 321
        NORMS = [(0, 1, OFF_ATTN), (3, 4, OFF_FFN), (6, 7, OFF_KV), (8, 9, OFF_ATTN + KT), (11, 12, OFF_FFN + KT)]
        GATES = [2, 5, 10, 13]

        def vector(v):
            return mods[:, v * KT:(v + 1) * KT]

        def landed(t, ring):
            v = 16 * (t.n // ring + 1)
            return v if t.i is None else t.i * (t.per // ring * 16) + v

        def keys(qt):
            return (qt + 1) * P

        @block.tensor
        def _(pe):
            pe.sem_inc(mm_done, SPLIT)
            pe.sem_inc(col_done, 1)
            uses = [Tally() for _ in PAIR]
            split_t = Tally(RAW)
            ada_t = Tally(ADA)
            ada_pe_t = Tally()
            exp_t, y_t, roped_t, diag_t, bc_t = (Tally() for _ in range(5))

            def use(p):
                if uses[p].n:
                    pe.wait_ge(emptied[p], uses[p].value())
                uses[p].step()

            def granule(n, left_hi, left_lo, kt0, pair, first, last):
                pe.wait_ge(split_done, split_t.step())
                for t in range(GK):
                    for r in range(RT):
                        hi = left_hi[:, kt0 + t, r * P:(r + 1) * P]
                        lo = left_lo[:, kt0 + t, r * P:(r + 1) * P]
                        a, z = first and t == 0, last and t == GK - 1
                        nc.tensor.matmul(pair[:, r, :], hi, w_hi[:, n % SPLIT, t, :], start=a, stop=False)
                        nc.tensor.matmul(pair[:, r, :], hi, w_lo[:, n % SPLIT, t, :], start=False, stop=False)
                        mm = nc.tensor.matmul(pair[:, r, :], lo, w_hi[:, n % SPLIT, t, :], start=False, stop=z)
                mm.then_inc(mm_done, 1)

            def chunk(p, n0, norm=None, granules=CG):
                use(p)
                for k in range(granules):
                    if norm is not None and k % 2 == 0:
                        pe.wait_ge(lhs_lo, norm + k // 2 + 1)
                    granule(n0 + k, h_hi, h_lo, k * GK, PAIR[p], k == 0, k == granules - 1)

            def mod_block(p):
                pe.wait_ge(ada_done, ada_t.step(KT))
                use(p)
                for q in range(ADA_W // P):
                    mm = nc.tensor.matmul(wide(PAIR[p])[:, q * P:(q + 1) * P], acc[:, q * P:(q + 1) * P], ident[:, :],
                                          start=True, stop=True, is_transpose=True)
                mm.then_inc(col_done, 1)

            def mod_tile():
                t = ada_pe_t.n
                kt = t % (KT // PE_TILE) * PE_TILE + PE_TILE - 1
                pe.wait_ge(ada_pe_full[t % 2], landed(ada_pe_t, 2))
                if kt == PE_TILE - 1:
                    use(pE)
                if t == 0:
                    pe.wait_ge(c_done, 1)
                n = ADA_W // P
                for q in range(n):
                    at = kt // PE_TILE * n + q
                    mm = nc.tensor.matmul(E[:, 0, at:at + 1], pe_tiles[:, t % 2, q * P:(q + 1) * P],
                                          c_act[:, kt:kt + 1], start=True, stop=True)
                mm.then_inc(ada_pe_done, 1)
                ada_pe_t.step()

            def mod_first_block():
                pe.wait_ge(ada_done, ada_t.step(KT - KT // PE_TILE))
                n = ADA_W // P
                for q in range(n):
                    at = KT // PE_TILE * n + q
                    mm = nc.tensor.matmul(E[:, 0, at:at + 1], acc[:, q * P:(q + 1) * P], tri_ones[:, P:P + 1],
                                          start=True, stop=True)
                mm.then_inc(col_done, 1)

            def turn(p, tiles):
                use(p)
                for k, tile in enumerate(tiles):
                    mm = nc.tensor.matmul(wide(PAIR[p])[:, k * P:(k + 1) * P], tile, ident[:, :], start=True, stop=True,
                                          is_transpose=True)
                mm.then_inc(turned, 1)

            def turn_quarter(e, p, into):
                if e != 3:
                    pe.wait_ge(y_done, y_t.step())
                    pe.wait_ge(y_act_done, y_t.value())
                turn(into, [ys[:, r, kt * P:(kt + 1) * P] for kt in range(4 * p, 4 * p + 4) for r in range(RT)])

            def turn_norm(e):
                plan["norm", e] = [u.n for u in uses]
                for p in range(4):
                    turn_quarter(e, p, p)

            def gate_row(pairs, part):
                if part == 0:
                    plan["gate", diag_t.n // 4] = pairs, [u.n for u in uses]
                p = pairs[part]
                use(p)
                for k in range(2):
                    pe.wait_ge(diag_done, diag_t.step())
                    nc.tensor.matmul(PAIR[p][:, k, :], tri_ones[:, P:2 * P], diag[:, k, :], start=True,
                                     stop=True).then_inc(ones_done, 1)

            def attention(steps, scores, probs, outs, between=None):
                last = len(steps) - 1
                for n in range(len(steps) + 2):
                    if n <= last:
                        use(n % 2)
                        scores(n, *steps[n]).then_inc(qk_done, 1)
                        if between is not None:
                            between(n)
                    if 1 <= n <= last + 1:
                        pe.wait_ge(exp_done, exp_t.step())
                        use(pC)
                        probs(n - 1, *steps[n - 1]).then_inc(p_turned, 1)
                    if n >= 2:
                        if n == last + 2:
                            pe.wait_ge(emptied[pC], uses[pC].value())
                        use(pE)
                        outs(n - 2, *steps[n - 2]).then_inc(pv_done, 1)

            pe.wait_ge(vecs_in, 16 * 11)
            use(pC)
            for k, n in enumerate((P, P, 66)):
                mm = nc.tensor.matmul(C[:, 0, k * P:k * P + n], vecs[0:n, k, :], ident[0:n, 0:n], start=True, stop=True,
                                      is_transpose=True)
            mm.then_inc(turned, 1)

            for _ in range(2):
                for _ in range(KT // PE_TILE):
                    mod_tile()
                mod_first_block()
            for p, into in enumerate((pA, pB, pE)):
                turn_quarter(0, p, into)
            plan["first"] = [u.n for u in uses]
            q_tiles, k_tiles = ([t[:, r * 4 + h, :] for h in range(4) for r in range(RT)] for t in (tq, tq_first))
            for part in range(2):
                for n in range(3 * HALF):
                    p, k = n // HALF, n % HALF
                    if part == 0 and k == 0:
                        use(p)
                    if k % 2 == 0:
                        pe.wait_ge(lhs_lo, 2 * part + k // 2 + 1)
                    granule(3 * HALF * part + n, h_hi, h_lo, (HALF * part + k) * GK, PAIR[p], part == 0 and k == 0,
                            part == 1 and k == HALF - 1)
                    if part == 0:
                        if n == 0:
                            turn_quarter(0, 3, pE)
                        for _ in range(sum(TILES_FIRST[:n + 1]) // PE_TILE - sum(TILES_FIRST[:n]) // PE_TILE):
                            mod_tile()
                        if n == 5:
                            mod_first_block()
                    if part == 1 and n == 2 * HALF:
                        pe.wait_ge(roped, roped_t.step())
                        turn(pE, q_tiles)
                if part == 0:
                    mod_first_block()
            pe.wait_ge(roped, roped_t.step())
            turn(pE, k_tiles)
            mod_block(pB)

            for half in range(2):
                plan["qkv", half] = [u.n for u in uses]
                with repeat(pe, GROUPS - (half == 0), (split_t, 3 * CG), (ada_t, KT), (roped_t, 2), (uses[pA], 1),
                            (uses[pB], 2),
                            (uses[pC], 1), (uses[pE], 2)):
                    chunk(pA, 0, norm=0)
                    chunk(pB, CG)
                    pe.wait_ge(roped, roped_t.step())
                    turn(pE, [tq[:, r * 4 + h, :] for h in range(4) for r in range(RT)])
                    chunk(pC, 2 * CG)
                    pe.wait_ge(roped, roped_t.step())
                    turn(pE, [tq[:, r * 4 + h, :] for h in range(4) for r in range(RT)])
                    mod_block(pB)

                def scores(n, h, qt):
                    for g in range(GROUPS):
                        mm = nc.tensor.matmul(wide(PAIR[n % 2])[:, g * SEQ:g * SEQ + keys(qt)],
                                              qT[:, g * 4 + h, qt * P:(qt + 1) * P], kT[:, g * 4 + h, 0:keys(qt)],
                                              start=True, stop=True)
                    return mm

                def probs(n, h, qt):
                    for g in range(GROUPS):
                        for kt in range(qt + 1):
                            at = g * SEQ + kt * P
                            mm = nc.tensor.matmul(wide(C)[:, at:at + P], s_a[n % S_RING][:, g, kt * P:(kt + 1) * P],
                                                  ident[:, :], start=True, stop=True, is_transpose=True)
                    return mm

                def outs(n, h, qt):
                    for g in range(GROUPS):
                        for kt in range(qt + 1):
                            mm = nc.tensor.matmul(E[:, 0, 0:P], s_a[n % S_RING][:, g, kt * P:(kt + 1) * P],
                                                  va[:, kt, g, h * P:(h + 1) * P], start=g == 0 and kt == 0,
                                                  stop=g == GROUPS - 1 and kt == qt)
                    return mm

                plan["attn", half] = [u.n for u in uses]
                pe.wait_ge(emptied[pC], uses[pC].value())
                pe.wait_ge(emptied[pE], uses[pE].value())
                attention([(h, qt) for h in range(4) for qt in range(RT)], scores, probs, outs)

            pe.wait_ge(emptied[pE], uses[pE].value())
            pe.wait_ge(consts_in, 16 * 4)
            for p in range(2):
                turn(p, [oa[:, r, kt * P:(kt + 1) * P] for kt in range(4 * p, 4 * p + 4) for r in range(RT)])
            for part in range(2):
                gate_row((pC, pE), part)
            for p in range(2):
                pe.wait_ge(emptied[p], uses[p].value())
            for q in range(NC):
                chunk(q % 2, q * (CG // 2), granules=CG // 2)
            mod_block(pC)

            def out_chunk(p, n0):
                use(p)
                for k in range(2):
                    granule(n0 + k, m_hi, m_lo, k * GK, PAIR[p], k == 0, k == 1)

            def ffn(e, passes, mod_first):
                def hidden():
                    pe.wait_ge(emptied[pB], uses[pB].value())
                    turn(pE, [mid[:, r, k * P:(k + 1) * P] for k in range(4) for r in range(RT)])

                chunk(pA, 0, norm=4 * e)
                chunk(pB, CG)
                if mod_first:
                    mod_block(pC)
                for times, with_mod in passes:
                    tallies = [(split_t, 3 * CG), (uses[pA], 2), (uses[pB], 1), (uses[pC], 2)]
                    tallies += [(ada_t, KT), (uses[pE], 3)] if with_mod else [(uses[pE], 2)]
                    with repeat(pe, times, *tallies):
                        chunk(pA, 0)
                        hidden()
                        chunk(pB, CG)
                        pe.wait_ge(emptied[pE], uses[pE].value())
                        for k, p in enumerate((pC, pE, pA, pC)):
                            out_chunk(p, 2 * CG + 2 * k)
                        if with_mod:
                            mod_block(pE)
                hidden()
                gate_row((pA, pB), 0)
                pe.wait_ge(emptied[pE], uses[pE].value())
                for k, p in enumerate((pC, pE, pA, pC)):
                    out_chunk(p, 2 * k)
                    if k == 0:
                        gate_row((pA, pB), 1)

            turn_norm(1)
            ffn(1, [(FJ - 1, True)], True)

            turn_norm(2)
            with repeat(pe, 2, (split_t, 4 * CG), (ada_t, KT), (uses[pA], 2), (uses[pB], 2), (uses[pC], 1),
                        (uses[pE], 2)):
                for c2 in range(2):
                    chunk(pA, 2 * c2 * CG, norm=8)
                    chunk(pB, (2 * c2 + 1) * CG)
                    pe.wait_ge(emptied[pA], uses[pA].value())
                    turn(pE, [tqb[:, r * 4 + h, :] for h in range(4) for r in range(RT)])
                mod_block(pC)
            pe.wait_ge(wf_done, 1)
            plan["z"] = [u.n for u in uses]
            use(pC)
            for r in range(RT):
                for kt in range(KT):
                    for k, (left, right) in enumerate(((h_hi, wf_hi), (h_hi, wf_lo), (h_lo, wf_hi))):
                        mm = nc.tensor.matmul(C[:, r, 0:HEADS_B], left[:, kt, r * P:(r + 1) * P], right[:, kt, :],
                                              start=kt == 0 and k == 0, stop=kt == KT - 1 and k == 2)
            mm.then_inc(z_done, 1)
            turn_norm(3)
            for q in range(4):
                chunk(q % 2, q * CG, norm=12)
                if q:
                    pe.wait_ge(emptied[1 - q % 2], uses[1 - q % 2].value())
                    turn(pE, [tqb[:, r * 4 + h, :] for h in range(4) for r in range(RT)])
                if q == 0:
                    pe.wait_ge(lf_dve, 2)
                    use(pC)
                    nc.tensor.matmul(C[:, 0, 0:HEADS_B], tri_ones[:, 0:P], neg_logf[:, 0, :], start=True, stop=True)
                    nc.tensor.matmul(C[:, 1, 0:HEADS_B], tri_ones[:, P:2 * P], neg_logf[:, 0, :], start=True,
                                     stop=False)
                    nc.tensor.matmul(C[:, 1, 0:HEADS_B], tri_ones[:, 0:P], neg_logf[:, 1, :], start=False,
                                     stop=True).then_inc(z_done, 1)
                if q == 2:
                    mod_block(pC)

            def forget_keys(i, into):
                pe.wait_ge(bc_done, bc_t.step())
                if i > 2:
                    pe.wait_ge(fk_read, i - 1)
                for h in range(2):
                    at = into[:, h * SEQ:(h + 1) * SEQ]
                    nc.tensor.matmul(at[:, 0:P], bc[:, i % 2, h, 0, :], tri_ones[:, 0:P], start=True, stop=True)
                    nc.tensor.matmul(at[:, P:2 * P], bc[:, i % 2, h, 0, :], tri_ones[:, P:2 * P], start=True,
                                     stop=False)
                    mm = nc.tensor.matmul(at[:, P:2 * P], bc[:, i % 2, h, 1, :], tri_ones[:, 0:P], start=False,
                                          stop=True)
                mm.then_inc(fk_done, 1)

            plan["fk"] = uses[pC].n
            use(pC)
            for i in range(2):
                forget_keys(i, C[:, i, :])
            pe.wait_ge(emptied[pB], uses[pB].value())
            turn(pE, [tqb[:, r * 4 + h, :] for h in range(4) for r in range(RT)])
            pe.wait_ge(emptied[pE], uses[pE].value())

            def scores(n, hg, qt):
                for h in range(HEAD_BATCH):
                    head = hg * HEAD_BATCH + h
                    mm = nc.tensor.matmul(wide(PAIR[n % 2])[:, h * SEQ:h * SEQ + keys(qt)],
                                          qo[:, head, qt * P:(qt + 1) * P], kTb[:, head, 0:keys(qt)], start=True,
                                          stop=True)
                return mm

            def probs(n, hg, qt):
                for h in range(HEAD_BATCH):
                    for kt in range(qt + 1):
                        at = h * SEQ + kt * P
                        mm = nc.tensor.matmul(wide(C)[:, at:at + P], s_b[n % S_RING][:, h, kt * P:(kt + 1) * P],
                                              ident[:, :], start=True, stop=True, is_transpose=True)
                return mm

            def outs(n, hg, qt):
                for h in range(HEAD_BATCH):
                    head = hg * HEAD_BATCH + h
                    for kt in range(qt + 1):
                        mm = nc.tensor.matmul(E[:, 0, h * P:(h + 1) * P], s_b[n % S_RING][:, h, kt * P:(kt + 1) * P],
                                              vb[:, kt, head * P:(head + 1) * P], start=kt == 0, stop=kt == qt)
                return mm

            def between(n):
                if n < 6:
                    forget_keys(n + 2, E[:, 1, :])

            plan["attn_b"] = [u.n for u in uses]
            attention([(hg, qt) for hg in range(4) for qt in range(RT)], scores, probs, outs, between)

            pe.wait_ge(emptied[pE], uses[pE].value())
            for p in range(4):
                turn(p, [qo[:, kt, r * P:(r + 1) * P] for kt in range(4 * p, 4 * p + 4) for r in range(RT)])
            for part in range(2):
                gate_row((pC, pE), part)
            for p in range(2):
                pe.wait_ge(emptied[p], uses[p].value())
            for q in range(NC):
                chunk(q % 2, q * CG)
                if q == 2:
                    mod_block(pC)
            turn_norm(4)
            ffn(4, [(2, True), (FJ - 3, False)], False)

        @block.sync
        def _(sp):
            used = Tally()
            m = Tally()

            def load(n, src):
                if used.n >= RAW:
                    sp.wait_ge(split_done, used.value(1))
                sp.dma_start(raw[:, n % RAW], src).then_inc(raw_full[n % RAW], 16)
                used.step()

            def load_ada(src):
                if m.n >= ADA:
                    sp.wait_ge(ada_done, m.value(1))
                slot = m.n % ADA
                sp.dma_start(ada[:, slot], src).then_inc(ada_full[slot], 16)
                m.step()

            def load_first_ada(t):
                src = ada_src(w_mod[0], t % KT, (0, 2, 1, 3)[t // KT])
                if t % PE_TILE != PE_TILE - 1:
                    load_ada(src)
                    return
                n = t // PE_TILE
                if n >= 2:
                    sp.wait_ge(ada_pe_done, n - 1)
                sp.dma_start(pe_tiles[:, n % 2], src).then_inc(ada_pe_full[n % 2], 16)

            def rows(w, g):
                return w[g * GK * P:(g + 1) * GK * P, :].rearrange("(t p) n -> p t n", p=P)

            def ada_src(w, kt, block_at):
                return w[kt * P:(kt + 1) * P, ds(block_at * ADA_W, ADA_W)]

            w_mod = [w_ada[0], w_ada_kv, w_ada[1]]
            by_tile = lambda t: t.rearrange("(a p) n -> p a n", p=P)

            def vec(row, tile, src, n):
                sp.dma_start(vecs[row:row + n, tile, :], src.rearrange("(a b) -> a b", b=P)).then_inc(vecs_in, 16)

            vec(0, 0, b_ada[0], 96)
            vec(96, 0, b_ada_kv, 32)
            vec(0, 1, b_ada[1], 96)
            vec(96, 1, c[0], 16)
            vec(112, 1, g_norm_kv, 16)
            vec(0, 2, g_norm_attn.rearrange("a b -> (a b)"), 32)
            vec(32, 2, g_norm_ffn.rearrange("a b -> (a b)"), 32)
            vec(64, 2, g_k_b, 1)
            vec(65, 2, g_q_b[0], 1)
            sp.dma_start(ident[:, :], causal[:, 2 * P:3 * P]).then_inc(vecs_in, 16)
            sp.dma_start(tri_ones[:, :], causal[:, 3 * P:5 * P]).then_inc(vecs_in, 16)
            for t in range(ADA):
                load_first_ada(t)
            sp.dma_start(xs, by_tile(x[0])).then_inc(x_in, 16)
            for t in range(ADA, 2 * KT):
                load_first_ada(t)

            def load_first_group(n):
                part, q, k = n // (3 * HALF), n // HALF % 3, n % HALF
                at = q * (GROUPS * HEADS_A * P)
                load(n, rows(w_qkv_a[0], HALF * part + k)[:, :, at:at + CW])

            for n in range(RAW):
                load_first_group(n)
            tile = 2 * KT
            for n, tiles in enumerate(TILES_FIRST):
                for _ in range(tiles):
                    load_first_ada(tile)
                    tile += 1
                if n < 3 * HALF - RAW:
                    load_first_group(RAW + n)
            for n in range(3 * HALF, 3 * HALF + SPLIT):
                load_first_group(n)
            sp.wait_ge(ada_pe_done, 4 * KT // PE_TILE)
            sp.dma_start(ropes.rearrange("p a b -> p (a b)"), rope).then_inc(rope_in, 16)
            sp.dma_start(gqk[:, :, :].rearrange("p a b -> p (a b)"),
                         g_qk_a.rearrange("l a b d -> (l a b d)").partition_broadcast(P)).then_inc(rope_in, 16)
            tile = 0
            for n in range(2 * HALF):
                load_first_group(3 * HALF + SPLIT + n)
                for _ in range(TILES_SECOND[n]):
                    load_ada(ada_src(w_mod[0], tile, 4))
                    tile += 1
            sp.dma_start(caus[:, :], causal[:, 0:2 * P]).then_inc(consts_in, 16)
            sp.dma_start(msk_a, mask_a).then_inc(consts_in, 16)
            sp.dma_start(wf_raw[:, :, :], w_f.rearrange("(k p) n -> p k n", p=P)).then_inc(consts_in, 16)
            sp.dma_start(bf_rows[:, :], b_f.partition_broadcast(P)).then_inc(consts_in, 16)

            for half in range(2):
                done = 1 - half
                with repeat(sp, GROUPS - done, (used, 3 * CG), (m, KT)) as g:
                    for n in range(3 * CG):
                        at = (g + done) * (HEADS_A * P) + (n // CG * GROUPS * HEADS_A * P + half * CW)
                        load(n, rows(w_qkv_a[0], n % CG)[:, :, ds(at, CW)])
                        if n >= CG:
                            load_ada(ada_src(w_mod[0], n - CG, g + (done + 4 + GROUPS * half)))
            for n in range(2 * CG):
                if n == CG:
                    sp.wait_ge(turned, 1 + 4 + 12 + 2)
                    sp.dma_start(xs, by_tile(x[0])).then_inc(x_in, 16)
                k = n % (CG // 2)
                load(n, rows(w_o_a[0], k)[:, :, n // (CG // 2) * CW:(n // (CG // 2) + 1) * CW])
                if n >= CG:
                    load_ada(ada_src(w_mod[0], n - CG, 10))

            def ffn(layer, passes, tiles, pass_tiles=()):
                wi, wo = w_ffn_in[layer], w_ffn_out[layer]
                for n in range(2 * CG):
                    load(n, rows(wi, n % CG)[:, :, n // CG * D_FF:n // CG * D_FF + CW])
                    if n < len(tiles):
                        load_ada(ada_src(w_mod[0], *tiles[n]))
                done = 0
                for times, which, first in passes:
                    tallies = [(used, 3 * CG)]
                    if which is not None:
                        tallies.append((m, KT + (len(pass_tiles) if done == 0 else 0)))
                    with repeat(sp, times, *tallies) as i:
                        for n in range(3 * CG):
                            if n < 2 * CG:
                                at = i * CW + (n // CG * D_FF + (done + 1) * CW)
                                load(n, rows(wi, n % CG)[:, :, ds(at, CW)])
                            else:
                                q, k = (n - 2 * CG) // 2, n % 2
                                hidden = wo.rearrange("(j k t p) n -> k p t j n", p=P, t=GK, k=2)[k]
                                src = hidden[:, :, ds(i + done, 1), q * CW:(q + 1) * CW]
                                load(n, src.rearrange("p t j n -> p t (j n)"))
                            if done == 0 and n < len(pass_tiles):
                                load_ada(ada_src(w_mod[0], *pass_tiles[n]))
                            if which is not None and n >= CG:
                                load_ada(ada_src(w_mod[which], n - CG, i + first))
                    done += times
                for n in range(CG):
                    q, k = n // 2, n % 2
                    at = (FJ - 1) * CW + k * GK * P
                    load(n, wo[at:at + GK * P, q * CW:(q + 1) * CW].rearrange("(t p) n -> p t n", p=P))

            ffn(0, [(1, 1, 0), (3, 1, 1), (6, 2, 0)],
                [(kt, 10) for kt in range(CG, KT)] + [(kt, 11) for kt in range(CG)], [(kt, 11) for kt in range(CG, KT)])
            with repeat(sp, 2, (used, 4 * CG), (m, KT)) as i:
                for n in range(4 * CG):
                    q = n // CG
                    load(n, rows(w_kv, n % CG)[:, :, ds(i * (2 * CW) + (q // 2 * CW + q % 2 * D), CW)])
                    if n % CG >= CG - 4:
                        load_ada(ada_src(w_mod[2], 4 * q + n % CG - (CG - 4), i + 6))
            sp.wait_ge(x_done, 8)
            sp.dma_start(by_tile(x_spill), xs).then_inc(x_spilled, 16)
            for n in range(4 * CG):
                load(n, rows(w_q_b[0], n % CG)[:, :, n // CG * CW:(n // CG + 1) * CW])
                if CG <= n < CG + KT:
                    load_ada(ada_src(w_mod[2], n - CG, 8))
            for n in range(4 * CG):
                if n == CG:
                    sp.wait_ge(turned, 54)
                    sp.wait_ge(x_spilled, 16)
                    sp.dma_start(xs, by_tile(x_spill)).then_inc(x_in, 16)
                load(n, rows(w_o_b[0], n % CG)[:, :, n // CG * CW:(n // CG + 1) * CW])
                if CG <= n < CG + KT:
                    load_ada(ada_src(w_mod[2], n - CG, 9))
            ffn(1, [(2, 2, 10), (FJ - 3, None, 0)], ())
            for q in range(NC):
                sp.wait_ge(x_done, 12 + q + 1)
                sp.dma_start(by_tile(out[0])[:, :, q * CW:(q + 1) * CW], xs[:, :, q * CW:(q + 1) * CW]
                             ).then_inc(stored, 16)
            sp.wait_ge(stored, 16 * NC)

        @block.scalar
        def _(act):
            w_t = Tally()
            turned_t, p_t, top_t, lo_t, root_t, gain_t, inv8_t, ones_t = (Tally() for _ in range(8))

            def split(k):
                act.wait_ge(raw_full[k % RAW], landed(w_t, RAW))
                act.wait_ge(mm_done, w_t.value(1))
                nc.scalar.activation(w_hi[:, k % SPLIT], raw[:, k % RAW], ACT.Copy).then_inc(hi_done, 1)
                w_t.step()

            def round_lhs(p, into):
                act.wait_ge(turned, turned_t.step())
                nc.scalar.activation(into, wide(PAIR[p]), ACT.Copy).then_inc(lhs_hi, 1)

            def square_sums(e, q):
                if e == 0:
                    act.wait_ge(x_in, 16)
                else:
                    act.wait_ge(x_done, {1: 0, 2: 4, 4: 8}[e] + q + 1)
                at = slice(q * CW, (q + 1) * CW)
                for r in range(RT):
                    ins = nc.scalar.activation(ys[:, r, at], xs[:, r, at], ACT.Square,
                                               accum_out=ss_parts[:, r, q:q + 1])
                if q == NC - 1:
                    ins.then_inc(sumsq, 1)

            def root_rows(e):
                nc.scalar.activation(warm[:, :], ident[:, 0:1], ACT.Sqrt).then_inc(warmed, 1)
                square_sums(e, NC - 1)
                act.wait_ge(rms_inv, root_t.step())
                nc.scalar.activation(rstd[:, :], rms[:, :], ACT.Sqrt).then_inc(root, 1)
                act.wait_ge(root, root_t.value())

            def normalize(q):
                at = slice(q * CW, (q + 1) * CW)
                nc.scalar.activation(ys[:, 1, at], xs[:, 1, at], ACT.Copy, scale=rstd[:, 1:2]).then_inc(y_act_done, 1)

            def norm(e, full):
                shift, _, _ = NORMS[e]

                if e != 3:
                    root_rows(e)
                    for q in range(2):
                        normalize(q)
                act.wait_ge(gain_done, gain_t.step())
                for p in range(4):
                    act.wait_ge(turned, turned_t.step())
                    if p % 2 == 0:
                        if p:
                            act.wait_ge(lhs_lo, lo_t.value(1))
                        for k in range(4):
                            kt = 4 * p + k
                            ins = nc.scalar.activation(full[p % 2][:, k, :], wide(PAIR[p])[:, k * SEQ:(k + 1) * SEQ],
                                                       ACT.Identity, scale=gain[:, kt:kt + 1],
                                                       bias=vector(shift)[:, kt:kt + 1])
                        ins.then_inc(emptied[p], 1)
                        act.wait_ge(emptied[p], plan["norm", e][p] + 1)
                    else:
                        act.wait_ge(emptied[p], plan["norm", e][p] + 1)
                    nc.scalar.activation(h_hi[:, 4 * p:4 * p + 4, :], full[p % 2], ACT.Copy).then_inc(lhs_hi, 1)
                    if p == 0 and e != 3:
                        for q in range(2, NC):
                            normalize(q)
                lo_t.step(4)

            def keep_gate():
                pairs = plan["gate", ones_t.n // 4][0]
                for k in range(4):
                    p = pairs[k // 2]
                    act.wait_ge(ones_done, ones_t.step())
                    ins = nc.scalar.activation(gate[:, k * CW:(k + 1) * CW], PAIR[p][:, k % 2, :], ACT.Copy)
                    ins.then_inc(gate_done if k % 2 == 0 else emptied[p], 1)

            def attention(n_steps, s_tiles, n_parts, n_tops):
                def turn_back(n):
                    act.wait_ge(p_turned, p_t.step())
                    turned_p = wide(C)[:, 0:n_parts * SEQ].rearrange("p (g k) -> p g k", g=n_parts)
                    nc.scalar.activation(s_tiles[n % S_RING][:, :, 0:keys(n % 2)], turned_p[:, :, 0:keys(n % 2)],
                                         ACT.Copy).then_inc(emptied[pC], 1)

                for n in range(n_steps + 1):
                    if n < n_steps:
                        act.wait_ge(top_done, top_t.step())
                        o, per = n % S_RING, n_parts // n_tops
                        for j in range(n_tops):
                            s = s_tiles[o][:, j * per:(j + 1) * per, 0:keys(n % 2)]
                            ins = nc.scalar.activation(s, s, ACT.Exp, bias=neg_top[:, o, j:j + 1],
                                                       accum_out=total[:, o, j:j + 1])
                        ins.then_inc(exp_done, 1)
                    if n:
                        turn_back(n - 1)

            def square(p, into):
                act.wait_ge(mm_done, w_t.value())
                nc.scalar.activation(into, PAIR[p][:, :, :], ACT.Square).then_inc(squared, 1)

            def root_heads():
                act.wait_ge(inv8, inv8_t.step())
                nc.scalar.activation(rstd8[:, :], rms8[:, :], ACT.Sqrt).then_inc(root8, 1)

            act.wait_ge(emptied[pC], 1)
            nc.scalar.activation(c_act[:, :], cols[:, OFF_C:OFF_C + KT], ACT.Silu).then_inc(c_done, 1)
            turned_t.step()
            for q in range(NC - 1):
                square_sums(0, q)
            root_rows(0)
            for q in range(NC):
                normalize(q)

            def modulate_quarter(p, source, into):
                for k in range(4):
                    kt = 4 * p + k
                    ins = nc.scalar.activation(into[:, k, :], source(k), ACT.Identity, scale=gain[:, kt:kt + 1],
                                               bias=vector(0)[:, kt:kt + 1])
                return ins

            def round_quarter(p):
                nc.scalar.activation(h_hi[:, 4 * p:4 * p + 4, :], full0[p % 2], ACT.Copy).then_inc(lhs_hi, 1)

            act.wait_ge(gain_done, gain_t.step())
            act.wait_ge(turned, turned_t.step())
            modulate_quarter(0, lambda k: wide(A)[:, k * SEQ:(k + 1) * SEQ], full0[0]).then_inc(emptied[pA], 1)
            act.wait_ge(emptied[pA], 1)
            round_quarter(0)
            turned_t.step()
            act.wait_ge(emptied[pB], 1)
            round_quarter(1)
            for p in (2, 3):
                act.wait_ge(turned, turned_t.step())
                act.wait_ge(lhs_lo, p - 1)
                nc.scalar.activation(full0[p % 2].rearrange("p a b -> p (a b)"), wide(E), ACT.Copy
                                     ).then_inc(emptied[pE], 1)
                if p == 2:
                    for k in range(SPLIT):
                        split(k)
            lo_t.step(4)
            for k in range(SPLIT, 3 * HALF + 2):
                split(k)
            act.wait_ge(gain_done, gain_t.step())
            act.wait_ge(emptied[pE], 4)
            modulate_quarter(2, lambda k: full0[0][:, k, :], full0[0]).then_inc(part_act, 1)
            act.wait_ge(part_act, 1)
            round_quarter(2)
            act.wait_ge(part_dve, 1)
            round_quarter(3)
            for k in range(3 * HALF + 2, 3 * HALF + SPLIT):
                split(k)
            for k in range(3 * HALF, 6 * HALF):
                split(SPLIT + k)
                if k in (4 * HALF - 1, 5 * HALF - 1):
                    square(pA if k < 4 * HALF else pB, sq)
                    root_heads()
                if k == 5 * HALF + 1:
                    act.wait_ge(turned, turned_t.step())
                    nc.scalar.activation(qT[:, 0:4, :].rearrange("p a b -> p (a b)"), wide(E), ACT.Copy,
                                         scale=float(P) ** -0.5).then_inc(emptied[pE], 1)
            act.wait_ge(turned, turned_t.step())
            nc.scalar.activation(va[:, :, 0, :], C[:, :, :], ACT.Copy).then_inc(emptied[pC], 1)
            nc.scalar.activation(kT[:, 0:4, :].rearrange("p a b -> p (a b)"), wide(E), ACT.Copy
                                 ).then_inc(emptied[pE], 1)

            for half in range(2):
                done = 1 - half
                with repeat(act, GROUPS - done, (w_t, 3 * CG), (turned_t, 2), (inv8_t, 2)) as g:
                    for k in range(3 * CG):
                        split(SPLIT + k)
                        if k == 7:
                            square(pA, sq)
                        if k == 8:
                            root_heads()
                        if k == 15:
                            square(pB, sq)
                        if k == 16:
                            act.wait_ge(turned, turned_t.step())
                            act.wait_ge(turned, 1)
                            nc.scalar.activation(qT[:, ds(g * 4 + 4 * done, 4), :].rearrange("p a b -> p (a b)"),
                                                 wide(E), ACT.Copy,
                                                 scale=float(P) ** -0.5).then_inc(emptied[pE], 1)
                            root_heads()
                    act.wait_ge(turned, turned_t.step())
                    act.wait_ge(turned, 1)
                    nc.scalar.activation(va[:, :, ds(g + done, 1), :].rearrange("p r g n -> p r (g n)"), C[:, :, :],
                                         ACT.Copy
                                         ).then_inc(emptied[pC], 1)
                    nc.scalar.activation(kT[:, ds(g * 4 + 4 * done, 4), :].rearrange("p a b -> p (a b)"), wide(E),
                                         ACT.Copy
                                         ).then_inc(emptied[pE], 1)
                if half == 0:
                    act.wait_ge(consts_in, 16 * 4)
                    nc.scalar.activation(wf_hi[:, :, :], wf_raw[:, :, :], ACT.Copy).then_inc(wf_hi_done, 1)
                attention(8, s_a, GROUPS, 1)
            for p in range(2):
                round_lhs(p, h_hi[:, 4 * p:4 * p + 4, :])
            keep_gate()
            for k in range(2 * CG):
                split(SPLIT + k)
                if k % 4 == 1 and k > 4:
                    square_sums(1, k // 4 - 1)

            def ffn():
                def part(n, turned_before):
                    for k in range(n):
                        split(SPLIT + k)
                        if k == CG - 1 and turned_before:
                            round_lhs(pE, m_hi[:, :, :])
                        if k == CG:
                            act.wait_ge(mm_done, w_t.value())
                            nc.scalar.activation(silu, A[:, :, :], ACT.Silu).then_inc(emptied[pA], 1)

                part(2 * CG, False)
                with repeat(act, FJ - 1, (w_t, 3 * CG), (turned_t, 1)):
                    part(3 * CG, True)
                round_lhs(pE, m_hi[:, :, :])
                keep_gate()

            norm(1, full)
            ffn()
            for k in range(CG):
                split(SPLIT + k)
                if k % 2 and k > 1:
                    square_sums(2, k // 2 - 1)
            norm(2, full)
            with repeat(act, 2, (w_t, 4 * CG), (turned_t, 2), (inv8_t, 2)) as i:
                for k in range(4 * CG):
                    split(SPLIT + k)
                    if k % (2 * CG) == 7:
                        square(pA, sqb)
                    if k % (2 * CG) == 8:
                        root_heads()
                    if k % (2 * CG) == 2 * CG - 1:
                        q = k // (2 * CG)
                        act.wait_ge(turned, turned_t.step())
                        act.wait_ge(turned, 1)
                        nc.scalar.activation(vb[:, :, ds(i * (2 * CW) + q * CW, CW)], B[:, :, :], ACT.Copy
                                             ).then_inc(emptied[pB], 1)
                        nc.scalar.activation(kTb[:, ds(i * 8 + q * 4, 4), :].rearrange("p a b -> p (a b)"), wide(E),
                                             ACT.Copy, scale=cols[:, OFF_GK:OFF_GK + 1]).then_inc(emptied[pE], 1)
            act.wait_ge(lf_dve, 1)
            nc.scalar.activation(lf[1][:, :, :], lf[0][:, :, :], ACT.Abs).then_inc(lf_act, 1)
            act.wait_ge(lf_act, 1)
            nc.scalar.activation(lf[2][:, :, :], lf[1][:, :, :], ACT.Exp, scale=-1.0).then_inc(lf_act, 1)
            act.wait_ge(lf_act, 2)
            nc.scalar.activation(lf[3][:, :, :], lf[2][:, :, :], ACT.Ln, bias=1.0).then_inc(lf_act, 1)
            norm(3, full)

            def keep_q(q):
                act.wait_ge(turned, turned_t.step())
                if q == 0:
                    act.wait_ge(x_spilled, 16)
                nc.scalar.activation(qo[:, 4 * q:4 * q + 4, :].rearrange("p a b -> p (a b)"), wide(E), ACT.Copy,
                                     scale=gq_scaled[:, 0:1]).then_inc(emptied[pE], 1)

            for q in range(4):
                for k in range(CG):
                    split(SPLIT + k)
                square(q % 2, sqb)
                root_heads()
                if q:
                    keep_q(q - 1)
            keep_q(3)
            attention(8, s_b, HEAD_BATCH, HEAD_BATCH)
            for p in range(4):
                round_lhs(p, h_hi[:, 4 * p:4 * p + 4, :])
            keep_gate()
            for k in range(4 * CG):
                split(SPLIT + k)
                if k % CG == 1 and k > CG:
                    square_sums(4, k // CG - 1)
            norm(4, full)
            ffn()
            for k in range(CG - SPLIT):
                split(SPLIT + k)

        @block.vector
        def _(dve):
            dve.sem_inc(split_done, RAW)
            dve.sem_inc(ada_done, ADA)
            lo_t = Tally()
            m_t = Tally()
            blk_t = Tally()
            own_t, turned_t, lhs_hi_t, lhs_lo_t, sq_t, root8_t, root_t = (Tally() for _ in range(7))
            qk_t, exp_t, pv_t, ones_t = (Tally() for _ in range(4))

            def chained(ins):
                ins.then_inc(own, 1)
                dve.wait_ge(own, own_t.step())

            def split(k):
                dve.wait_ge(hi_done, lo_t.value(1))
                nc.vector.tensor_tensor(w_lo[:, k % SPLIT], raw[:, k % RAW], w_hi[:, k % SPLIT].bitcast(f32),
                                        ALU.subtract).then_inc(split_done, 1)
                lo_t.step()

            def modulate(first=None):
                slot, kt = m_t.n % ADA, m_t.n % KT
                done = (m_t.n + 4 * KT // PE_TILE) // KT + 1
                if first is not None:
                    kt, done = first[0], first[1] + 1
                dve.wait_ge(ada_full[slot], landed(m_t, ADA))
                if kt == 0:
                    dve.wait_ge(col_done, done if m_t.i is None else m_t.i * (m_t.per // KT) + done)
                    ins = nc.vector.tensor_scalar(acc[:, :], ada[:, slot], c_act[:, 0:1], None, ALU.mult)
                else:
                    dve.wait_ge(ada_done, m_t.value(ADA))
                    ins = nc.vector.scalar_tensor_tensor(out=acc[:, :], in0=ada[:, slot], scalar=c_act[:, kt:kt + 1],
                                                         in1=acc[:, :], op0=ALU.mult, op1=ALU.add)
                ins.then_inc(ada_done, 1)
                m_t.step()

            def modulate_first(t):
                if t % PE_TILE != PE_TILE - 1:
                    modulate((t % KT, t // KT))

            def keep_block(p, place=None):
                n = ADA_W // P
                at = blk_t.value() * n if place is None else place * n
                dve.wait_ge(col_done, blk_t.value(2))
                if place is None:
                    parts = wide(PAIR[p]).rearrange("p (a b) -> p a b", b=P)
                else:
                    parts = PAIR[p][:, 0, 0:(KT // PE_TILE + 1) * n].rearrange("p (a b) -> p b a", b=n)
                chained(nc.vector.reduce_sum(block_sum[:, :], parts, AX.X))
                nc.vector.tensor_tensor(mods[:, ds(at, n)], block_sum[:, :], cols[:, ds(at, n)], ALU.add
                                        ).then_inc(emptied[p], 1)
                blk_t.step()

            def norm_stats():
                dve.wait_ge(sumsq, root_t.value(1))
                chained(nc.vector.reduce_sum(ss[:, :], ss_parts[:, :, :], AX.X))
                chained(nc.vector.tensor_scalar(ms[:, :], ss[:, :], 1.0 / D, EPS, ALU.mult, ALU.add))
                nc.vector.reciprocal(rms[:, :], ms[:, :]).then_inc(rms_inv, 1)
                dve.wait_ge(root, root_t.step())
                for q in range(NC):
                    at = slice(q * CW, (q + 1) * CW)
                    nc.vector.tensor_scalar(ys[:, 0, at], xs[:, 0, at], rstd[:, 0:1], None, ALU.mult
                                            ).then_inc(y_done, 1)

            def norm_gain(e, first=0, end=KT):
                _, scale, g = NORMS[e]
                nc.vector.scalar_tensor_tensor(out=gain[:, first:end], in0=vector(scale)[:, first:end], scalar=1.0,
                                               in1=cols[:, g + first:g + end], op0=ALU.add, op1=ALU.mult
                                               ).then_inc(gain_done, 1)

            def lo_quarter(p, full):
                dve.wait_ge(lhs_hi, lhs_hi_t.step())
                nc.vector.tensor_tensor(h_lo[:, 4 * p:4 * p + 4, :], full[p % 2],
                                        h_hi[:, 4 * p:4 * p + 4, :].bitcast(f32), ALU.subtract).then_inc(lhs_lo, 1)
                lhs_lo_t.step()

            def norm_split(e, full):
                shift, _, _ = NORMS[e]

                def modulated(p):
                    dve.wait_ge(turned, turned_t.value(p + 1))
                    for k in range(4):
                        kt = 4 * p + k
                        ins = nc.vector.tensor_scalar(full[1][:, k, :], wide(PAIR[p])[:, k * SEQ:(k + 1) * SEQ],
                                                      gain[:, kt:kt + 1], vector(shift)[:, kt:kt + 1], ALU.mult,
                                                      ALU.add)
                    ins.then_inc(emptied[p], 1)

                def lo(p):
                    lo_quarter(p, full)

                dve.wait_ge(gain_done, e + 2)
                modulated(1)
                lo(0)
                lo(1)
                dve.wait_ge(lhs_lo, lhs_lo_t.value())
                modulated(3)
                lo(2)
                lo(3)
                turned_t.step(4)

            def lo_of(p, hi, lo):
                dve.wait_ge(lhs_hi, lhs_hi_t.step())
                nc.vector.tensor_tensor(lo, wide(PAIR[p]), hi.bitcast(f32), ALU.subtract).then_inc(emptied[p], 1)

            def head_stats(squares):
                dve.wait_ge(squared, sq_t.step())
                chained(nc.vector.reduce_sum(ss8[:, :], squares, AX.X))
                chained(nc.vector.tensor_scalar(ms8[:, :], ss8[:, :], 1.0 / P, EPS, ALU.mult, ALU.add))
                nc.vector.reciprocal(rms8[:, :], ms8[:, :]).then_inc(inv8, 1)

            def head_scale(p, into):
                dve.wait_ge(root8, root8_t.step())
                dve.wait_ge(turned, turned_t.value())
                nc.vector.tensor_tensor(into, wide(PAIR[p]).rearrange("p (h d) -> p h d", d=P),
                                        rstd8[:, :].unsqueeze(2).to_broadcast([P, 8, P]), ALU.mult
                                        ).then_inc(emptied[p], 1)

            def diagonal(v, k):
                if k >= 2:
                    dve.wait_ge(ones_done, ones_t.value(k - 1))
                nc.vector.tensor_tensor(diag[:, k % 2].rearrange("p (a b) -> p a b", b=P),
                                        ident[:, :].unsqueeze(1).to_broadcast([P, 4, P]),
                                        vector(v)[:, 4 * k:4 * k + 4].unsqueeze(2).to_broadcast([P, 4, P]), ALU.mult
                                        ).then_inc(diag_done, 1)

            def gate_ready(n):
                pairs, before = plan["gate", n]
                dve.wait_ge(emptied[pairs[1]], before[pairs[1]] + 1)

            def add_gated(p, at, ahead):
                dve.wait_ge(mm_done, lo_t.value(ahead))
                dve.wait_ge(split_done, lo_t.value(RAW))
                for r in range(RT):
                    ins = nc.vector.tensor_tensor(silu[:, r, :], PAIR[p][:, r, :], gate[:, ds(at, CW)], ALU.mult)
                chained(ins)
                for r in range(RT):
                    nc.vector.tensor_tensor(xs[:, r, ds(at, CW)], xs[:, r, ds(at, CW)], silu[:, r, :], ALU.add
                                            ).then_inc(x_done if r else emptied[p], 1)

            def attention(steps, s_tiles, bias, n_parts, n_tops, key, o_rows, between=None):
                before, per = plan[key], n_parts // n_tops
                for n in range(len(steps) + 2):
                    if n < len(steps):
                        o, seen = n % S_RING, keys(steps[n][1])
                        dve.wait_ge(qk_done, qk_t.step())
                        for j in range(n_tops):
                            scores = wide(PAIR[n % 2])[:, j * per * SEQ:(j + 1) * per * SEQ]
                            ins = nc.vector.tensor_tensor_reduce(
                                out=s_tiles[o][:, j * per:(j + 1) * per, 0:seen],
                                in0=scores.rearrange("p (g k) -> p g k", g=per)[:, :, 0:seen],
                                in1=bias(j, *steps[n]), scale=1.0, scalar=LOWEST, op0=ALU.add, op1=ALU.max,
                                accum_out=top[:, o, j:j + 1])
                        ins.then_inc(emptied[n % 2], 1)
                        dve.wait_ge(emptied[n % 2], before[n % 2] + n // 2 + 1)
                        nc.vector.tensor_scalar(neg_top[:, o, 0:n_tops], top[:, o, 0:n_tops], -1.0, None, ALU.mult
                                                ).then_inc(top_done, 1)
                        if between is not None:
                            between(n)
                    if n >= 2:
                        o = (n - 2) % S_RING
                        dve.wait_ge(exp_done, exp_t.step())
                        chained(nc.vector.reciprocal(inv_total[:, o, 0:n_tops], total[:, o, 0:n_tops]))
                        dve.wait_ge(pv_done, pv_t.step())
                        nc.vector.tensor_tensor(
                            o_rows(*steps[n - 2]), E[:, 0, 0:n_tops * P].rearrange("p (h d) -> p h d", d=P),
                            inv_total[:, o, 0:n_tops].unsqueeze(2).to_broadcast([P, n_tops, P]), ALU.mult
                        ).then_inc(emptied[pE], 1)

            dve.wait_ge(turned, turned_t.step())
            nc.vector.tensor_copy(cols[:, :], C[:, 0, 0:322]).then_inc(emptied[pC], 1)
            dve.wait_ge(emptied[pC], 1)
            chained(nc.vector.tensor_scalar(gq_scaled[:, :], cols[:, OFF_GQ:OFF_GQ + 1], float(P) ** -0.5, None,
                                            ALU.mult))
            dve.wait_ge(c_done, 1)
            for b in (0, 2):
                for k in range(KT):
                    modulate_first(b // 2 * KT + k)
                keep_block(pE, b)
                if b == 0:
                    norm_stats()
            dve.wait_ge(emptied[pE], 2)
            norm_gain(0, 0, KT // 2)

            def modulate_quarter(p, source, into):
                for k in range(4):
                    kt = 4 * p + k
                    ins = nc.vector.tensor_scalar(into[:, k, :], source(k), gain[:, kt:kt + 1],
                                                  vector(0)[:, kt:kt + 1], ALU.mult, ALU.add)
                return ins

            dve.wait_ge(gain_done, 1)
            dve.wait_ge(turned, turned_t.value(2))
            modulate_quarter(1, lambda k: wide(B)[:, k * SEQ:(k + 1) * SEQ], full0[1]).then_inc(emptied[pB], 1)
            lo_quarter(0, full0)
            lo_quarter(1, full0)
            turned_t.step(4)
            for k in range(SPLIT // 2):
                split(k)
            for n, tiles in enumerate(TILES_FIRST):
                if SPLIT // 2 + n < 3 * HALF:
                    split(SPLIT // 2 + n)
                for t in range(sum(TILES_FIRST[:n]), sum(TILES_FIRST[:n + 1])):
                    modulate_first(2 * KT + t)
                if n == 5:
                    keep_block(pE, 1)
            keep_block(pE, 3)
            dve.wait_ge(emptied[pE], 6)
            norm_gain(0, KT // 2, KT)
            dve.wait_ge(gain_done, 2)
            modulate_quarter(3, lambda k: full0[1][:, k, :], full0[1]).then_inc(part_dve, 1)
            for p in (2, 3):
                split(3 * HALF + p - 2)
                lo_quarter(p, full0)
            for k in range(3 * HALF + 2, 3 * HALF + SPLIT):
                split(k)
            for n in range(3 * HALF):
                k = 3 * HALF + n
                split(SPLIT + k)
                if k in (4 * HALF - 1, 5 * HALF - 1):
                    head_stats(sq)
                    modulate()
                    first = k < 4 * HALF
                    head_scale(pA if first else pB, tq if first else tq_first)
                    modulate()
                else:
                    for _ in range(TILES_SECOND[n]):
                        modulate()
            turned_t.step(2)
            keep_block(pB)

            for half in range(2):
                with repeat(dve, GROUPS - (half == 0), (lo_t, 3 * CG), (m_t, KT), (blk_t, 1), (own_t, 5), (turned_t, 2),
                            (sq_t, 2), (root8_t, 2)):
                    for k in range(3 * CG):
                        split(SPLIT + k)
                        if k < KT:
                            modulate()
                        if k in (7, 16):
                            head_stats(sq)
                        if k == 9:
                            head_scale(pA, tq)
                            turned_t.step()
                        if k == 18:
                            head_scale(pB, tq)
                            turned_t.step()
                    keep_block(pB)
                if half == 0:
                    dve.wait_ge(consts_in, 16 * 4)
                    dve.wait_ge(wf_hi_done, 1)
                    nc.vector.tensor_tensor(wf_lo[:, :, :], wf_raw[:, :, :], wf_hi[:, :, :].bitcast(f32), ALU.subtract
                                            ).then_inc(wf_done, 1)
                masks = msk_a.rearrange("p (r g k) -> p r g k", r=RT, g=GROUPS)
                attention([(h, qt) for h in range(4) for qt in range(RT)], s_a,
                          lambda _, h, qt: masks[:, qt, :, 0:keys(qt)], GROUPS, 1, ("attn", half),
                          lambda h, qt, half=half: oa[:, qt, (4 * half + h) * P:(4 * half + h + 1) * P].unsqueeze(1))
            diagonal(GATES[0], 0)
            diagonal(GATES[0], 1)
            for p in range(2):
                lo_of(p, h_hi[:, 4 * p:4 * p + 4, :].rearrange("p a b -> p (a b)"),
                      h_lo[:, 4 * p:4 * p + 4, :].rearrange("p a b -> p (a b)"))
            turned_t.step(2)
            diagonal(GATES[0], 2)
            diagonal(GATES[0], 3)
            ones_t.step(4)
            gate_ready(0)
            dve.wait_ge(x_in, 32)
            for k in range(2 * CG):
                last = k == 2 * CG - 1
                if last:
                    add_gated(k // 4 % 2, k // 4 * CW, SPLIT)
                    split(0)
                elif k < 2 * CG - SPLIT:
                    split(SPLIT + k)
                if not last:
                    modulate()
                    if k == 1:
                        modulate()
                    if k % 4 == 3:
                        add_gated(k // 4 % 2, k // 4 * CW, 0)

            def ffn(e, layer, passes, mod_first):
                def turned_lo():
                    lo_of(pE, m_hi[:, :, :].rearrange("p a b -> p (a b)"), m_lo[:, :, :].rearrange("p a b -> p (a b)"))
                    turned_t.step()

                def part(n, with_mod, outputs):
                    for k in range(n):
                        split(SPLIT + k)
                        if with_mod and k < KT:
                            modulate()
                        if k == CG and outputs:
                            turned_lo()
                        if k == 2 * CG - 1:
                            dve.wait_ge(emptied[pA], a_t.value(1))
                            chained(nc.vector.tensor_tensor(mid[:, 0, :], silu[:, 0, :], B[:, 0, :], ALU.mult))
                            nc.vector.tensor_tensor(mid[:, 1, :], silu[:, 1, :], B[:, 1, :], ALU.mult
                                                    ).then_inc(emptied[pB], 1)
                        if k >= 2 * CG and k % 2:
                            q = (k - 2 * CG) // 2
                            p = (pC, pE, pA, pC)[q]
                            at = yacc[:, :, q * CW:(q + 1) * CW]
                            nc.vector.tensor_tensor(at, PAIR[p][:, :, :], at, ALU.add).then_inc(emptied[p], 1)
                    a_t.step(2 if outputs else 1)

                a_t = Tally(plan["norm", e][pA] + 1)
                part(2 * CG, mod_first, False)
                if mod_first:
                    keep_block(pC)
                dve.wait_ge(zeroed, layer + 1)
                for times, with_mod in passes:
                    tallies = [(lo_t, 3 * CG), (own_t, 2 if with_mod else 1), (lhs_hi_t, 1), (turned_t, 1), (a_t, 2)]
                    tallies += [(m_t, KT), (blk_t, 1)] if with_mod else []
                    with repeat(dve, times, *tallies):
                        part(3 * CG, with_mod, True)
                        if with_mod:
                            keep_block(pE)
                for k in range(4):
                    if k == 2:
                        turned_lo()
                    diagonal(GATES[2 * layer + 1], k)
                ones_t.step(4)
                last = layer == 1
                n0 = lo_t.n - SPLIT
                for k in range(CG):
                    if k < SPLIT:
                        split(SPLIT + k)
                    if k % 2:
                        q = k // 2
                        p = (pC, pE, pA, pC)[q]
                        if q == 0:
                            gate_ready(2 * layer + 1)
                        dve.wait_ge(mm_done, SPLIT + n0 + k + 1)
                        at = slice(q * CW, (q + 1) * CW)
                        if q:
                            dve.wait_ge(x_done, 8 * layer + 4 + q)
                        chained(nc.vector.tensor_tensor(yacc[:, :, at], PAIR[p][:, :, :], yacc[:, :, at], ALU.add))
                        for r in range(RT):
                            ins = nc.vector.tensor_tensor(silu[:, r, :], yacc[:, r, at], gate[:, at], ALU.mult)
                        chained(ins)
                        for r in range(RT):
                            nc.vector.tensor_tensor(xs[:, r, at], xs[:, r, at], silu[:, r, :], ALU.add
                                                    ).then_inc(x_done if r else emptied[p], 1)
                if not last:
                    split(CG)

            norm_gain(1)
            norm_stats()
            split(1)
            keep_block(pC)
            norm_split(1, full)
            for k in range(2, SPLIT):
                split(k)
            ffn(1, 0, [(FJ - 1, True)], True)

            norm_gain(2)
            norm_stats()
            split(1)
            norm_split(2, full)
            for k in range(2, SPLIT):
                split(k)
            with repeat(dve, 2, (lo_t, 4 * CG), (m_t, KT), (blk_t, 1), (own_t, 5), (turned_t, 2), (sq_t, 2),
                        (root8_t, 2)):
                for k in range(4 * CG):
                    split(SPLIT + k)
                    if k % CG < 4:
                        modulate()
                    if k % (2 * CG) == 7:
                        head_stats(sqb)
                    if k % (2 * CG) == 9:
                        head_scale(pA, tqb)
                        turned_t.step()
                keep_block(pC)
            dve.wait_ge(z_done, 1)
            for r in range(RT):
                ins = nc.vector.tensor_tensor(lf[0][:, r, :], C[:, r, 0:HEADS_B], bf_rows[:, :], ALU.add)
            ins.then_inc(emptied[pC], 1)
            dve.wait_ge(emptied[pC], plan["z"][pC] + 1)
            chained(nc.vector.tensor_scalar(z_neg[:, :, :], lf[0][:, :, :], 0.0, None, ALU.min))
            nc.vector.tensor_scalar(z_neg[:, :, :], z_neg[:, :, :], -1.0, None, ALU.mult).then_inc(lf_dve, 1)
            norm_gain(3)
            norm_split(3, full)
            dve.wait_ge(lf_act, 3)
            nc.vector.tensor_tensor(neg_logf[:, :, :], lf[3][:, :, :], z_neg[:, :, :], ALU.add).then_inc(lf_dve, 1)
            for q in range(4):
                for k in range(CG):
                    split(SPLIT + k)
                    if q * CG + k < KT:
                        modulate()
                head_stats(sqb)
                head_scale(q % 2, tqb)
                turned_t.step()
                if q == 0:
                    dve.wait_ge(z_done, 2)
                    nc.vector.tensor_scalar(fq[:, :, :], C[:, :, 0:HEADS_B], -1.0, None, ALU.mult
                                            ).then_inc(emptied[pC], 1)
                if q == 2:
                    keep_block(pC)

            def forget_bias(i, keys_at):
                dve.wait_ge(fk_done, i + 1)
                for h in range(2):
                    head = 2 * i + h
                    into = fb[:, head // HEAD_BATCH % 2, head % HEAD_BATCH]
                    fk = keys_at[:, h * SEQ:(h + 1) * SEQ]
                    nc.vector.scalar_tensor_tensor(out=into[:, 0, :], in0=fk[:, 0:P], scalar=fq[:, 0, head:head + 1],
                                                   in1=caus[:, P:2 * P], op0=ALU.add, op1=ALU.add)
                    ins = nc.vector.scalar_tensor_tensor(out=into[:, 1:3, :].rearrange("p a b -> p (a b)"), in0=fk,
                                                         scalar=fq[:, 1, head:head + 1], in1=caus[:, :], op0=ALU.add,
                                                         op1=ALU.add)
                ins.then_inc(emptied[pC] if i == 1 else fk_read, 1)
                if i == 1:
                    dve.wait_ge(emptied[pC], plan["fk"] + 1)
                elif i % 2:
                    dve.wait_ge(fk_read, i)

            def forget(h, hg, qt):
                if qt == 0:
                    return fb[:, hg % 2, h, 0:1, :]
                return fb[:, hg % 2, h, 1:3, :].rearrange("p a b -> p (a b)").unsqueeze(1)

            def between(n):
                if n < 6:
                    forget_bias(n + 2, E[:, 1, :])

            for i in range(2):
                forget_bias(i, C[:, i, :])
            attention([(hg, qt) for hg in range(4) for qt in range(RT)], s_b, forget, HEAD_BATCH, HEAD_BATCH, "attn_b",
                      lambda hg, qt: qo[:, hg * HEAD_BATCH:(hg + 1) * HEAD_BATCH, qt * P:(qt + 1) * P], between)
            diagonal(GATES[2], 0)
            diagonal(GATES[2], 1)
            for p in range(4):
                lo_of(p, h_hi[:, 4 * p:4 * p + 4, :].rearrange("p a b -> p (a b)"),
                      h_lo[:, 4 * p:4 * p + 4, :].rearrange("p a b -> p (a b)"))
            turned_t.step(4)
            diagonal(GATES[2], 2)
            diagonal(GATES[2], 3)
            ones_t.step(4)
            gate_ready(2)
            dve.wait_ge(x_in, 48)
            for k in range(4 * CG):
                last = k == 4 * CG - 1
                if last:
                    add_gated(k // CG % 2, k // CG * CW, 1)
                split(SPLIT + k)
                if k < KT:
                    modulate()
                if k % CG == CG - 1 and not last:
                    add_gated(k // CG % 2, k // CG * CW, 0)
                if k == 3 * CG:
                    keep_block(pC)
            norm_gain(4)
            norm_stats()
            norm_split(4, full)
            ffn(4, 1, [(2, True), (FJ - 3, False)], False)

        @block.gpsimd
        def _(pool):
            own_p = Tally()

            def gain_and_rotate(pair, uses_t, which, g, rows):
                def chained(*ins):
                    for one in ins:
                        one.then_inc(pool_own, 1)
                    pool.wait_ge(pool_own, own_p.step(len(ins)))

                def half(k):
                    return rows[:, :, 16 * k:16 * k + 16]

                def part(k):
                    return turn4[:, k, :].rearrange("p (h d) -> p h d", d=16)

                cos, sin = (ropes[:, k, :].rearrange("p (h d) -> p h d", d=16) for k in range(2))
                pool.wait_ge(emptied[pair], uses_t)
                pool.wait_ge(rope_in, 16 * 2)
                gains = gqk[:, which, ds(g * P, P)].unsqueeze(1).to_broadcast([P, 8, P])
                chained(nc.gpsimd.tensor_tensor(rows, rows, gains, ALU.mult))
                chained(nc.gpsimd.tensor_tensor(part(0), half(0), cos, ALU.mult),
                        nc.gpsimd.tensor_tensor(part(1), half(1), sin, ALU.mult),
                        nc.gpsimd.tensor_tensor(part(2), half(1), cos, ALU.mult),
                        nc.gpsimd.tensor_tensor(part(3), half(0), sin, ALU.mult))
                chained(nc.gpsimd.tensor_tensor(half(0), part(0), part(1), ALU.subtract))
                nc.gpsimd.tensor_tensor(half(1), part(2), part(3), ALU.add).then_inc(roped, 1)

            gain_and_rotate(pA, plan["first"][pA] + 1, 0, 0, tq)
            gain_and_rotate(pB, plan["first"][pB] + 1, 1, 0, tq_first)
            for half in range(2):
                before, done = plan["qkv", half], 1 - half
                with repeat(pool, GROUPS - done, (own_p, 12)) as g:
                    gain_and_rotate(pA, g + (before[pA] + 1), 0, g + done, tq)
                    gain_and_rotate(pB, g * 2 + (before[pB] + 1), 1, g + done, tq)
            pool.wait_ge(turned, 1 + 4 + 12 + 2 + 4)
            nc.gpsimd.memset(yacc, 0.0).then_inc(zeroed, 1)
            pool.wait_ge(col_done, 25 + 1)
            pool.wait_ge(lf_dve, 2)
            for i in range(HEADS_B // 2):
                if i >= 2:
                    pool.wait_ge(fk_done, i - 1)
                for h in range(2):
                    for j in range(RT):
                        ins = nc.gpsimd.tensor_scalar(bc[:, i % 2, h, j, :], tri_ones[:, P:2 * P],
                                                      neg_logf[:, j, 2 * i + h:2 * i + h + 1], None, ALU.mult)
                ins.then_inc(bc_done, 1)
            pool.wait_ge(turned, 54 + 4)
            nc.gpsimd.memset(yacc, 0.0).then_inc(zeroed, 1)


_INS = ["x", "c", "w_ada", "b_ada", "g_norm_attn", "g_norm_ffn", "w_qkv_a", "g_qk_a", "w_o_a", "w_ada_kv", "b_ada_kv",
        "g_norm_kv", "w_kv", "g_k_b", "w_f", "b_f", "w_q_b", "g_q_b", "w_o_b", "w_ffn_in", "w_ffn_out"]


def _tables():
    import numpy as np

    rot = P // 4
    inv = np.float32(500000.0) ** (-np.arange(0, rot, 2, dtype=np.float32) / np.float32(rot))
    ang = np.arange(SEQ, dtype=np.float32)[:, None] * inv[None, :].astype(np.float32)
    rope = np.empty((P, 2, RT, 4, rot // 2), np.float32)
    for k, t in enumerate((np.cos(ang), np.sin(ang))):
        rope[:, k] = t.reshape(RT, P, 1, rot // 2).transpose(1, 0, 2, 3)
    q, k = np.arange(SEQ)[:, None], np.arange(SEQ)[None, :]
    masks = np.empty((SEQ, GROUPS, SEQ), np.float32)
    for g, (window, dilation) in enumerate(((128, 1), (512, 4), (2048, 16))):
        seen = (k <= q) & ((q - k) % dilation == 0) & ((q - k) // dilation <= window // dilation)
        masks[:, g] = np.where(seen, 0.0, -1e30)
    masks = masks.reshape(RT, P, GROUPS * SEQ).transpose(1, 0, 2).reshape(P, -1)
    a, b = np.arange(P)[:, None], np.arange(P)[None, :]
    causal = np.zeros((P, 5 * P), np.float32)
    causal[:, P:2 * P] = np.where(b <= a, 0.0, -1e30)
    causal[:, 2 * P:3 * P] = a == b
    causal[:, 3 * P:4 * P] = a <= b
    causal[:, 4 * P:] = 1.0
    return np.ascontiguousarray(rope.reshape(P, -1)), np.ascontiguousarray(masks), causal


def kernel(**inputs):
    import numpy as np
    import concourse.bacc as bacc
    from concourse.bass_utils import run_bass_kernel_spmd

    nc = bacc.Bacc("TRN2", target_bir_lowering=False, num_devices=1)
    arrays = {f"in_{n}": np.ascontiguousarray(inputs[n]) for n in _INS}
    arrays.update(zip(("rope", "mask_a", "causal"), _tables()))
    aps = [nc.dram_tensor(n, a.shape, mybir.dt.from_np(a.dtype), kind="ExternalInput").ap() for n, a in arrays.items()]
    out = nc.dram_tensor("out", (1, SEQ, D), mybir.dt.float32, kind="ExternalOutput").ap()
    build(nc, *aps, out)
    return run_bass_kernel_spmd(nc, [arrays], core_ids=[0]).results[0]["out"]
```
